# Optimizing a Trainium2 kernel written in Bass

```python
import math
import jax, jax.numpy as jnp
from jax import lax
import numpy as np

D_MODEL = 1024
BATCH = 1
SEQ = 1024
DEPTH = 1

N_MEM = 256
D_MIX = D_MODEL
D_RNN = D_MIX // 2
RNN_HEADS = 8
RNN_HEAD_DIM = D_RNN // RNN_HEADS
CONV_WIDTH = 4
LRU_C = 8.0
D_POOL = D_MIX // 4
POOL_WINDOWS = (2, 4, 8, 16)
POOL_GROUPS = len(POOL_WINDOWS)
POOL_GROUP_DIM = D_POOL // POOL_GROUPS
MAX_WINDOW = max(POOL_WINDOWS)
D_XATTN = D_MIX // 4
XATTN_HEADS = 4
XATTN_HEAD_DIM = D_XATTN // XATTN_HEADS
D_IN = 2 * D_RNN + D_POOL + D_XATTN
N_EXPERTS = 32
TOP_K = 4
D_FF = D_MODEL
SWIGLU_ALPHA = 1.702
SWIGLU_LIMIT = 7.0
MOE_BLOCK = 128
RMS_EPS = 1e-6

kernel_name = "hymba_rglru_pool_memxattn_moe"

def rmsnorm(x, g):
    xf = x.astype(jnp.float32)
    y = xf * lax.rsqrt(jnp.mean(xf * xf, axis=-1, keepdims=True) + RMS_EPS)
    return (y * g.astype(jnp.float32)).astype(x.dtype)

def causal_depthwise_conv(u, w, b):
    y = lax.conv_general_dilated(
        u, w[:, None, :].astype(u.dtype), window_strides=(1,),
        padding=[(CONV_WIDTH - 1, 0)],
        dimension_numbers=("NWC", "WIO", "NWC"),
        feature_group_count=u.shape[-1])
    return y + b.astype(u.dtype)

def rg_lru(u, w_a, b_a, w_i, b_i, lam):
    B, S, C = u.shape
    uh = u.reshape(B, S, RNN_HEADS, RNN_HEAD_DIM)
    r = jax.nn.sigmoid(jnp.einsum("bshi,hij->bshj", uh, w_a).reshape(B, S, C) + b_a)
    i = jax.nn.sigmoid(jnp.einsum("bshi,hij->bshj", uh, w_i).reshape(B, S, C) + b_i)
    log_a = -LRU_C * r.astype(jnp.float32) * jax.nn.softplus(-lam.astype(jnp.float32))
    a = jnp.exp(log_a)
    mult = jnp.sqrt(jnp.maximum(-jnp.expm1(2.0 * log_a), 0.0))
    is_start = (jnp.arange(S) == 0)[None, :, None]
    mult = jnp.where(is_start, 1.0, mult)
    bx = mult * (i * u).astype(jnp.float32)

    def combine(left, right):
        a1, b1 = left
        a2, b2 = right
        return a1 * a2, a2 * b1 + b2

    _, h = lax.associative_scan(combine, (a, bx), axis=1)
    return h.astype(u.dtype)

def multiscale_pool(u, w_pool, scale):
    B, S, _ = u.shape
    uf = u.astype(jnp.float32).reshape(B, S, POOL_GROUPS, POOL_GROUP_DIM)
    csum = jnp.cumsum(uf, axis=1)
    cpad = jnp.pad(csum, ((0, 0), (MAX_WINDOW, 0), (0, 0), (0, 0)))
    pos = jnp.arange(1, S + 1, dtype=jnp.float32)[None, :, None]
    outs = []
    for g, w in enumerate(POOL_WINDOWS):
        prev = cpad[:, MAX_WINDOW - w: MAX_WINDOW - w + S, g]
        mean = (csum[:, :, g] - prev) / jnp.minimum(pos, float(w))
        outs.append(mean - uf[:, :, g])
    d = jnp.stack(outs, axis=2).astype(u.dtype)
    y = jnp.einsum("bsgi,gij->bsgj", d, w_pool).reshape(B, S, D_POOL)
    return y * scale

def memory_cross_attention(q, mem_n, w_mem_kv):
    B, S, _ = q.shape
    kv = mem_n @ w_mem_kv
    k, v = jnp.split(kv, 2, axis=-1)
    qh = q.reshape(B, S, XATTN_HEADS, XATTN_HEAD_DIM)
    kh = k.reshape(B, -1, XATTN_HEADS, XATTN_HEAD_DIM)
    vh = v.reshape(B, -1, XATTN_HEADS, XATTN_HEAD_DIM)
    s = jnp.einsum("bshd,bmhd->bhsm", qh, kh).astype(jnp.float32) * (XATTN_HEAD_DIM ** -0.5)
    p = jax.nn.softmax(s, axis=-1).astype(vh.dtype)
    o = jnp.einsum("bhsm,bmhd->bshd", p, vh)
    return o.reshape(B, S, D_XATTN)

def moe_ffn(x, w_router, b_router, w_gu, b_gu, w_down, b_down):
    B, S, D = x.shape
    T = B * S
    TK = T * TOP_K
    xt = x.reshape(T, D)
    logits = (xt @ w_router + b_router).astype(jnp.float32)
    top_vals, top_idx = lax.top_k(logits, TOP_K)
    gates = jax.nn.softmax(top_vals, axis=-1)
    flat_e = top_idx.reshape(-1).astype(jnp.int32)
    flat_tok = jnp.arange(TK, dtype=jnp.int32) // TOP_K
    order = jnp.argsort(flat_e, stable=True)
    sorted_e = flat_e[order]
    sorted_tok = flat_tok[order]
    sorted_gate = gates.reshape(-1)[order]
    counts = jnp.bincount(flat_e, length=N_EXPERTS)
    padded = ((counts + MOE_BLOCK - 1) // MOE_BLOCK) * MOE_BLOCK
    pad_end = jnp.cumsum(padded)
    pad_start = pad_end - padded
    start = jnp.cumsum(counts) - counts
    dest = pad_start[sorted_e] + (jnp.arange(TK, dtype=jnp.int32) - start[sorted_e])
    n_blocks = (TK + N_EXPERTS * (MOE_BLOCK - 1) + MOE_BLOCK - 1) // MOE_BLOCK
    n_pad = n_blocks * MOE_BLOCK
    buf_tok = jnp.full((n_pad,), T, jnp.int32).at[dest].set(sorted_tok)
    buf_gate = jnp.zeros((n_pad,), jnp.float32).at[dest].set(sorted_gate)
    block_start = jnp.arange(n_blocks, dtype=jnp.int32) * MOE_BLOCK
    block_e = jnp.minimum(jnp.searchsorted(pad_end, block_start, side="right"), N_EXPERTS - 1)
    xpad = jnp.concatenate([xt, jnp.zeros((1, D), xt.dtype)], axis=0)

    def expert_block(args):
        e, tok = args
        xb = xpad[tok]
        gu = xb @ w_gu[e] + b_gu[e]
        g, up = jnp.split(gu, 2, axis=-1)
        g = jnp.minimum(g, SWIGLU_LIMIT)
        up = jnp.clip(up, -SWIGLU_LIMIT, SWIGLU_LIMIT)
        glu = g * jax.nn.sigmoid(g * SWIGLU_ALPHA)
        return ((up + 1.0) * glu) @ w_down[e] + b_down[e]

    yb = lax.map(expert_block, (block_e, buf_tok.reshape(n_blocks, MOE_BLOCK)))
    y = yb.reshape(n_pad, D) * buf_gate[:, None].astype(yb.dtype)
    out = jnp.zeros((T + 1, D), yb.dtype).at[buf_tok].add(y)[:T]
    return out.reshape(B, S, D)

def setup_inputs(seed: int = 0) -> dict:
    key = jax.random.key(seed)
    ks = jax.random.split(key, 24)
    f32 = jnp.float32
    L = DEPTH

    def nrm(k, shape, scale):
        return jax.random.normal(k, shape, f32) * scale

    a_c = jax.random.uniform(ks[9], (L, D_RNN), f32, 0.9, 0.999)
    a0 = a_c ** (1.0 / LRU_C)
    lru_lambda = jnp.log(a0) - jnp.log1p(-a0)
    return {
        "x": nrm(ks[0], (BATCH, SEQ, D_MODEL), 1.0),
        "mem": nrm(ks[1], (BATCH, N_MEM, D_MODEL), 1.0),
        "norm_mix_g": 1.0 + nrm(ks[2], (L, D_MODEL), 0.02),
        "w_in": nrm(ks[3], (L, D_MODEL, D_IN), D_MODEL ** -0.5),
        "conv_w": nrm(ks[4], (L, CONV_WIDTH, D_RNN), CONV_WIDTH ** -0.5),
        "conv_b": nrm(ks[5], (L, D_RNN), 0.01),
        "w_rg_a": nrm(ks[6], (L, RNN_HEADS, RNN_HEAD_DIM, RNN_HEAD_DIM), RNN_HEAD_DIM ** -0.5),
        "b_rg_a": nrm(ks[7], (L, D_RNN), 0.01),
        "w_rg_i": nrm(ks[8], (L, RNN_HEADS, RNN_HEAD_DIM, RNN_HEAD_DIM), RNN_HEAD_DIM ** -0.5),
        "b_rg_i": nrm(ks[10], (L, D_RNN), 0.01),
        "lru_lambda": lru_lambda,
        "w_pool": nrm(ks[11], (L, POOL_GROUPS, POOL_GROUP_DIM, POOL_GROUP_DIM), POOL_GROUP_DIM ** -0.5),
        "pool_scale": 1.0 + nrm(ks[12], (L, D_POOL), 0.1),
        "mem_norm_g": 1.0 + nrm(ks[13], (L, D_MODEL), 0.02),
        "w_mem_kv": nrm(ks[14], (L, D_MODEL, 2 * D_XATTN), D_MODEL ** -0.5),
        "w_out": nrm(ks[15], (L, D_MIX, D_MODEL), D_MIX ** -0.5),
        "norm_ffn_g": 1.0 + nrm(ks[16], (L, D_MODEL), 0.02),
        "w_router": nrm(ks[17], (L, D_MODEL, N_EXPERTS), D_MODEL ** -0.5),
        "b_router": nrm(ks[18], (L, N_EXPERTS), 0.01),
        "w_gu": nrm(ks[19], (L, N_EXPERTS, D_MODEL, 2 * D_FF), D_MODEL ** -0.5),
        "b_gu": nrm(ks[20], (L, N_EXPERTS, 2 * D_FF), 0.01),
        "w_down": nrm(ks[21], (L, N_EXPERTS, D_FF, D_MODEL), D_FF ** -0.5),
        "b_down": nrm(ks[22], (L, N_EXPERTS, D_MODEL), 0.01),
        "final_norm_g": 1.0 + nrm(ks[23], (D_MODEL,), 0.02),
    }

def reference(x, mem, norm_mix_g, w_in, conv_w, conv_b, w_rg_a, b_rg_a, w_rg_i, b_rg_i,
              lru_lambda, w_pool, pool_scale, mem_norm_g, w_mem_kv, w_out, norm_ffn_g,
              w_router, b_router, w_gu, b_gu, w_down, b_down, final_norm_g):
    for l in range(DEPTH):
        h = rmsnorm(x, norm_mix_g[l])
        proj = h @ w_in[l]
        u_rnn = proj[..., :D_RNN]
        g_rnn = proj[..., D_RNN:2 * D_RNN]
        u_pool = proj[..., 2 * D_RNN:2 * D_RNN + D_POOL]
        q_mem = proj[..., 2 * D_RNN + D_POOL:]
        y_rnn = rg_lru(causal_depthwise_conv(u_rnn, conv_w[l], conv_b[l]),
                       w_rg_a[l], b_rg_a[l], w_rg_i[l], b_rg_i[l], lru_lambda[l])
        y_rnn = y_rnn * jax.nn.gelu(g_rnn)
        y_pool = multiscale_pool(u_pool, w_pool[l], pool_scale[l])
        y_mem = memory_cross_attention(q_mem, rmsnorm(mem, mem_norm_g[l]), w_mem_kv[l])
        mixed = jnp.concatenate([y_rnn, y_pool, y_mem], axis=-1)
        x = x + mixed @ w_out[l]
        x = x + moe_ffn(rmsnorm(x, norm_ffn_g[l]), w_router[l], b_router[l],
                        w_gu[l], b_gu[l], w_down[l], b_down[l])
    return rmsnorm(x, final_norm_g)


_drawn_inputs = setup_inputs


def setup_inputs(seed=0):
    import zlib

    import numpy as np

    out = dict(_drawn_inputs(seed))
    spreads = {}
    factors = {'b_rg_a': 52.001,
     'b_rg_i': 31.595,
     'mem_norm_g': 4.605,
     'b_gu': 8.0,
     'b_down': 8.0,
     'final_norm_g': 8.448,
     'b_router': 2.97}
    for name, (base, spread) in spreads.items():
        noise = np.random.default_rng([zlib.crc32(name.encode()), seed]).standard_normal(out[name].shape)
        drawn = base * np.exp(spread * noise) if base else spread * noise
        out[name] = __import__('jax').numpy.asarray(drawn.astype(out[name].dtype))
    for name, factor in factors.items():
        out[name] = (out[name] * factor).astype(out[name].dtype)
    return out
```

```python
import concourse.bass as bass
import numpy as np
from concourse import mybir
from contextlib import ExitStack

F32 = mybir.dt.float32
F32R = mybir.dt.float32r
I32 = mybir.dt.int32
U32 = mybir.dt.uint32
ALU = mybir.AluOpType
ACT = mybir.ActivationFunctionType
AX = mybir.AxisListType

P = 128
SEQ, D = 1024, 1024
TT, KT = SEQ // P, D // P
HALF = 512
N_MEM = 256
MT = N_MEM // P
D_RNN, D_POOL, D_XATTN = 512, 256, 256
D_IN = 2 * D_RNN + D_POOL + D_XATTN
RT, PT_ = D_RNN // P, D_POOL // P
CONV = 4
POOL_WINDOWS = (2, 4, 8, 16)
PAD = max(POOL_WINDOWS)
HEADS, HD = 4, 64
E, TOPK = 32, 4
FF = D
EPS = 1e-6
LRU_C = 8.0
SWIGLU_ALPHA, SWIGLU_LIMIT = 1.702, 7.0

UNIT = 256
CAP = SEQ
UNITS_PER_E = CAP // UNIT
DUMP = P
ROWS = SEQ + DUMP
GU_CH, DN_CH = 4, 2
CH = GU_CH + DN_CH
HALFK = KT // 2
RAW = 4
SPLIT = 6
AHEAD = SPLIT // 2

V_CONVW, V_CONVB, V_BA, V_BI, V_LAM, V_PS, V_GMIX, V_GMEM, V_N = 0, 16, 20, 24, 28, 32, 34, 42, 50


def hold(eng, sem, value, held):
    eng.wait_ge(sem, value)
    eng.sem_inc(held, 1)


def ring_value(item, slots):
    return 16 * (item // slots + 1)


def mixer_phase(nc, dram, scratch, shared):
    ctx = ExitStack()
    with ctx:
        def sb(name, shape, dt=F32):
            return ctx.enter_context(nc.sbuf_tensor(name, shape, dt))

        def sem(name):
            return ctx.enter_context(nc.semaphore(name))

        raw, utab, ps = shared["raw"], shared["utab"], shared["ps"]

        def bank(i, n=1):
            return ps[:, i:i + n, :]

        rows = sb("rows", [P, 3, D])
        region_a = sb("region_a", [P, KT * SEQ])
        xnT = region_a[:, :].rearrange("p (k t) -> p k t", k=KT)
        w_out_sb = region_a[:, :].rearrange("p (k n) -> p k n", k=KT)
        mixedT = sb("mixedT", [P, KT, SEQ])
        w_in_sb = sb("w_in_sb", [P, 3, KT, P])
        region_c = sb("region_c", [P, 3 * (PAD + SEQ) + 4 * SEQ])

        def c_tile(i):
            if i < 3:
                return region_c[:, i * (PAD + SEQ):(i + 1) * (PAD + SEQ)]
            o = 3 * (PAD + SEQ) + (i - 3) * SEQ
            return region_c[:, o:o + SEQ]

        u_pad, r_pad, i_pad = c_tile(0), c_tile(1), c_tile(2)
        uc, a_t, m_t, g_t = c_tile(3), c_tile(4), c_tile(5), c_tile(6)
        x2 = [c_tile(0)[:, 0:D], c_tile(1)[:, 0:D]]
        h2 = [c_tile(2)[:, 0:D], c_tile(3)]
        h2T = [c_tile(4).rearrange("p (k t) -> p k t", k=KT), c_tile(5).rearrange("p (k t) -> p k t", k=KT)]
        g2_row = c_tile(6)
        region_d = sb("region_d", [P, KT * 2 * D_XATTN + KT * N_MEM])
        w_kv_sb = region_d[:, 0:KT * 2 * D_XATTN].rearrange("p (k n) -> p k n", k=KT)
        memnT = region_d[:, KT * 2 * D_XATTN:].rearrange("p (k m) -> p k m", k=KT)
        prob = region_d[:, 0:2 * D].rearrange("p (b h m) -> p b h m", b=2, h=HEADS)
        probT = region_d[:, 2 * D:4 * D].rearrange("p (b h c t) -> p b h c t", b=2, h=HEADS, c=MT)
        qT = region_d[:, 4 * D:4 * D + 2 * SEQ].rearrange("p (c t) -> p c t", c=2)
        kT = sb("kT", [P, 2, N_MEM])
        v_sb = sb("v_sb", [P, MT, D_XATTN])
        ident = sb("ident", [P, P])
        lower = sb("lower", [P, P])
        ones = sb("ones", [P, P])
        blockdiag = sb("blockdiag", [P, 10, P])
        vrows = sb("vrows", [64, P])
        vec = sb("vec", [P, V_N])
        small = sb("small", [P, 64])
        lam = sb("lam", [P, 8, RT])
        inv_w = sb("inv_w", [P, PT_, PAD])
        iota_e = sb("iota_e", [P, E])
        iota_p = sb("iota_p", [P, 1])
        tokid = sb("tokid", [P, TT], I32)
        empty = a_t[:, 0:2 * UNIT].bitcast(I32).rearrange("p (s w) -> p s w", w=2)
        w_r_sb = sb("w_r_sb", [P, KT, E])
        b_r_row = sb("b_r_row", [P, E])
        logits = sb("logits", [P, E])
        top8 = sb("top8", [P, 8])
        idx8 = sb("idx8", [P, 8], U32)
        idxf = sb("idxf", [P, TOPK])
        onehot = sb("onehot", [P, TOPK, E])
        picked = sb("picked", [P, TOPK, E])
        mask = sb("mask", [P, E])
        run = sb("run", [P, E])
        slotm = sb("slotm", [P, E])
        slotf = sb("slotf", [P, TOPK])
        sloti = sb("sloti", [P, TT, TOPK], I32)
        entry = sb("entry", [P, TT, TOPK, 2], I32)
        gexp = sb("gexp", [P, TOPK])
        cnt = sb("cnt", [P, 8, E])
        ucol = sb("ucol", [P, 12])
        mx = sb("mx", [P, 4, HEADS])

        ss, ms, sd, rs = (small[:, i * 10:(i + 1) * 10] for i in range(4))
        ss2, ms2, sd2, rs2 = (small[:, 40 + i * 2:42 + i * 2] for i in range(4))

        rows_in = [sem(f"rows_in{i}") for i in range(3)]
        w_in_in = [sem(f"w_in_in{i}") for i in range(3)]
        vrows_in, bd_in, kv_in, wout_in, router_in = (sem(n) for n in ("vrows_in", "bd_in", "kv_in", "wout_in", "router_in"))
        gain_in = sem("gain_in_ffn")
        consts, bd_zero, zero_set, zero_out, table_set = (sem(n) for n in ("consts", "bd_zero", "zero_set", "zero_out", "table_set"))
        vecT_ready, vec_done, lam_abs, lam_exp, lam_done, inv_done = (sem(n) for n in ("vecT_ready", "vec_done", "lam_abs", "lam_exp", "lam_done", "inv_done"))
        ss_done, ms_done, sd_done, xn_done, xT_ready, xT_done = (sem(n) for n in ("ss_done", "ms_done", "sd_done", "xn_done", "xT_ready", "xT_done"))
        proj_ready, proj_free, kv_ready, kv_done = (sem(n) for n in ("proj_ready", "proj_free", "kv_ready", "kv_done"))
        u_done, pu_done, conv_done, gates_ready, sig_done, tanh_done, neg_done, mult_done, gelu_done, rnn_done = (
            sem(n) for n in ("u_done", "pu_done", "conv_done", "gates_ready", "sig_done", "tanh_done", "neg_done", "mult_done", "gelu_done", "rnn_done"))
        pads_zero, d_done, pool_ready, pool_done, q_done = (sem(n) for n in ("pads_zero", "d_done", "pool_ready", "pool_done", "q_done"))
        s_ready, nmax_done, exp_done, prob_done, pT_ready, pT_done, o_ready, o_done = (
            sem(n) for n in ("s_ready", "nmax_done", "exp_done", "prob_done", "pT_ready", "pT_done", "o_ready", "o_done"))
        out_ready, x2_done, ss2_done, ms2_done, sd2_done, h2_done, h2T_ready, h2T_done = (
            sem(n) for n in ("out_ready", "x2_done", "ss2_done", "ms2_done", "sd2_done", "h2_done", "h2T_ready", "h2T_done"))
        stored = [sem("stored0"), sem("stored1")]
        logits_ready, logits_done, top_done, gexp_done, mask_done, rank_ready, slot_done, scattered = (
            sem(n) for n in ("logits_ready", "logits_done", "top_done", "gexp_done", "mask_done", "rank_ready", "slot_done", "scattered"))
        ucol_done, utab_ready = sem("ucol_done"), sem("utab_ready")
        dve_step, pool_step = sem("dve_step"), sem("pool_step")

        NORMED = TT + MT
        NPROJ = D_IN // P
        PROJ = [c for r in range(RT) for c in (r, RT + r)] + list(range(2 * RT, NPROJ))

        block = ctx.enter_context(nc.Block("mixer"))

        @block.sync
        def _(sp):
            def load_rows(item):
                if item < TT or item >= NORMED:
                    t = item if item < TT else item - NORMED
                    src = dram["x"][0, t * P:(t + 1) * P, :]
                else:
                    src = dram["mem"][0, (item - TT) * P:(item - TT + 1) * P, :]
                sp.dma_start(rows[:, item % 3, :], src).then_inc(rows_in[item % 3], 16)

            def load_w_in(n):
                c = PROJ[n]
                sp.dma_start(w_in_sb[:, n % 3, :, :],
                             dram["w_in"][0].rearrange("(k p) n -> p k n", p=P)[:, :, c * P:(c + 1) * P])\
                    .then_inc(w_in_in[n % 3], 16)

            for item in range(3):
                load_rows(item)
            load_w_in(0)
            for item in range(3, NORMED):
                sp.wait_ge(xT_ready, item - 2)
                load_rows(item)
                if item == 4:
                    load_w_in(1)
                if item == 6:
                    load_w_in(2)
            sp.dma_start(w_kv_sb, dram["w_mem_kv"][0].rearrange("(k p) n -> p k n", p=P)).then_inc(kv_in, 16)
            for n in range(3, NPROJ):
                sp.wait_ge(proj_ready, 2 * (n - 2))
                load_w_in(n)
                if n == 3:
                    for item in range(NORMED, NORMED + 3):
                        sp.wait_ge(xT_ready, item - 2)
                        load_rows(item)
                if n >= 4 and n < 4 + RAW:
                    load_half(sp, dram, shared, 0, n - 4)
            sp.wait_ge(proj_ready, 2 * NPROJ)
            sp.dma_start(w_out_sb, dram["w_out"][0].rearrange("(k p) n -> p k n", p=P)).then_inc(wout_in, 16)
            sp.wait_ge(rnn_done, RT)
            sp.dma_start(g2_row, dram["norm_ffn_g"][0:1, :].broadcast_to([P, D])).then_inc(gain_in, 16)
            for t in range(TT):
                sp.wait_ge(h2_done, t + 1)
                sp.dma_start(scratch["acc"][t * P:(t + 1) * P, :], x2[t % 2]).then_inc(stored[t % 2], 16)
                sp.dma_start(scratch["h2"][t * P:(t + 1) * P, :], h2[t % 2]).then_inc(stored[t % 2], 16)
                if t + 3 < TT:
                    sp.wait_ge(x2_done, t + 1)
                    load_rows(NORMED + t + 3)
            for i in range(2):
                sp.wait_ge(stored[i], 32 * (TT // 2))
            sp.wait_ge(zero_out, 32)
            sp.wait_ge(scattered, 16 * TT * TOPK)

        @block.gpsimd
        def _(pool):
            pool.memset(ident[:, :], 0.0).then_inc(pool_step, 1)
            pool.memset(ones[:, :], 1.0).then_inc(pool_step, 1)
            pool.memset(vrows[:, :], 0.0).then_inc(pool_step, 1)
            pool.wait_ge(pool_step, 3)
            vector_rows = [
                (V_CONVW, CONV * RT, dram["conv_w"][0].rearrange("w (c p) -> (w c) p", p=P)),
                (V_CONVB, RT, dram["conv_b"][0].rearrange("(c p) -> c p", p=P)),
                (V_BA, RT, dram["b_rg_a"][0].rearrange("(c p) -> c p", p=P)),
                (V_BI, RT, dram["b_rg_i"][0].rearrange("(c p) -> c p", p=P)),
                (V_LAM, RT, dram["lru_lambda"][0].rearrange("(c p) -> c p", p=P)),
                (V_PS, PT_, dram["pool_scale"][0].rearrange("(c p) -> c p", p=P)),
                (V_GMIX, KT, dram["norm_mix_g"][0].rearrange("(c p) -> c p", p=P)),
                (V_GMEM, KT, dram["mem_norm_g"][0].rearrange("(c p) -> c p", p=P)),
            ]
            for r, n, src in vector_rows:
                pool.dma_start(vrows[r:r + n, :], src).then_inc(vrows_in, 16)
            pool.affine_select(out=ident[:, :], in_=ident[:, :], compare_op=ALU.not_equal, fill=1.0,
                               base=0, pattern=[[-1, P]], channel_multiplier=1).then_inc(consts, 1)
            pool.affine_select(out=lower[:, :], in_=ones[:, :], compare_op=ALU.is_gt, fill=0.0,
                               base=0, pattern=[[1, P]], channel_multiplier=-1).then_inc(consts, 1)
            pool.iota(iota_e[:, :], [[1, E]], base=0, channel_multiplier=0,
                      allow_small_or_imprecise_dtypes=True).then_inc(consts, 1)
            pool.iota(iota_p[:, :], [[0, 1]], base=0, channel_multiplier=1,
                      allow_small_or_imprecise_dtypes=True).then_inc(consts, 1)
            pool.iota(tokid[:, :], [[P, TT]], base=0, channel_multiplier=1).then_inc(consts, 1)
            for j in range(PT_):
                pool.iota(inv_w[:, j, :], [[1, PAD]], base=1, channel_multiplier=0,
                          allow_small_or_imprecise_dtypes=True).then_inc(consts, 1)
            pool.iota(run[:, :], [[CAP, E]], base=0, channel_multiplier=0,
                      allow_small_or_imprecise_dtypes=True).then_inc(consts, 1)
            pool.memset(blockdiag[:, :, :], 0.0).then_inc(bd_zero, 1)
            pool.wait_ge(bd_zero, 1)
            maps = [(0, RT, dram["w_rg_a"][0]), (RT, RT, dram["w_rg_i"][0]), (2 * RT, PT_, dram["w_pool"][0])]
            for first, n, w in maps:
                pairs = w.rearrange("(c two) i j -> two i c j", two=2)
                pool.dma_start(blockdiag[0:HD, first:first + n, 0:HD], pairs[0]).then_inc(bd_in, 16)
                pool.dma_start(blockdiag[HD:P, first:first + n, HD:P], pairs[1]).then_inc(bd_in, 16)
            pool.memset(r_pad, 0.0).then_inc(zero_set, 1)
            pool.memset(i_pad[:, 0:PAD], 0.0).then_inc(pads_zero, 1)
            pool.memset(u_pad[:, 0:PAD], 0.0).then_inc(pads_zero, 1)
            pool.iota(empty[:, :, 0].rearrange("p (b s) -> p b s", b=2), [[0, 2], [1, P]], base=SEQ,
                      channel_multiplier=0).then_inc(zero_set, 1)
            pool.memset(empty[:, :, 1], 0).then_inc(zero_set, 1)
            pool.wait_ge(zero_set, 3)
            pool.dma_start(scratch["acc"][SEQ:ROWS, :], r_pad[:, 0:D]).then_inc(zero_out, 16)
            pool.dma_start(scratch["h2"][SEQ:ROWS, :], r_pad[:, 0:D]).then_inc(zero_out, 16)
            pool.dma_start(scratch["table"].rearrange("(p s) w -> p s w", p=P), empty[:, :, :]).then_inc(table_set, 16)
            pool.dma_start(w_r_sb[:, :, :], dram["w_router"][0].rearrange("(k p) n -> p k n", p=P)).then_inc(router_in, 16)
            pool.dma_start(b_r_row[:, :], dram["b_router"][0:1, :].broadcast_to([P, E])).then_inc(router_in, 16)
            pool.wait_ge(table_set, 16)
            for t in range(TT):
                pool.wait_ge(slot_done, t + 1)
                for j in range(TOPK):
                    pool.indirect_dma_start(
                        out=scratch["table"], out_offset=bass.IndirectOffsetOnAxis(ap=sloti[:, t, j:j + 1], axis=0),
                        in_=entry[:, t, j, :], in_offset=None).then_inc(scattered, 16)

        @block.scalar
        def _(act):
            def norms():
                for s in range(NORMED):
                    act.wait_ge(rows_in[s % 3], ring_value(s, 3))
                    if s:
                        act.wait_ge(ss_done, s)
                    nc.scalar.activation(g_t, rows[:, s % 3, :], ACT.Square, accum_out=ss[:, s:s + 1])\
                        .then_inc(ss_done, 1)
                    act.wait_ge(ms_done, s + 1)
                    nc.scalar.activation(sd[:, s:s + 1], ms[:, s:s + 1], ACT.Sqrt).then_inc(sd_done, 1)

            norms()
            act.wait_ge(lam_abs, 1)
            nc.scalar.activation(lam[:, 1, :], lam[:, 0, :], ACT.Exp, scale=-1.0).then_inc(lam_exp, 1)
            act.wait_ge(pads_zero, 2)
            act.wait_ge(zero_out, 32)
            act.wait_ge(table_set, 16)
            act.wait_ge(vec_done, 1)
            act.wait_ge(lam_done, 1)
            for c in range(RT):
                if c:
                    act.wait_ge(conv_done, c)
                for h in range(2):
                    act.wait_ge(proj_ready, 4 * c + h + 1)
                    nc.scalar.activation(u_pad[:, PAD + h * HALF:PAD + (h + 1) * HALF], bank(2 * ((2 * c) % 2) + h)[:, 0, :],
                                         ACT.Copy).then_inc(u_done, 1)
                if c:
                    act.wait_ge(rnn_done, c)
                act.wait_ge(ss_done, NORMED)
                for h in range(2):
                    act.wait_ge(proj_ready, 4 * c + 2 + h + 1)
                    nc.scalar.activation(g_t[:, h * HALF:(h + 1) * HALF], bank(2 + h)[:, 0, :],
                                         ACT.Gelu_apprx_tanh).then_inc(gelu_done, 1)
                if c == 0:
                    act.wait_ge(kv_ready, 1)
                    nc.scalar.activation(kT[:, :, :], bank(4)[:, 0, :].rearrange("p (c m) -> p c m", c=2), ACT.Copy)\
                        .then_inc(kv_done, 1)
                    nc.scalar.activation(v_sb[:, :, :], bank(5)[:, 0, :].rearrange("p (c m) -> p c m", c=MT), ACT.Copy)\
                        .then_inc(kv_done, 1)
                act.wait_ge(gates_ready, c + 1)
                r_f, i_f = r_pad[:, 0:SEQ], i_pad[:, 0:SEQ]
                nc.scalar.activation(r_f, bank(4, 2).rearrange("p b n -> p (b n)"), ACT.Sigmoid,
                                     bias=vec[:, V_BA + c:V_BA + c + 1]).then_inc(sig_done, 1)
                nc.scalar.activation(i_f, bank(6, 2).rearrange("p b n -> p (b n)"), ACT.Sigmoid,
                                     bias=vec[:, V_BI + c:V_BI + c + 1]).then_inc(sig_done, 1)
                act.wait_ge(sig_done, 2 * c + 1)
                nc.scalar.activation(a_t, r_f, ACT.Tanh, scale=lam[:, 7, c:c + 1]).then_inc(tanh_done, 1)
                act.wait_ge(neg_done, c + 1)
                nc.scalar.activation(r_f, r_f, ACT.Sqrt).then_inc(mult_done, 1)
            for j in range(PT_):
                n = 2 * RT + j
                if j == 0:
                    act.wait_ge(conv_done, RT)
                else:
                    act.wait_ge(d_done, j)
                for h in range(2):
                    act.wait_ge(proj_ready, 2 * n + h + 1)
                    nc.scalar.activation(u_pad[:, PAD + h * HALF:PAD + (h + 1) * HALF], bank(2 * (n % 2) + h)[:, 0, :],
                                         ACT.Copy).then_inc(pu_done, 1)
            for j in range(2):
                n = 2 * RT + PT_ + j
                for h in range(2):
                    act.wait_ge(proj_ready, 2 * n + h + 1)
                    nc.scalar.activation(qT[:, j, h * HALF:(h + 1) * HALF], bank(2 * (n % 2) + h)[:, 0, :],
                                         ACT.Copy).then_inc(q_done, 1)
            for j in range(PT_):
                act.wait_ge(pool_ready, j + 1)
                nc.scalar.activation(mixedT[:, RT + j, :], bank(4 + 2 * j, 2).rearrange("p b n -> p (b n)"), ACT.Copy,
                                     scale=vec[:, V_PS + j:V_PS + j + 1]).then_inc(pool_done, 1)

            def probT_evac(t):
                act.wait_ge(pT_ready, t + 1)
                if t >= 2:
                    act.wait_ge(o_ready, t - 1)
                for b in range(2):
                    nc.scalar.activation(probT[:, t % 2, 2 * b:2 * b + 2, :, :],
                                         bank(b)[:, 0, :].rearrange("p (h c t) -> p h c t", h=2, c=MT), ACT.Copy)\
                        .then_inc(pT_done, 1)

            for t in range(TT):
                act.wait_ge(nmax_done, t + 1)
                if t >= 2:
                    act.wait_ge(pT_ready, t - 1)
                for h in range(HEADS):
                    at = 2 * (h % 2) + h // 2
                    nc.scalar.activation(prob[:, t % 2, h, :], ps[:, 4 + 2 * (t % 2) + h % 2, (h // 2) * N_MEM:(h // 2 + 1) * N_MEM],
                                         ACT.Exp, bias=mx[:, 1, at:at + 1], scale=HD ** -0.5,
                                         accum_out=mx[:, 2, h:h + 1]).then_inc(exp_done, 1)
                if t:
                    probT_evac(t - 1)
            probT_evac(TT - 1)

            def h2T_evac(t):
                act.wait_ge(h2T_ready, t + 1)
                if t >= 2:
                    act.wait_ge(logits_ready, t - 1)
                for b in range(2):
                    nc.scalar.activation(h2T[t % 2][:, 4 * b:4 * b + 4, :], bank(4 + b)[:, 0, :].rearrange("p (k t) -> p k t", k=4),
                                         ACT.Copy).then_inc(h2T_done, 1)

            def gate_exp(t):
                act.wait_ge(top_done, t + 1)
                nc.scalar.activation(gexp[:, :], top8[:, 0:TOPK], ACT.Exp, bias=small[:, 48:49],
                                     accum_out=small[:, 49:50]).then_inc(gexp_done, 1)

            act.wait_ge(rnn_done, RT)
            for t in range(TT):
                act.wait_ge(x2_done, t + 1)
                if t >= 2:
                    act.wait_ge(stored[t % 2], 32 * (t // 2))
                nc.scalar.activation(h2[t % 2], x2[t % 2], ACT.Square, accum_out=ss2[:, t % 2:t % 2 + 1]).then_inc(ss2_done, 1)
                act.wait_ge(ms2_done, t + 1)
                nc.scalar.activation(sd2[:, t % 2:t % 2 + 1], ms2[:, t % 2:t % 2 + 1], ACT.Sqrt).then_inc(sd2_done, 1)
                if t:
                    h2T_evac(t - 1)
                    if t >= 2:
                        gate_exp(t - 2)
            h2T_evac(TT - 1)
            gate_exp(TT - 2)
            gate_exp(TT - 1)

        @block.vector
        def _(dve):
            steps = [0]

            def link(ins):
                steps[0] += 1
                ins.then_inc(dve_step, 1)
                dve.wait_ge(dve_step, steps[0])

            V = nc.vector

            def vector_columns():
                dve.wait_ge(vecT_ready, 1)
                V.tensor_copy(vec[:, :], bank(0)[:, 0, 0:V_N]).then_inc(vec_done, 1)

            def row_scale(s):
                dve.wait_ge(sd_done, s + 1)
                link(V.reciprocal(rs[:, s:s + 1], sd[:, s:s + 1]))
                V.tensor_scalar(rows[:, s % 3, :], rows[:, s % 3, :], rs[:, s:s + 1], None, ALU.mult).then_inc(xn_done, 1)

            def mean_square(s):
                dve.wait_ge(ss_done, s + 1)
                V.tensor_scalar(ms[:, s:s + 1], ss[:, s:s + 1], 1.0 / D, EPS, ALU.mult, ALU.add).then_inc(ms_done, 1)

            def xT_evac(s):
                dve.wait_ge(xT_ready, s + 1)
                gain = V_GMIX if s < TT else V_GMEM
                for b in range(2):
                    dst = xnT[:, 4 * b:4 * b + 4, s * P:(s + 1) * P] if s < TT else \
                        memnT[:, 4 * b:4 * b + 4, (s - TT) * P:(s - TT + 1) * P]
                    V.tensor_tensor(dst, bank(4 + 2 * (s % 2) + b)[:, 0, :].rearrange("p (k t) -> p k t", k=4),
                                    vec[:, gain + 4 * b:gain + 4 * b + 4].unsqueeze(2).broadcast_to([P, 4, P]),
                                    ALU.mult).then_inc(xT_done, 1)

            mean_square(0)
            row_scale(0)
            vector_columns()
            dve.wait_ge(vec_done, 1)
            for s in range(1, NORMED):
                mean_square(s)
                xT_evac(s - 1)
                row_scale(s)
            xT_evac(NORMED - 1)

            y, z, s_, s2_, p_, t_ = (lam[:, i, :] for i in (2, 1, 3, 4, 5, 6))
            link(V.tensor_scalar(y, vec[:, V_LAM:V_LAM + RT], -1.0, None, ALU.mult))
            V.tensor_tensor(lam[:, 0, :], y, vec[:, V_LAM:V_LAM + RT], ALU.max).then_inc(lam_abs, 1)
            dve.wait_ge(lam_exp, 1)
            link(V.tensor_scalar(t_, z, 2.0, None, ALU.add))
            link(V.reciprocal(t_, t_))
            link(V.tensor_tensor(s_, z, t_, ALU.mult))
            link(V.tensor_tensor(s2_, s_, s_, ALU.mult))
            link(V.tensor_scalar(p_, s2_, 1.0 / 17, None, ALU.mult))
            for k in (15, 13, 11, 9, 7, 5, 3):
                link(V.scalar_tensor_tensor(p_, p_, 1.0 / k, s2_, ALU.add, ALU.mult))
            link(V.scalar_tensor_tensor(p_, p_, 1.0, s_, ALU.add, ALU.mult))
            link(V.tensor_scalar(p_, p_, 2.0, None, ALU.mult))
            link(V.scalar_tensor_tensor(t_, y, 0.0, p_, ALU.max, ALU.add))
            V.tensor_scalar(lam[:, 7, :], t_, -LRU_C / 2, None, ALU.mult).then_inc(lam_done, 1)
            dve.wait_ge(consts, 8)
            for j in range(PT_):
                for g in range(2):
                    part = inv_w[g * HD:(g + 1) * HD, j, :]
                    link(V.tensor_scalar(part, part, float(POOL_WINDOWS[2 * j + g]), None, ALU.min))
            link(V.reciprocal(inv_w[:, :, :], inv_w[:, :, :]))

            U0 = PAD - (CONV - 1)
            r_f, i_f = r_pad[:, 0:SEQ], i_pad[:, 0:SEQ]
            for c in range(RT):
                dve.wait_ge(u_done, 2 * c + 2)
                tap = [vec[:, V_CONVW + w * RT + c:V_CONVW + w * RT + c + 1] for w in range(CONV)]
                link(V.tensor_scalar(uc, u_pad[:, PAD:PAD + SEQ], tap[CONV - 1], vec[:, V_CONVB + c:V_CONVB + c + 1],
                                     ALU.mult, ALU.add))
                for w in range(CONV - 1):
                    ins = V.scalar_tensor_tensor(uc, u_pad[:, U0 + w:U0 + w + SEQ], tap[w], uc, ALU.mult, ALU.add)
                    if w < CONV - 2:
                        link(ins)
                    else:
                        ins.then_inc(conv_done, 1)
                dve.wait_ge(tanh_done, c + 1)
                link(V.tensor_scalar(m_t, a_t, -1.0, 1.0, ALU.mult, ALU.add))
                link(V.reciprocal(m_t, m_t))
                link(V.scalar_tensor_tensor(m_t, a_t, 2.0, m_t, ALU.mult, ALU.mult))
                link(V.scalar_tensor_tensor(r_f, m_t, 2.0, m_t, ALU.add, ALU.mult))
                V.tensor_scalar(r_f, r_f, -1.0, 0.0, ALU.mult, ALU.max).then_inc(neg_done, 1)
                dve.wait_ge(sig_done, 2 * c + 2)
                link(V.tensor_tensor(i_f, i_f, uc, ALU.mult))
                link(V.tensor_scalar(a_t, m_t, 1.0, None, ALU.add))
                dve.wait_ge(mult_done, c + 1)
                link(V.memset(r_f[:, 0:1], 1.0))
                link(V.tensor_tensor(i_f, i_f, r_f, ALU.mult))
                link(V.tensor_tensor_scan(m_t, a_t, i_f, 0.0, ALU.mult, ALU.add))
                dve.wait_ge(gelu_done, 2 * c + 2)
                V.tensor_tensor(mixedT[:, c, :], m_t, g_t, ALU.mult).then_inc(rnn_done, 1)

            dve.wait_ge(rnn_done, RT)
            link(V.memset(r_pad[:, 0:PAD], 0.0))
            for j in range(PT_):
                dve.wait_ge(pu_done, 2 * j + 2)
                W = PAD + SEQ
                src, width = u_pad, 1
                bufs = [r_pad, i_pad]
                n_all = 1 if j == 0 else 3
                for k in range(n_all):
                    lead = 2 * width - 1
                    dst = bufs[k % 2]
                    link(V.tensor_tensor(dst[:, lead:W], src[:, lead:W], src[:, lead - width:W - width], ALU.add))
                    src, width = dst, 2 * width
                other = bufs[n_all % 2]
                lead = 2 * width - 1
                V.tensor_tensor(other[HD:P, lead:W], src[HD:P, lead:W], src[HD:P, lead - width:W - width], ALU.add)\
                    .then_inc(dve_step, 1)
                steps[0] += 1
                link(V.tensor_copy(other[0:HD, PAD:W], src[0:HD, PAD:W]))
                link(V.tensor_tensor(src[:, PAD:2 * PAD], other[:, PAD:2 * PAD], inv_w[:, j, :], ALU.mult))
                if j:
                    dve.wait_ge(pool_ready, j)
                link(V.scalar_tensor_tensor(m_t, other[:, PAD:W], inv_w[:, j, PAD - 1:PAD], u_pad[:, PAD:W],
                                            ALU.mult, ALU.subtract))
                V.tensor_tensor(m_t[:, 0:PAD], src[:, PAD:2 * PAD], u_pad[:, PAD:2 * PAD], ALU.subtract).then_inc(d_done, 1)

            def soft_max(t):
                dve.wait_ge(s_ready, t + 1)
                if t:
                    dve.wait_ge(prob_done, t)
                link(V.tensor_reduce(mx[:, 0, :], bank(4 + 2 * (t % 2), 2).rearrange("p b (h m) -> p (b h) m", h=2),
                                     AX.X, ALU.max))
                V.tensor_scalar(mx[:, 1, :], mx[:, 0, :], -(HD ** -0.5), None, ALU.mult).then_inc(nmax_done, 1)
                dve.wait_ge(exp_done, HEADS * (t + 1))
                link(V.reciprocal(mx[:, 3, :], mx[:, 2, :]))
                V.tensor_tensor(prob[:, t % 2], prob[:, t % 2], mx[:, 3, :].unsqueeze(2).broadcast_to([P, HEADS, N_MEM]),
                                ALU.mult).then_inc(prob_done, 1)

            def o_evac(t):
                dve.wait_ge(o_ready, t + 1)
                V.tensor_copy(mixedT[:, RT + PT_:KT, t * P:(t + 1) * P],
                              bank(2 + t % 2)[:, 0, 0:2 * P].rearrange("p (c t) -> p c t", c=2)).then_inc(o_done, 1)

            for t in range(TT):
                soft_max(t)
                if t:
                    o_evac(t - 1)
            o_evac(TT - 1)

            def residual(t):
                dve.wait_ge(out_ready, t + 1)
                item = NORMED + t
                dve.wait_ge(rows_in[item % 3], ring_value(item, 3))
                if t >= 2:
                    dve.wait_ge(stored[t % 2], 32 * (t // 2))
                V.tensor_tensor(x2[t % 2], bank(2 * (t % 2), 2).rearrange("p b n -> p (b n)"), rows[:, item % 3, :],
                                ALU.add).then_inc(x2_done, 1)

            def norm(t):
                i = t % 2
                dve.wait_ge(ss2_done, t + 1)
                V.tensor_scalar(ms2[:, i:i + 1], ss2[:, i:i + 1], 1.0 / D, EPS, ALU.mult, ALU.add).then_inc(ms2_done, 1)
                dve.wait_ge(sd2_done, t + 1)
                link(V.reciprocal(rs2[:, i:i + 1], sd2[:, i:i + 1]))
                if t >= 2:
                    dve.wait_ge(h2T_ready, t - 1)
                V.scalar_tensor_tensor(h2[i], x2[i], rs2[:, i:i + 1], g2_row, ALU.mult, ALU.mult).then_inc(h2_done, 1)

            def pick(t):
                dve.wait_ge(logits_ready, t + 1)
                link(V.tensor_tensor(logits[:, :], bank(6)[:, 0, 0:E], b_r_row[:, :], ALU.add))
                link(V.max(top8[:, :], logits[:, :]))
                V.tensor_scalar(small[:, 48:49], top8[:, 0:1], -1.0, None, ALU.mult).then_inc(top_done, 1)
                link(V.max_index(idx8[:, :], top8[:, :], logits[:, :]))
                link(V.tensor_copy(idxf[:, :], idx8[:, 0:TOPK]))
                link(V.tensor_tensor(onehot[:, :, :], iota_e[:, :].unsqueeze(1).broadcast_to([P, TOPK, E]),
                                     idxf[:, :].unsqueeze(2).broadcast_to([P, TOPK, E]), ALU.is_equal))
                V.tensor_reduce(mask[:, :], onehot[:, :, :].rearrange("p j e -> p e j"), AX.X, ALU.add).then_inc(mask_done, 1)

            def place(t):
                dve.wait_ge(gexp_done, t + 1)
                link(V.reciprocal(small[:, 50:51], small[:, 49:50]))
                link(V.tensor_scalar(entry[:, t, :, 1].bitcast(F32), gexp[:, :], small[:, 50:51], None, ALU.mult))
                link(V.tensor_copy(entry[:, t, :, 0], tokid[:, t:t + 1].broadcast_to([P, TOPK])))
                dve.wait_ge(rank_ready, t + 1)
                link(V.tensor_tensor(slotm[:, :], bank(7)[:, 0, 0:E], run[:, :], ALU.add))
                link(V.tensor_tensor(run[:, :], bank(7)[:, 0, E:2 * E], run[:, :], ALU.add))
                link(V.tensor_tensor(picked[:, :, :], onehot[:, :, :], slotm[:, :].unsqueeze(1).broadcast_to([P, TOPK, E]),
                                     ALU.mult))
                link(V.tensor_reduce(slotf[:, :], picked[:, :, :], AX.X, ALU.add))
                V.tensor_copy(sloti[:, t, :], slotf[:, :]).then_inc(slot_done, 1)

            dve.wait_ge(router_in, 32)
            dve.wait_ge(gain_in, 16)
            for t in range(TT):
                residual(t)
                norm(t)
                if t >= 2:
                    place(t - 2)
                if t:
                    pick(t - 1)
            place(TT - 2)
            pick(TT - 1)
            place(TT - 1)

            rows_of, total, end, le = cnt[:, 0, :], cnt[:, 1, :], cnt[:, 2, :], cnt[:, 3, :]
            link(V.scalar_tensor_tensor(rows_of, iota_e[:, :], -float(CAP), run[:, :], ALU.mult, ALU.add))
            link(V.tensor_scalar(total, rows_of, 0.0, None, ALU.is_gt))
            link(V.memset(total[:, 0:1], 1.0))
            for k in range(1, UNITS_PER_E):
                link(V.scalar_tensor_tensor(total, rows_of, float(UNIT * k), total, ALU.is_gt, ALU.add))
            link(V.tensor_tensor_scan(end, ones[:, 0:E], total, 0.0, ALU.mult, ALU.add))
            expert, b_, row0, two, first_u, left = (ucol[:, i:i + 1] for i in range(6))
            link(V.tensor_scalar(le, end, iota_p[:, 0:1], None, ALU.is_le))
            link(V.tensor_reduce(expert, le, AX.X, ALU.add))
            link(V.tensor_tensor(cnt[:, 4, :], le, total, ALU.mult))
            link(V.tensor_reduce(first_u, cnt[:, 4, :], AX.X, ALU.add))
            link(V.tensor_tensor(b_, iota_p[:, 0:1], first_u, ALU.subtract))
            link(V.tensor_scalar(cnt[:, 5, :], iota_e[:, :], expert, None, ALU.is_equal))
            link(V.tensor_tensor(cnt[:, 6, :], cnt[:, 5, :], rows_of, ALU.mult))
            link(V.tensor_reduce(left, cnt[:, 6, :], AX.X, ALU.add))
            link(V.scalar_tensor_tensor(left, b_, -float(UNIT), left, ALU.mult, ALU.add))
            link(V.tensor_scalar(ucol[:, 8:9], left, float(P), None, ALU.is_gt))
            link(V.tensor_scalar(ucol[:, 6:7], expert, float(E - 1), None, ALU.min))
            link(V.scalar_tensor_tensor(row0, expert, float(UNITS_PER_E), b_, ALU.mult, ALU.add))
            link(V.tensor_scalar(ucol[:, 7:8], row0, float(E * UNITS_PER_E - 1), None, ALU.min))
            link(V.tensor_scalar(ucol[:, 7:8], ucol[:, 7:8], float(UNIT), None, ALU.mult))
            V.tensor_copy(ucol[:, 9:10], end[:, E - 1:E]).then_inc(ucol_done, 1)
            dve.wait_ge(utab_ready, 1)
            link(V.tensor_copy(utab[0:1, :], bank(6)[0:1, 0, :]))

        @block.tensor
        def _(pe):
            T = nc.tensor
            pe.wait_ge(vrows_in, 16 * 8)
            pe.wait_ge(consts, 1)
            T.transpose(bank(0)[:, 0, 0:V_N], vrows[0:V_N, :], ident[0:V_N, 0:V_N]).then_inc(vecT_ready, 1)
            for s in range(NORMED):
                pe.wait_ge(xn_done, s + 1)
                if s >= 2:
                    pe.wait_ge(xT_done, 2 * (s - 1))
                for k in range(KT):
                    last = T.transpose(bank(4 + 2 * (s % 2) + k // 4)[:, 0, (k % 4) * P:(k % 4 + 1) * P],
                                       rows[:, s % 3, k * P:(k + 1) * P], ident[:, :])
                last.then_inc(xT_ready, 1)

            def project(n):
                pe.wait_ge(w_in_in[n % 3], ring_value(n, 3))
                for h in range(2):
                    if n == 0:
                        pe.wait_ge(xT_done, 2 * 4 * (h + 1))
                        pe.wait_ge(vec_done, 1)
                    if n == 2 or n == 3:
                        pe.wait_ge(u_done if n == 2 else gelu_done, h + 1)
                    elif 4 <= n < 2 * RT + 2:
                        c = (n - 2) // 2
                        pe.wait_ge(u_done if n % 2 == 0 else gelu_done, 2 * c + h + 1)
                    elif n >= 2 * RT + 2:
                        pe.wait_ge(pu_done, 2 * (n - 2 * RT - 2) + h + 1)
                    for k in range(KT):
                        last = T.matmul(bank(2 * (n % 2) + h)[:, 0, :], w_in_sb[:, n % 3, k, :],
                                        xnT[:, k, h * HALF:(h + 1) * HALF], start=(k == 0), stop=(k == KT - 1))
                    last.then_inc(proj_ready, 1)

            def keys_values():
                pe.wait_ge(kv_in, 16)
                pe.wait_ge(xT_done, 2 * NORMED)
                for c in range(2):
                    for k in range(KT):
                        T.matmul(bank(4)[:, 0, c * N_MEM:(c + 1) * N_MEM], w_kv_sb[:, k, c * P:(c + 1) * P],
                                 memnT[:, k, :], start=(k == 0), stop=(k == KT - 1))
                for m in range(MT):
                    for k in range(KT):
                        last = T.matmul(bank(5)[:, 0, m * D_XATTN:(m + 1) * D_XATTN], memnT[:, k, m * P:(m + 1) * P],
                                        w_kv_sb[:, k, D_XATTN:2 * D_XATTN], start=(k == 0), stop=(k == KT - 1))
                last.then_inc(kv_ready, 1)

            def gates(c):
                pe.wait_ge(conv_done, c + 1)
                pe.wait_ge(bd_in, 16 * 6)
                if c == 0:
                    pe.wait_ge(kv_done, 2)
                else:
                    pe.wait_ge(sig_done, 2 * c)
                for g in range(2):
                    for h in range(2):
                        last = T.matmul(bank(4 + 2 * g + h)[:, 0, :], blockdiag[:, g * RT + c, :],
                                        uc[:, h * HALF:(h + 1) * HALF], start=True, stop=True)
                last.then_inc(gates_ready, 1)

            for c in range(RT):
                project(2 * c)
                project(2 * c + 1)
                if c == 0:
                    keys_values()
                gates(c)

            def pool_map(j):
                pe.wait_ge(d_done, j + 1)
                if j == 0:
                    pe.wait_ge(sig_done, 2 * RT)
                for h in range(2):
                    last = T.matmul(bank(4 + 2 * j + h)[:, 0, :], blockdiag[:, 2 * RT + j, :],
                                    m_t[:, h * HALF:(h + 1) * HALF], start=True, stop=True)
                last.then_inc(pool_ready, 1)

            project(2 * RT)
            project(2 * RT + 1)
            project(2 * RT + 2)
            pool_map(0)
            project(2 * RT + 3)
            pool_map(1)

            def scores(t):
                if t < 2:
                    pe.wait_ge(pool_done, t + 1)
                    pe.wait_ge(q_done, 4)
                else:
                    pe.wait_ge(exp_done, HEADS * (t - 1))
                for h in range(HEADS):
                    half = slice((h % 2) * HD, (h % 2 + 1) * HD)
                    last = T.matmul(ps[:, 4 + 2 * (t % 2) + h % 2, (h // 2) * N_MEM:(h // 2 + 1) * N_MEM],
                                    qT[half, h // 2, t * P:(t + 1) * P], kT[half, h // 2, :], start=True, stop=True)
                last.then_inc(s_ready, 1)

            def attend(t):
                pe.wait_ge(prob_done, t + 1)
                if t:
                    pe.wait_ge(pT_done, 2 * t)
                for h in range(HEADS):
                    for m in range(MT):
                        o = ((h % 2) * MT + m) * P
                        last = T.transpose(bank(h // 2)[:, 0, o:o + P], prob[:, t % 2, h, m * P:(m + 1) * P], ident[:, :])
                last.then_inc(pT_ready, 1)
                pe.wait_ge(pT_done, 2 * (t + 1))
                if t >= 2:
                    pe.wait_ge(o_done, t - 1)
                for h in range(HEADS):
                    for m in range(MT):
                        last = T.matmul(ps[(h % 2) * HD:(h % 2 + 1) * HD, 2 + t % 2, (h // 2) * P:(h // 2 + 1) * P],
                                        v_sb[:, m, h * HD:(h + 1) * HD], probT[:, t % 2, h, m, :],
                                        start=(m == 0), stop=(m == MT - 1))
                last.then_inc(o_ready, 1)

            scores(0)
            for t in range(TT):
                if t + 1 < TT:
                    scores(t + 1)
                attend(t)

            def out_project(t):
                if t == 0:
                    pe.wait_ge(wout_in, 16)
                    pe.wait_ge(rnn_done, RT)
                    pe.wait_ge(pool_done, PT_)
                    pe.wait_ge(o_done, TT)
                elif t >= 2:
                    pe.wait_ge(x2_done, t - 1)
                for k in range(KT):
                    for h in range(2):
                        last = T.matmul(bank(2 * (t % 2) + h)[:, 0, :], mixedT[:, k, t * P:(t + 1) * P],
                                        w_out_sb[:, k, h * HALF:(h + 1) * HALF], start=(k == 0), stop=(k == KT - 1))
                last.then_inc(out_ready, 1)

            def route(t):
                pe.wait_ge(h2_done, t + 1)
                if t:
                    pe.wait_ge(h2T_done, 2 * t)
                else:
                    pe.wait_ge(exp_done, HEADS * TT)
                for k in range(KT):
                    last = T.transpose(bank(4 + k // 4)[:, 0, (k % 4) * P:(k % 4 + 1) * P],
                                       h2[t % 2][:, k * P:(k + 1) * P], ident[:, :])
                last.then_inc(h2T_ready, 1)
                pe.wait_ge(h2T_done, 2 * (t + 1))
                if t:
                    pe.wait_ge(mask_done, t)
                else:
                    pe.wait_ge(router_in, 32)
                for k in range(KT):
                    last = T.matmul(bank(6)[:, 0, 0:E], h2T[t % 2][:, k, :], w_r_sb[:, k, :],
                                    start=(k == 0), stop=(k == KT - 1))
                last.then_inc(logits_ready, 1)

            def rank(t):
                pe.wait_ge(mask_done, t + 1)
                pe.wait_ge(consts, 8)
                if t:
                    pe.wait_ge(slot_done, t)
                T.matmul(bank(7)[:, 0, 0:E], lower[:, :], mask[:, :], start=True, stop=True)
                T.matmul(bank(7)[:, 0, E:2 * E], ones[:, :], mask[:, :], start=True, stop=True).then_inc(rank_ready, 1)

            out_project(0)
            for t in range(TT):
                if t + 1 < TT:
                    out_project(t + 1)
                if t:
                    rank(t - 1)
                route(t)
            rank(TT - 1)
            pe.wait_ge(ucol_done, 1)
            for i in range(4):
                last = T.matmul(bank(6)[0:1, 0, i * P:(i + 1) * P], ucol[:, 6 + i:7 + i], ident[:, :], start=True, stop=True)
            last.then_inc(utab_ready, 1)


def load_half(sp, dram, shared, expert, j):
    at = bass.ds(expert, 1) if not isinstance(expert, int) else slice(expert, expert + 1)
    c, h = j // 2, j % 2
    ks = slice(h * HALFK, (h + 1) * HALFK)
    slot, signal = shared["raw"][:, j % RAW, :, :], shared["raw_in"][j % RAW]
    if c < GU_CH:
        w = dram["w_gu"][0, at].rearrange("a (k p) n -> p (a k) n", p=P)
        q = FF // GU_CH
        for g in range(2):
            lo = g * FF + c * q
            sp.dma_start(slot[:, :, g * q:(g + 1) * q], w[:, ks, lo:lo + q]).then_inc(signal, 16)
    else:
        w = dram["w_down"][0, at].rearrange("a (k p) n -> p (a k) n", p=P)
        lo = (c - GU_CH) * HALF
        for g in range(2):
            part = slice(h * HALFK + g * HALFK // 2, h * HALFK + (g + 1) * HALFK // 2)
            sp.dma_start(slot[:, g * HALFK // 2:(g + 1) * HALFK // 2, :], w[:, part, lo:lo + HALF]).then_inc(signal, 16)


def expert_phase(nc, dram, scratch, shared):
    ctx = ExitStack()
    with ctx:
        def sb(name, shape, dt=F32):
            return ctx.enter_context(nc.sbuf_tensor(name, shape, dt))

        def sem(name):
            return ctx.enter_context(nc.semaphore(name))

        raw, utab, ps, raw_in = shared["raw"], shared["utab"], shared["ps"], shared["raw_in"]
        w_hi = sb("w_hi", [P, SPLIT, HALFK, HALF], F32R)
        w_lo = sb("w_lo", [P, SPLIT, HALFK, HALF], F32R)
        x_rows = sb("x_rows", [P, 2, D])
        xT_hi = sb("xT_hi", [P, KT, UNIT], F32R)
        xT_lo = sb("xT_lo", [P, KT, UNIT], F32R)
        hT_hi = sb("hT_hi", [P, KT, UNIT], F32R)
        hT_lo = sb("hT_lo", [P, KT, UNIT], F32R)
        y = sb("y", [P, 2, D])
        b_gu_row = sb("b_gu_row", [P, 2, FF])
        b_dn_row = sb("b_dn_row", [P, D])
        gu = sb("gu", [P, 2, 2, HALF])
        sg = sb("sg", [P, 2, 2, HALF // 2])
        next_list = sb("next_list", [P, 2, 2], I32)
        this_list = sb("this_list", [P, 2, 2], I32)
        stand_in = sb("stand_in", [1, 2], I32)
        ident = sb("ident2", [P, P])

        hi_done, lo_done, mm_done, acc_free = (sem(n) for n in ("hi_done", "lo_done", "mm_done", "acc_free"))
        gmin_done, sig_done, h_done, pool_step = (sem(n) for n in ("gmin_done", "sig_done2", "h_done", "pool_step2"))
        hT_ready, hT_hi_done, hT_lo_done = (sem(n) for n in ("hT_ready", "hT_hi_done", "hT_lo_done"))
        xT_ready, xT_hi_done, xT_lo_done = (sem(n) for n in ("xT_ready2", "xT_hi_done", "xT_lo_done"))
        y_biased, y_gated = sem("y_biased"), sem("y_gated")
        b_gu_in, b_dn_in, next_in, this_in, x_in, added = (
            sem(n) for n in ("b_gu_in", "b_dn_in", "next_in", "this_in", "x_in", "added"))
        id_done = sem("id_done")
        held = {e: sem(f"held_{e}") for e in ("sp", "pool", "act", "dve", "pe")}
        Q = FF // GU_CH

        block = ctx.enter_context(nc.Block("experts"))

        def unit_value(eng, row, u, top):
            return eng.value_load(utab[0:1, bass.ds(u + row * P, 1)], min_val=0, max_val=top)

        def n_units(eng):
            return eng.value_load(utab[0:1, 3 * P:3 * P + 1], min_val=1, max_val=E + TOPK * SEQ // UNIT)

        @block.sync
        def _(sp):
            n = n_units(sp)

            with sp.Fori(0, n) as u:
                expert = unit_value(sp, 0, u, E - 1)
                after = unit_value(sp, 0, u + 1, E - 1)
                for j in range(RAW, RAW + 2 * CH):
                    hold(sp, lo_done, 2 * CH * u + j - RAW + 1, held["sp"])
                    if j < 2 * CH:
                        load_half(sp, dram, shared, expert, j)
                    else:
                        with sp.If(u + 1 < n):
                            load_half(sp, dram, shared, after, j - 2 * CH)

        @block.gpsimd
        def _(pool):
            G = nc.gpsimd
            n = n_units(pool)
            pool.memset(ident[:, :], 0.0).then_inc(pool_step, 1)
            pool.wait_ge(pool_step, 1)
            pool.affine_select(out=ident[:, :], in_=ident[:, :], compare_op=ALU.not_equal, fill=1.0,
                               base=0, pattern=[[-1, P]], channel_multiplier=1).then_inc(id_done, 1)

            def load_list(dst, row0, signal):
                pool.dma_start(dst[:, :, :], scratch["table"][bass.ds(row0, UNIT), :]
                               .rearrange("(b p) w -> p b w", p=P)).then_inc(signal, 16)

            def gate_up_bias(expert):
                pool.dma_start(b_gu_row[:, :, :].rearrange("p g f -> p (g f)"),
                               dram["b_gu"][0, bass.ds(expert, 1)].broadcast_to([P, 2 * FF])).then_inc(b_gu_in, 16)

            def gather():
                for b in range(2):
                    pool.indirect_dma_start(
                        out=x_rows[:, b, :], out_offset=None, in_=scratch["h2"],
                        in_offset=bass.IndirectOffsetOnAxis(ap=next_list[:, b, 0:1], axis=0)).then_inc(x_in, 16)

            for i in range(2):
                pool.dma_start(stand_in[:, :], scratch["table"][0:1, :]).then_inc(added, 16)
                pool.wait_ge(added, 16 * (i + 1))
            load_list(next_list, unit_value(pool, 1, 0, E * CAP - UNIT), next_in)
            pool.wait_ge(next_in, 16)
            gather()
            gate_up_bias(unit_value(pool, 0, 0, E - 1))
            with pool.Fori(0, n) as u:
                expert = unit_value(pool, 0, u, E - 1)
                expert_next = unit_value(pool, 0, u + 1, E - 1)
                row0 = unit_value(pool, 1, u, E * CAP - UNIT)
                row0_next = unit_value(pool, 1, u + 1, E * CAP - UNIT)
                two = unit_value(pool, 2, u, 1)
                hold(pool, added, 32 * u + 32, held["pool"])
                load_list(this_list, row0, this_in)
                hold(pool, x_in, 32 * (u + 1), held["pool"])
                load_list(next_list, row0_next, next_in)
                pool.dma_start(b_dn_row[:, :], dram["b_down"][0, bass.ds(expert, 1)].broadcast_to([P, D]))\
                    .then_inc(b_dn_in, 16)
                for c in range(GU_CH):
                    par = c % 2
                    hold(pool, sig_done, 2 * (GU_CH * u + c + 1), held["pool"])

                    def swiglu(nb, c=c, par=par):
                        gate, up = gu[:, par, 0:nb, 0:Q], gu[:, par, 0:nb, Q:2 * Q]
                        G.tensor_tensor(gate, gate, sg[:, par, 0:nb, :], ALU.mult).then_inc(pool_step, 1)
                        pool.wait_ge(pool_step, GU_CH * u + c + 2)
                        G.tensor_tensor(up, up, gate, ALU.mult).then_inc(h_done, 1)

                    with pool.If(two > 0):
                        swiglu(2)
                    with pool.Else():
                        swiglu(1)
                    if c == 0:
                        hold(pool, next_in, 16 * (u + 2), held["pool"])
                        hold(pool, xT_ready, KT // 2 * (u + 1), held["pool"])
                        gather()
                gate_up_bias(expert_next)
                hold(pool, y_gated, DN_CH * (u + 1), held["pool"])
                with pool.If(two > 0):
                    pool.indirect_dma_start(
                        out=scratch["acc"], out_offset=bass.IndirectOffsetOnAxis(ap=this_list[:, 1, 0:1], axis=0),
                        in_=y[:, 1, :], in_offset=None, compute_op=ALU.add).then_inc(added, 16)
                with pool.Else():
                    pool.dma_start(stand_in[:, :], scratch["table"][0:1, :]).then_inc(added, 16)
                pool.indirect_dma_start(
                    out=scratch["acc"], out_offset=bass.IndirectOffsetOnAxis(ap=this_list[:, 0, 0:1], axis=0),
                    in_=y[:, 0, :], in_offset=None, compute_op=ALU.add).then_inc(added, 16)
            hold(pool, added, 32 * n + 32, held["pool"])
            hold(pool, x_in, 32 * (n + 1), held["pool"])
            hold(pool, next_in, 16 * (n + 1), held["pool"])
            hold(pool, b_gu_in, 16 * (n + 1), held["pool"])

        @block.scalar
        def _(act):
            n = n_units(act)

            def split_hi(j):
                nc.scalar.activation(w_hi[:, j % SPLIT, :, :], raw[:, j % RAW, :, :], ACT.Copy).then_inc(hi_done, 1)

            def x_hi(nb):
                def emit(g):
                    nc.scalar.activation(xT_hi[:, 2 * g:2 * g + 2, 0:nb * P],
                                         ps[:, 6 + g % 2, :].rearrange("p (k t) -> p k t", k=2)[:, :, 0:nb * P],
                                         ACT.Copy).then_inc(xT_hi_done, 1)
                return emit

            def next_x(base, two):
                with act.If(two > 0):
                    for g in range(KT // 2):
                        act.wait_ge(xT_ready, base + g + 1)
                        x_hi(2)(g)
                with act.Else():
                    for g in range(KT // 2):
                        act.wait_ge(xT_ready, base + g + 1)
                        x_hi(1)(g)

            act.preload_act_table(ACT.Sigmoid)
            next_x(0, unit_value(act, 2, 0, 1))
            for j in range(SPLIT):
                act.wait_ge(raw_in[j % RAW], 32 * (j // RAW + 1))
                split_hi(j)
            with act.Fori(0, n) as u:
                two = unit_value(act, 2, u, 1)
                two_next = unit_value(act, 2, u + 1, 1)

                def sigmoid(c):
                    hold(act, gmin_done, 2 * (GU_CH * u + c) + 1, held["act"])

                    def for_nb(nb):
                        up = gu[:, c % 2, 0:nb, Q:2 * Q]
                        nc.scalar.activation(sg[:, c % 2, 0:nb, :], gu[:, c % 2, 0:nb, 0:Q], ACT.Sigmoid,
                                             scale=SWIGLU_ALPHA).then_inc(sig_done, 1)
                        act.wait_ge(gmin_done, 2 * (GU_CH * u + c) + 2)
                        nc.scalar.activation(up, up, ACT.Copy, bias=1.0).then_inc(sig_done, 1)
                    with act.If(two > 0):
                        for_nb(2)
                    with act.Else():
                        for_nb(1)

                def h_hi(c):
                    hold(act, hT_ready, GU_CH * u + c + 1, held["act"])
                    for_nb = lambda nb: nc.scalar.activation(
                        hT_hi[:, 2 * c:2 * c + 2, 0:nb * P],
                        ps[:, 4 + c % 2, :].rearrange("p (k t) -> p k t", k=2)[:, :, 0:nb * P],
                        ACT.Copy).then_inc(hT_hi_done, 1)
                    with act.If(two > 0):
                        for_nb(2)
                    with act.Else():
                        for_nb(1)

                def gate_y(c):
                    i = c - GU_CH
                    hold(act, y_biased, DN_CH * u + i + 1, held["act"])
                    cols = slice(i * HALF, (i + 1) * HALF)
                    gates = this_list[:, :, 1].bitcast(F32)
                    hold(act, this_in, 16 * (u + 1), held["act"])
                    with act.If(two > 0):
                        nc.scalar.activation(y[:, 1, cols], y[:, 1, cols], ACT.Copy, scale=gates[:, 1:2])
                        nc.scalar.activation(y[:, 0, cols], y[:, 0, cols], ACT.Copy, scale=gates[:, 0:1]).then_inc(y_gated, 1)
                    with act.Else():
                        nc.scalar.activation(y[:, 0, cols], y[:, 0, cols], ACT.Copy, scale=gates[:, 0:1]).then_inc(y_gated, 1)

                def splits(c, hs):
                    for h in hs:
                        j = 2 * (c + AHEAD) + h
                        act.wait_ge(raw_in[j % RAW], 32 * 2 * CH // RAW * u + 32 * (j // RAW + 1))
                        split_hi(j)

                for c in range(CH):
                    hold(act, mm_done, CH * u + c + 1, held["act"])
                    if c < AHEAD:
                        splits(c, (0,))
                        sigmoid(c)
                        if c:
                            h_hi(c - 1)
                        splits(c, (1,))
                    else:
                        if c < GU_CH:
                            sigmoid(c)
                            h_hi(c - 1)
                        with act.If(u + 1 < n):
                            splits(c, (0, 1))
                        if c == GU_CH - 1:
                            next_x(KT // 2 * (u + 1), two_next)
                            h_hi(c)
                        if c >= GU_CH:
                            gate_y(c)

        @block.vector
        def _(dve):
            V = nc.vector
            n = n_units(dve)
            dve.sem_inc(acc_free, 1)
            dve.sem_inc(hT_lo_done, 1)

            def split_lo(j, before):
                dve.wait_ge(hi_done, before + j + 1)
                V.tensor_tensor(w_lo[:, j % SPLIT, :, :], raw[:, j % RAW, :, :], w_hi[:, j % SPLIT, :, :].bitcast(F32),
                                ALU.subtract).then_inc(lo_done, 1)

            def next_x(base, two):
                def emit(g, nb):
                    dve.wait_ge(xT_hi_done, base + g + 1)
                    V.tensor_tensor(xT_lo[:, 2 * g:2 * g + 2, 0:nb * P],
                                    ps[:, 6 + g % 2, :].rearrange("p (k t) -> p k t", k=2)[:, :, 0:nb * P],
                                    xT_hi[:, 2 * g:2 * g + 2, 0:nb * P].bitcast(F32), ALU.subtract).then_inc(xT_lo_done, 1)
                with dve.If(two > 0):
                    for g in range(KT // 2):
                        emit(g, 2)
                with dve.Else():
                    for g in range(KT // 2):
                        emit(g, 1)

            next_x(0, unit_value(dve, 2, 0, 1))
            for j in range(SPLIT):
                split_lo(j, 0)
            with dve.Fori(0, n) as u:
                two = unit_value(dve, 2, u, 1)
                two_next = unit_value(dve, 2, u + 1, 1)

                def evacuate(c):
                    hold(dve, mm_done, CH * u + c + 1, held["dve"])
                    if c < GU_CH:
                        if c == 0:
                            hold(dve, b_gu_in, 16 * (u + 1), held["dve"])
                        if c >= 2:
                            hold(dve, hT_ready, GU_CH * u + c - 1, held["dve"])
                        bias = b_gu_row[:, :, c * Q:(c + 1) * Q]
                        dst = lambda nb: gu[:, c % 2, 0:nb, :]
                    else:
                        if c == GU_CH:
                            hold(dve, b_dn_in, 16 * (u + 1), held["dve"])
                            hold(dve, added, 32 * u + 32, held["dve"])
                        i = c - GU_CH
                        bias = b_dn_row[:, i * HALF:(i + 1) * HALF].rearrange("p (g q) -> p g q", g=2)
                        dst = lambda nb: y[:, 0:nb, i * HALF:(i + 1) * HALF]

                    def emit(nb):
                        ins = V.tensor_tensor(dst(nb).rearrange("p b (g q) -> p b g q", g=2),
                                              ps[:, 2 * (c % 2):2 * (c % 2) + nb, :].rearrange("p b (g q) -> p b g q", g=2),
                                              bias.unsqueeze(1).broadcast_to([P, nb, 2, HALF // 2]), ALU.add)
                        ins.then_inc(acc_free, 1)
                        if c >= GU_CH:
                            V.engine_nop().then_inc(y_biased, 1)
                        if c < GU_CH:
                            gate, up = gu[:, c % 2, 0:nb, 0:Q], gu[:, c % 2, 0:nb, Q:2 * Q]
                            dve.wait_ge(acc_free, CH * u + c + 2)
                            V.tensor_scalar(gate, gate, SWIGLU_LIMIT, None, ALU.min).then_inc(gmin_done, 1)
                            V.tensor_scalar(up, up, -SWIGLU_LIMIT, SWIGLU_LIMIT, ALU.max, ALU.min).then_inc(gmin_done, 1)
                    with dve.If(two > 0):
                        emit(2)
                    with dve.Else():
                        emit(1)

                def h_lo(c):
                    hold(dve, hT_hi_done, GU_CH * u + c + 1, held["dve"])
                    for_nb = lambda nb: V.tensor_tensor(
                        hT_lo[:, 2 * c:2 * c + 2, 0:nb * P],
                        ps[:, 4 + c % 2, :].rearrange("p (k t) -> p k t", k=2)[:, :, 0:nb * P],
                        hT_hi[:, 2 * c:2 * c + 2, 0:nb * P].bitcast(F32), ALU.subtract).then_inc(hT_lo_done, 1)
                    with dve.If(two > 0):
                        for_nb(2)
                    with dve.Else():
                        for_nb(1)

                for c in range(CH):
                    j = 2 * (c + AHEAD)
                    evacuate(c)
                    if c < AHEAD:
                        split_lo(j, 2 * CH * u)
                        if c:
                            h_lo(c - 1)
                        split_lo(j + 1, 2 * CH * u)
                    else:
                        if c < GU_CH:
                            h_lo(c - 1)
                        with dve.If(u + 1 < n):
                            split_lo(j, 2 * CH * u)
                            split_lo(j + 1, 2 * CH * u)
                        if c == GU_CH - 1:
                            next_x(KT // 2 * (u + 1), two_next)
                            h_lo(c)

        @block.tensor
        def _(pe):
            T = nc.tensor
            n = n_units(pe)

            def transpose_x(base, two, after_unit, groups=range(KT // 2)):
                for g in groups:
                    if g >= 2 or after_unit:
                        pe.wait_ge(xT_lo_done, base + g - 1)
                    def block_of(b, g=g):
                        for j in range(2):
                            last = T.transpose(ps[:, 6 + g % 2, (2 * j + b) * P:(2 * j + b + 1) * P],
                                               x_rows[:, b, (2 * g + j) * P:(2 * g + j + 1) * P], ident[:, :])
                        return last
                    with pe.If(two > 0):
                        block_of(1)
                    block_of(0).then_inc(xT_ready, 1)

            pe.wait_ge(id_done, 1)
            pe.wait_ge(x_in, 32)
            transpose_x(0, unit_value(pe, 2, 0, 1), False)
            with pe.Fori(0, n) as u:
                two = unit_value(pe, 2, u, 1)
                two_next = unit_value(pe, 2, u + 1, 1)

                def three_pass(c, b, k, first, last_k):
                    hi, lo = (xT_hi, xT_lo) if c < GU_CH else (hT_hi, hT_lo)
                    rows_b = slice(b * P, (b + 1) * P)
                    out = ps[:, 2 * (c % 2) + b, :]
                    T.matmul(out, hi[:, k, rows_b], w_hi[:, (2 * c + k // HALFK) % SPLIT, k % HALFK, :], start=first, stop=False)
                    T.matmul(out, hi[:, k, rows_b], w_lo[:, (2 * c + k // HALFK) % SPLIT, k % HALFK, :], start=False, stop=False)
                    return T.matmul(out, lo[:, k, rows_b], w_hi[:, (2 * c + k // HALFK) % SPLIT, k % HALFK, :], start=False, stop=last_k)

                def part(c, b, ks):
                    for k in ks:
                        last = three_pass(c, b, k, k == 0, k == KT - 1)
                    return last

                def chunk(c, ks, base_lo):
                    for h in range(2):
                        half = [k for k in ks if k // HALFK == h]
                        if half:
                            pe.wait_ge(lo_done, base_lo + 2 * c + h + 1)
                    with pe.If(two > 0):
                        part(c, 1, ks)
                    return part(c, 0, ks)

                def transpose_h(c):
                    hold(pe, h_done, GU_CH * u + c + 1, held["pe"])
                    if c >= 2:
                        pe.wait_ge(hT_lo_done, GU_CH * u + c - 1 + 1)
                    else:
                        pe.wait_ge(hT_lo_done, GU_CH * u + 1)

                    def block_of(b):
                        for j in range(2):
                            last = T.transpose(ps[:, 4 + c % 2, (2 * j + b) * P:(2 * j + b + 1) * P],
                                               gu[:, c % 2, b, Q + j * P:Q + (j + 1) * P], ident[:, :])
                        return last
                    with pe.If(two > 0):
                        block_of(1)
                    block_of(0).then_inc(hT_ready, 1)

                base_lo = 2 * CH * u
                pe.wait_ge(xT_lo_done, KT // 2 * (u + 1))
                for c in range(GU_CH):
                    if c < 2:
                        pe.wait_ge(acc_free, CH * u + 1)
                    else:
                        pe.wait_ge(acc_free, CH * u + c - 1 + 1)
                    chunk(c, range(KT), base_lo).then_inc(mm_done, 1)
                    if c:
                        transpose_h(c - 1)
                pe.wait_ge(acc_free, CH * u + GU_CH - 1 + 1)
                pe.wait_ge(hT_lo_done, GU_CH * u + GU_CH - 1 + 1)
                chunk(GU_CH, range(3), base_lo)
                pe.wait_ge(x_in, 32 * (u + 2))
                transpose_x(KT // 2 * (u + 1), two_next, True, (0, 1))
                chunk(GU_CH, range(3, KT - 2), base_lo)
                transpose_x(KT // 2 * (u + 1), two_next, True, (2, 3))
                transpose_h(GU_CH - 1)
                pe.wait_ge(hT_lo_done, GU_CH * (u + 1) + 1)
                chunk(GU_CH, range(KT - 2, KT), base_lo).then_inc(mm_done, 1)
                pe.wait_ge(acc_free, CH * u + GU_CH + 1)
                chunk(GU_CH + 1, range(KT), base_lo).then_inc(mm_done, 1)


def final_phase(nc, dram, scratch, out):
    ctx = ExitStack()
    with ctx:
        def sb(name, shape, dt=F32):
            return ctx.enter_context(nc.sbuf_tensor(name, shape, dt))

        def sem(name):
            return ctx.enter_context(nc.semaphore(name))

        acc = sb("acc_sb", [P, TT, D])
        square = sb("square", [P, D])
        gain = sb("gain", [P, D])
        stat = sb("stat", [P, 4, TT])
        acc_in = [sem(f"acc_in{t}") for t in range(TT)]
        gain_in, ssq, msq, root, inv, normed, out_done = (
            sem(n) for n in ("gain_in", "ssq", "msq", "root", "inv", "normed", "out_done"))
        block = ctx.enter_context(nc.Block("final"))

        @block.sync
        def _(sp):
            for t in range(TT):
                sp.dma_start(acc[:, t, :], scratch["acc"][t * P:(t + 1) * P, :]).then_inc(acc_in[t], 16)
            for t in range(TT):
                sp.wait_ge(normed, t + 1)
                sp.dma_start(out[0, t * P:(t + 1) * P, :], acc[:, t, :]).then_inc(out_done, 16)
            sp.wait_ge(out_done, 16 * TT)

        @block.scalar
        def _(act):
            act.dma_start(gain[:, :], dram["final_norm_g"].unsqueeze(0).broadcast_to([P, D])).then_inc(gain_in, 16)
            for t in range(TT):
                act.wait_ge(acc_in[t], 16)
                if t:
                    act.wait_ge(ssq, t)
                nc.scalar.activation(square[:, :], acc[:, t, :], ACT.Square, accum_out=stat[:, 0, t:t + 1]).then_inc(ssq, 1)
                act.wait_ge(msq, t + 1)
                nc.scalar.activation(stat[:, 2, t:t + 1], stat[:, 1, t:t + 1], ACT.Sqrt).then_inc(root, 1)

        @block.vector
        def _(dve):
            V = nc.vector
            for t in range(TT):
                dve.wait_ge(ssq, t + 1)
                V.tensor_scalar(stat[:, 1, t:t + 1], stat[:, 0, t:t + 1], 1.0 / D, EPS, ALU.mult, ALU.add).then_inc(msq, 1)
                dve.wait_ge(root, t + 1)
                V.reciprocal(stat[:, 3, t:t + 1], stat[:, 2, t:t + 1]).then_inc(inv, 1)
                dve.wait_ge(inv, t + 1)
                if t == 0:
                    dve.wait_ge(gain_in, 16)
                V.scalar_tensor_tensor(acc[:, t, :], acc[:, t, :], stat[:, 3, t:t + 1], gain[:, :], ALU.mult, ALU.mult)\
                    .then_inc(normed, 1)


def hymba_moe_kernel(nc, dram, out):
    scratch = {
        "h2": nc.dram_tensor("h2_rows", (ROWS, D), F32, kind="Internal").ap(),
        "acc": nc.dram_tensor("acc_rows", (ROWS, D), F32, kind="Internal").ap(),
        "table": nc.dram_tensor("token_lists", (E * CAP, 2), I32, kind="Internal").ap(),
    }
    with ExitStack() as ctx:
        shared = {
            "raw": ctx.enter_context(nc.sbuf_tensor("raw_weights", [P, RAW, HALFK, HALF], F32)),
            "utab": ctx.enter_context(nc.sbuf_tensor("unit_table", [1, 4 * P], I32)),
            "ps": ctx.enter_context(nc.psum_tensor("ps", [P, 8, HALF], F32)),
            "raw_in": [ctx.enter_context(nc.semaphore(f"raw_in{i}")) for i in range(RAW)],
        }
        mixer_phase(nc, dram, scratch, shared)
        expert_phase(nc, dram, scratch, shared)
        final_phase(nc, dram, scratch, out)


_INS = ["x", "mem", "norm_mix_g", "w_in", "conv_w", "conv_b", "w_rg_a", "b_rg_a", "w_rg_i", "b_rg_i",
        "lru_lambda", "w_pool", "pool_scale", "mem_norm_g", "w_mem_kv", "w_out", "norm_ffn_g",
        "w_router", "b_router", "w_gu", "b_gu", "w_down", "b_down", "final_norm_g"]


def kernel(**inputs):
    import numpy as _np
    import concourse.bacc as _bacc
    from concourse import mybir as _mybir
    from concourse.bass_utils import run_bass_kernel_spmd as _run

    nc = _bacc.Bacc("TRN2", target_bir_lowering=False, num_devices=1)
    arrays, dram = {}, {}
    for name in _INS:
        a = _np.ascontiguousarray(inputs[name])
        arrays[f"in_{name}"] = a
        dram[name] = nc.dram_tensor(f"in_{name}", a.shape, _mybir.dt.from_np(a.dtype), kind="ExternalInput").ap()
    out = nc.dram_tensor("out_rows", (1, SEQ, D), _mybir.dt.float32, kind="ExternalOutput").ap()
    hymba_moe_kernel(nc, dram, out)
    r = _run(nc, [arrays], core_ids=[0])
    return r.results[0]["out_rows"]
```

```python
import concourse.bass as bass
import numpy as np
from concourse import mybir
from contextlib import ExitStack

F32 = mybir.dt.float32
F32R = mybir.dt.float32r
I32 = mybir.dt.int32
U32 = mybir.dt.uint32
ALU = mybir.AluOpType
ACT = mybir.ActivationFunctionType
AX = mybir.AxisListType

P = 128
SEQ, D = 1024, 1024
TT, KT = SEQ // P, D // P
HALF = 512
N_MEM = 256
MT = N_MEM // P
D_RNN, D_POOL, D_XATTN = 512, 256, 256
D_IN = 2 * D_RNN + D_POOL + D_XATTN
RT, PT_ = D_RNN // P, D_POOL // P
CONV = 4
POOL_WINDOWS = (2, 4, 8, 16)
PAD = max(POOL_WINDOWS)
HEADS, HD = 4, 64
E, TOPK = 32, 4
FF = D
EPS = 1e-6
LRU_C = 8.0
SWIGLU_ALPHA, SWIGLU_LIMIT = 1.702, 7.0

UNIT = 256
TAIL = P // 2
CAP = SEQ
UNITS_PER_E = CAP // UNIT
DUMP = P
ROWS = SEQ + DUMP
GU_CH, DN_CH = 4, 2
CH = GU_CH + DN_CH
HALFK = KT // 2
RAW = 4
SPLIT = 6
AHEAD = SPLIT // 2

V_CONVW, V_CONVB, V_BA, V_BI, V_LAM, V_PS, V_GMIX, V_GMEM, V_N = 0, 16, 20, 24, 28, 32, 34, 42, 50


def hold(eng, sem, value, held):
    eng.wait_ge(sem, value)
    eng.sem_inc(held, 1)


def ring_value(item, slots):
    return 16 * (item // slots + 1)


def mixer_phase(nc, dram, scratch, shared):
    ctx = ExitStack()
    with ctx:
        def sb(name, shape, dt=F32):
            return ctx.enter_context(nc.sbuf_tensor(name, shape, dt))

        def sem(name):
            return ctx.enter_context(nc.semaphore(name))

        raw, utab, ps = shared["raw"], shared["utab"], shared["ps"]

        def bank(i, n=1):
            return ps[:, i:i + n, :]

        rows = sb("rows", [P, 3, D])
        region_a = sb("region_a", [P, KT * SEQ])
        xnT = region_a[:, :].rearrange("p (k t) -> p k t", k=KT)
        w_out_sb = region_a[:, :].rearrange("p (k n) -> p k n", k=KT)
        mixedT = sb("mixedT", [P, KT, SEQ])
        w_in_sb = sb("w_in_sb", [P, 3, KT, P])
        region_c = sb("region_c", [P, 3 * (PAD + SEQ) + 4 * SEQ])

        def c_tile(i):
            if i < 3:
                return region_c[:, i * (PAD + SEQ):(i + 1) * (PAD + SEQ)]
            o = 3 * (PAD + SEQ) + (i - 3) * SEQ
            return region_c[:, o:o + SEQ]

        u_pad, r_pad, i_pad = c_tile(0), c_tile(1), c_tile(2)
        uc, a_t, m_t, g_t = c_tile(3), c_tile(4), c_tile(5), c_tile(6)
        x2 = [c_tile(0)[:, 0:D], c_tile(1)[:, 0:D]]
        h2 = [c_tile(2)[:, 0:D], c_tile(3)]
        h2T = [c_tile(4).rearrange("p (k t) -> p k t", k=KT), c_tile(5).rearrange("p (k t) -> p k t", k=KT)]
        g2_row = c_tile(6)
        region_d = sb("region_d", [P, KT * 2 * D_XATTN + KT * N_MEM])
        w_kv_sb = region_d[:, 0:KT * 2 * D_XATTN].rearrange("p (k n) -> p k n", k=KT)
        memnT = region_d[:, KT * 2 * D_XATTN:].rearrange("p (k m) -> p k m", k=KT)
        prob = region_d[:, 0:2 * D].rearrange("p (b h m) -> p b h m", b=2, h=HEADS)
        probT = region_d[:, 2 * D:4 * D].rearrange("p (b h c t) -> p b h c t", b=2, h=HEADS, c=MT)
        qT = region_d[:, 4 * D:4 * D + 2 * SEQ].rearrange("p (c t) -> p c t", c=2)
        kT = sb("kT", [P, 2, N_MEM])
        v_sb = sb("v_sb", [P, MT, D_XATTN])
        ident = sb("ident", [P, P])
        lower = sb("lower", [P, P])
        ones = sb("ones", [P, P])
        blockdiag = sb("blockdiag", [P, 10, P])
        vrows = sb("vrows", [64, P])
        vec = sb("vec", [P, V_N])
        small = sb("small", [P, 64])
        lam = sb("lam", [P, 8, RT])
        inv_w = sb("inv_w", [P, PT_, PAD])
        iota_e = sb("iota_e", [P, E])
        iota_p = sb("iota_p", [P, 1])
        tokid = sb("tokid", [P, TT], I32)
        empty = a_t[:, 0:2 * UNIT].bitcast(I32).rearrange("p (s w) -> p s w", w=2)
        w_r_sb = sb("w_r_sb", [P, KT, E])
        b_r_row = sb("b_r_row", [P, E])
        logits = sb("logits", [P, E])
        top8 = sb("top8", [P, 8])
        idx8 = sb("idx8", [P, 8], U32)
        idxf = sb("idxf", [P, TOPK])
        onehot = sb("onehot", [P, TOPK, E])
        picked = sb("picked", [P, TOPK, E])
        mask = sb("mask", [P, E])
        run = sb("run", [P, E])
        slotm = sb("slotm", [P, E])
        slotf = sb("slotf", [P, TOPK])
        sloti = sb("sloti", [P, TT, TOPK], I32)
        entry = sb("entry", [P, TT, TOPK, 2], I32)
        gexp = sb("gexp", [P, TOPK])
        cnt = sb("cnt", [P, 8, E])
        ucol = sb("ucol", [P, 12])
        mx = sb("mx", [P, 4, HEADS])

        ss, ms, sd, rs = (small[:, i * 10:(i + 1) * 10] for i in range(4))
        ss2, ms2, sd2, rs2 = (small[:, 40 + i * 2:42 + i * 2] for i in range(4))

        rows_in = [sem(f"rows_in{i}") for i in range(3)]
        w_in_in = [sem(f"w_in_in{i}") for i in range(3)]
        vrows_in, bd_in, kv_in, wout_in, router_in = (sem(n) for n in ("vrows_in", "bd_in", "kv_in", "wout_in", "router_in"))
        gain_in = sem("gain_in_ffn")
        consts, bd_zero, zero_set, zero_out, table_set = (sem(n) for n in ("consts", "bd_zero", "zero_set", "zero_out", "table_set"))
        vecT_ready, vec_done, lam_abs, lam_exp, lam_done, inv_done = (sem(n) for n in ("vecT_ready", "vec_done", "lam_abs", "lam_exp", "lam_done", "inv_done"))
        ss_done, ms_done, sd_done, xn_done, xT_ready, xT_done = (sem(n) for n in ("ss_done", "ms_done", "sd_done", "xn_done", "xT_ready", "xT_done"))
        proj_ready, proj_free, kv_ready, kv_done = (sem(n) for n in ("proj_ready", "proj_free", "kv_ready", "kv_done"))
        u_done, pu_done, conv_done, gates_ready, sig_done, tanh_done, neg_done, mult_done, gelu_done, rnn_done = (
            sem(n) for n in ("u_done", "pu_done", "conv_done", "gates_ready", "sig_done", "tanh_done", "neg_done", "mult_done", "gelu_done", "rnn_done"))
        pads_zero, d_done, pool_ready, pool_done, q_done = (sem(n) for n in ("pads_zero", "d_done", "pool_ready", "pool_done", "q_done"))
        s_ready, nmax_done, exp_done, prob_done, pT_ready, pT_done, o_ready, o_done = (
            sem(n) for n in ("s_ready", "nmax_done", "exp_done", "prob_done", "pT_ready", "pT_done", "o_ready", "o_done"))
        out_ready, x2_done, ss2_done, ms2_done, sd2_done, h2_done, h2T_ready, h2T_done = (
            sem(n) for n in ("out_ready", "x2_done", "ss2_done", "ms2_done", "sd2_done", "h2_done", "h2T_ready", "h2T_done"))
        stored = [sem("stored0"), sem("stored1")]
        logits_ready, logits_done, top_done, gexp_done, mask_done, rank_ready, slot_done, scattered = (
            sem(n) for n in ("logits_ready", "logits_done", "top_done", "gexp_done", "mask_done", "rank_ready", "slot_done", "scattered"))
        ucol_done, utab_ready = sem("ucol_done"), sem("utab_ready")
        dve_step, pool_step = sem("dve_step"), sem("pool_step")

        NORMED = TT + MT
        NPROJ = D_IN // P
        PROJ = [c for r in range(RT) for c in (r, RT + r)] + list(range(2 * RT, NPROJ))

        block = ctx.enter_context(nc.Block("mixer"))

        @block.sync
        def _(sp):
            def load_rows(item):
                if item < TT or item >= NORMED:
                    t = item if item < TT else item - NORMED
                    src = dram["x"][0, t * P:(t + 1) * P, :]
                else:
                    src = dram["mem"][0, (item - TT) * P:(item - TT + 1) * P, :]
                sp.dma_start(rows[:, item % 3, :], src).then_inc(rows_in[item % 3], 16)

            def load_w_in(n):
                c = PROJ[n]
                sp.dma_start(w_in_sb[:, n % 3, :, :],
                             dram["w_in"][0].rearrange("(k p) n -> p k n", p=P)[:, :, c * P:(c + 1) * P])\
                    .then_inc(w_in_in[n % 3], 16)

            for item in range(3):
                load_rows(item)
            load_w_in(0)
            for item in range(3, NORMED):
                sp.wait_ge(xT_ready, item - 2)
                load_rows(item)
                if item == 4:
                    load_w_in(1)
                if item == 6:
                    load_w_in(2)
            sp.dma_start(w_kv_sb, dram["w_mem_kv"][0].rearrange("(k p) n -> p k n", p=P)).then_inc(kv_in, 16)
            for n in range(3, NPROJ):
                sp.wait_ge(proj_ready, 2 * (n - 2))
                load_w_in(n)
                if n == 3:
                    for item in range(NORMED, NORMED + 3):
                        sp.wait_ge(xT_ready, item - 2)
                        load_rows(item)
                if n >= 4 and n < 4 + RAW:
                    load_half(sp, dram, shared, 0, n - 4)
            sp.wait_ge(proj_ready, 2 * NPROJ)
            sp.dma_start(w_out_sb, dram["w_out"][0].rearrange("(k p) n -> p k n", p=P)).then_inc(wout_in, 16)
            sp.wait_ge(rnn_done, RT)
            sp.dma_start(g2_row, dram["norm_ffn_g"][0:1, :].broadcast_to([P, D])).then_inc(gain_in, 16)
            for t in range(TT):
                sp.wait_ge(h2_done, t + 1)
                sp.dma_start(scratch["acc"][t * P:(t + 1) * P, :], x2[t % 2]).then_inc(stored[t % 2], 16)
                sp.dma_start(scratch["h2"][t * P:(t + 1) * P, :], h2[t % 2]).then_inc(stored[t % 2], 16)
                if t + 3 < TT:
                    sp.wait_ge(x2_done, t + 1)
                    load_rows(NORMED + t + 3)
            for i in range(2):
                sp.wait_ge(stored[i], 32 * (TT // 2))
            sp.wait_ge(zero_out, 32)
            sp.wait_ge(scattered, 16 * TT * TOPK)

        @block.gpsimd
        def _(pool):
            pool.memset(ident[:, :], 0.0).then_inc(pool_step, 1)
            pool.memset(ones[:, :], 1.0).then_inc(pool_step, 1)
            pool.memset(vrows[:, :], 0.0).then_inc(pool_step, 1)
            pool.wait_ge(pool_step, 3)
            vector_rows = [
                (V_CONVW, CONV * RT, dram["conv_w"][0].rearrange("w (c p) -> (w c) p", p=P)),
                (V_CONVB, RT, dram["conv_b"][0].rearrange("(c p) -> c p", p=P)),
                (V_BA, RT, dram["b_rg_a"][0].rearrange("(c p) -> c p", p=P)),
                (V_BI, RT, dram["b_rg_i"][0].rearrange("(c p) -> c p", p=P)),
                (V_LAM, RT, dram["lru_lambda"][0].rearrange("(c p) -> c p", p=P)),
                (V_PS, PT_, dram["pool_scale"][0].rearrange("(c p) -> c p", p=P)),
                (V_GMIX, KT, dram["norm_mix_g"][0].rearrange("(c p) -> c p", p=P)),
                (V_GMEM, KT, dram["mem_norm_g"][0].rearrange("(c p) -> c p", p=P)),
            ]
            for r, n, src in vector_rows:
                pool.dma_start(vrows[r:r + n, :], src).then_inc(vrows_in, 16)
            pool.affine_select(out=ident[:, :], in_=ident[:, :], compare_op=ALU.not_equal, fill=1.0,
                               base=0, pattern=[[-1, P]], channel_multiplier=1).then_inc(consts, 1)
            pool.affine_select(out=lower[:, :], in_=ones[:, :], compare_op=ALU.is_gt, fill=0.0,
                               base=0, pattern=[[1, P]], channel_multiplier=-1).then_inc(consts, 1)
            pool.iota(iota_e[:, :], [[1, E]], base=0, channel_multiplier=0,
                      allow_small_or_imprecise_dtypes=True).then_inc(consts, 1)
            pool.iota(iota_p[:, :], [[0, 1]], base=0, channel_multiplier=1,
                      allow_small_or_imprecise_dtypes=True).then_inc(consts, 1)
            pool.iota(tokid[:, :], [[P, TT]], base=0, channel_multiplier=1).then_inc(consts, 1)
            for j in range(PT_):
                pool.iota(inv_w[:, j, :], [[1, PAD]], base=1, channel_multiplier=0,
                          allow_small_or_imprecise_dtypes=True).then_inc(consts, 1)
            pool.iota(run[:, :], [[CAP, E]], base=0, channel_multiplier=0,
                      allow_small_or_imprecise_dtypes=True).then_inc(consts, 1)
            pool.memset(blockdiag[:, :, :], 0.0).then_inc(bd_zero, 1)
            pool.wait_ge(bd_zero, 1)
            maps = [(0, RT, dram["w_rg_a"][0]), (RT, RT, dram["w_rg_i"][0]), (2 * RT, PT_, dram["w_pool"][0])]
            for first, n, w in maps:
                pairs = w.rearrange("(c two) i j -> two i c j", two=2)
                pool.dma_start(blockdiag[0:HD, first:first + n, 0:HD], pairs[0]).then_inc(bd_in, 16)
                pool.dma_start(blockdiag[HD:P, first:first + n, HD:P], pairs[1]).then_inc(bd_in, 16)
            pool.memset(r_pad, 0.0).then_inc(zero_set, 1)
            pool.memset(i_pad[:, 0:PAD], 0.0).then_inc(pads_zero, 1)
            pool.memset(u_pad[:, 0:PAD], 0.0).then_inc(pads_zero, 1)
            pool.iota(empty[:, :, 0].rearrange("p (b s) -> p b s", b=2), [[0, 2], [1, P]], base=SEQ,
                      channel_multiplier=0).then_inc(zero_set, 1)
            pool.memset(empty[:, :, 1], 0).then_inc(zero_set, 1)
            pool.wait_ge(zero_set, 3)
            pool.dma_start(scratch["acc"][SEQ:ROWS, :], r_pad[:, 0:D]).then_inc(zero_out, 16)
            pool.dma_start(scratch["h2"][SEQ:ROWS, :], r_pad[:, 0:D]).then_inc(zero_out, 16)
            pool.dma_start(scratch["table"].rearrange("(p s) w -> p s w", p=P), empty[:, :, :]).then_inc(table_set, 16)
            pool.dma_start(w_r_sb[:, :, :], dram["w_router"][0].rearrange("(k p) n -> p k n", p=P)).then_inc(router_in, 16)
            pool.dma_start(b_r_row[:, :], dram["b_router"][0:1, :].broadcast_to([P, E])).then_inc(router_in, 16)
            pool.wait_ge(table_set, 16)
            for t in range(TT):
                pool.wait_ge(slot_done, t + 1)
                for j in range(TOPK):
                    pool.indirect_dma_start(
                        out=scratch["table"], out_offset=bass.IndirectOffsetOnAxis(ap=sloti[:, t, j:j + 1], axis=0),
                        in_=entry[:, t, j, :], in_offset=None).then_inc(scattered, 16)

        @block.scalar
        def _(act):
            def norms():
                for s in range(NORMED):
                    act.wait_ge(rows_in[s % 3], ring_value(s, 3))
                    if s:
                        act.wait_ge(ss_done, s)
                    nc.scalar.activation(g_t, rows[:, s % 3, :], ACT.Square, accum_out=ss[:, s:s + 1])\
                        .then_inc(ss_done, 1)
                    act.wait_ge(ms_done, s + 1)
                    nc.scalar.activation(sd[:, s:s + 1], ms[:, s:s + 1], ACT.Sqrt).then_inc(sd_done, 1)

            norms()
            act.wait_ge(lam_abs, 1)
            nc.scalar.activation(lam[:, 1, :], lam[:, 0, :], ACT.Exp, scale=-1.0).then_inc(lam_exp, 1)
            act.wait_ge(pads_zero, 2)
            act.wait_ge(zero_out, 32)
            act.wait_ge(table_set, 16)
            act.wait_ge(vec_done, 1)
            act.wait_ge(lam_done, 1)
            for c in range(RT):
                if c:
                    act.wait_ge(conv_done, c)
                for h in range(2):
                    act.wait_ge(proj_ready, 4 * c + h + 1)
                    nc.scalar.activation(u_pad[:, PAD + h * HALF:PAD + (h + 1) * HALF], bank(2 * ((2 * c) % 2) + h)[:, 0, :],
                                         ACT.Copy).then_inc(u_done, 1)
                if c:
                    act.wait_ge(rnn_done, c)
                act.wait_ge(ss_done, NORMED)
                for h in range(2):
                    act.wait_ge(proj_ready, 4 * c + 2 + h + 1)
                    nc.scalar.activation(g_t[:, h * HALF:(h + 1) * HALF], bank(2 + h)[:, 0, :],
                                         ACT.Gelu_apprx_tanh).then_inc(gelu_done, 1)
                if c == 0:
                    act.wait_ge(kv_ready, 1)
                    nc.scalar.activation(kT[:, :, :], bank(4)[:, 0, :].rearrange("p (c m) -> p c m", c=2), ACT.Copy)\
                        .then_inc(kv_done, 1)
                    nc.scalar.activation(v_sb[:, :, :], bank(5)[:, 0, :].rearrange("p (c m) -> p c m", c=MT), ACT.Copy)\
                        .then_inc(kv_done, 1)
                act.wait_ge(gates_ready, c + 1)
                r_f, i_f = r_pad[:, 0:SEQ], i_pad[:, 0:SEQ]
                nc.scalar.activation(r_f, bank(4, 2).rearrange("p b n -> p (b n)"), ACT.Sigmoid,
                                     bias=vec[:, V_BA + c:V_BA + c + 1]).then_inc(sig_done, 1)
                nc.scalar.activation(i_f, bank(6, 2).rearrange("p b n -> p (b n)"), ACT.Sigmoid,
                                     bias=vec[:, V_BI + c:V_BI + c + 1]).then_inc(sig_done, 1)
                act.wait_ge(sig_done, 2 * c + 1)
                nc.scalar.activation(a_t, r_f, ACT.Tanh, scale=lam[:, 7, c:c + 1]).then_inc(tanh_done, 1)
                act.wait_ge(neg_done, c + 1)
                nc.scalar.activation(r_f, r_f, ACT.Sqrt).then_inc(mult_done, 1)
            for j in range(PT_):
                n = 2 * RT + j
                if j == 0:
                    act.wait_ge(conv_done, RT)
                else:
                    act.wait_ge(d_done, j)
                for h in range(2):
                    act.wait_ge(proj_ready, 2 * n + h + 1)
                    nc.scalar.activation(u_pad[:, PAD + h * HALF:PAD + (h + 1) * HALF], bank(2 * (n % 2) + h)[:, 0, :],
                                         ACT.Copy).then_inc(pu_done, 1)
            for j in range(2):
                n = 2 * RT + PT_ + j
                for h in range(2):
                    act.wait_ge(proj_ready, 2 * n + h + 1)
                    nc.scalar.activation(qT[:, j, h * HALF:(h + 1) * HALF], bank(2 * (n % 2) + h)[:, 0, :],
                                         ACT.Copy).then_inc(q_done, 1)
            for j in range(PT_):
                act.wait_ge(pool_ready, j + 1)
                nc.scalar.activation(mixedT[:, RT + j, :], bank(4 + 2 * j, 2).rearrange("p b n -> p (b n)"), ACT.Copy,
                                     scale=vec[:, V_PS + j:V_PS + j + 1]).then_inc(pool_done, 1)

            def probT_evac(t):
                act.wait_ge(pT_ready, t + 1)
                if t >= 2:
                    act.wait_ge(o_ready, t - 1)
                for b in range(2):
                    nc.scalar.activation(probT[:, t % 2, 2 * b:2 * b + 2, :, :],
                                         bank(b)[:, 0, :].rearrange("p (h c t) -> p h c t", h=2, c=MT), ACT.Copy)\
                        .then_inc(pT_done, 1)

            def exps(t):
                act.wait_ge(nmax_done, t + 1)
                if t >= 2:
                    act.wait_ge(pT_ready, t - 1)
                for h in range(HEADS):
                    at = 2 * (h % 2) + h // 2
                    nc.scalar.activation(prob[:, t % 2, h, :], ps[:, 4 + 2 * (t % 2) + h % 2, (h // 2) * N_MEM:(h // 2 + 1) * N_MEM],
                                         ACT.Exp, bias=mx[:, 1, at:at + 1], scale=HD ** -0.5,
                                         accum_out=mx[:, 2, h:h + 1]).then_inc(exp_done, 1)

            exps(0)
            exps(1)
            for t in range(TT):
                probT_evac(t)
                if t + 2 < TT:
                    exps(t + 2)

            def h2T_evac(t):
                act.wait_ge(h2T_ready, t + 1)
                if t >= 2:
                    act.wait_ge(logits_ready, t - 1)
                for b in range(2):
                    nc.scalar.activation(h2T[t % 2][:, 4 * b:4 * b + 4, :], bank(4 + b)[:, 0, :].rearrange("p (k t) -> p k t", k=4),
                                         ACT.Copy).then_inc(h2T_done, 1)

            def gate_exp(t):
                act.wait_ge(top_done, t + 1)
                nc.scalar.activation(gexp[:, :], top8[:, 0:TOPK], ACT.Exp, bias=small[:, 48:49],
                                     accum_out=small[:, 49:50]).then_inc(gexp_done, 1)

            act.wait_ge(rnn_done, RT)
            for t in range(TT):
                if t >= 2:
                    gate_exp(t - 2)
                if t:
                    act.preload_act_table(ACT.Sqrt)
                    h2T_evac(t - 1)
                act.wait_ge(x2_done, t + 1)
                if t >= 2:
                    act.wait_ge(stored[t % 2], 32 * (t // 2))
                nc.scalar.activation(h2[t % 2], x2[t % 2], ACT.Square, accum_out=ss2[:, t % 2:t % 2 + 1]).then_inc(ss2_done, 1)
                act.wait_ge(ms2_done, t + 1)
                nc.scalar.activation(sd2[:, t % 2:t % 2 + 1], ms2[:, t % 2:t % 2 + 1], ACT.Sqrt).then_inc(sd2_done, 1)
            gate_exp(TT - 2)
            h2T_evac(TT - 1)
            gate_exp(TT - 1)

        @block.vector
        def _(dve):
            steps = [0]

            def link(ins):
                steps[0] += 1
                ins.then_inc(dve_step, 1)
                dve.wait_ge(dve_step, steps[0])

            V = nc.vector

            def vector_columns():
                dve.wait_ge(vecT_ready, 1)
                V.tensor_copy(vec[:, :], bank(0)[:, 0, 0:V_N]).then_inc(vec_done, 1)

            def row_scale(s):
                dve.wait_ge(sd_done, s + 1)
                link(V.reciprocal(rs[:, s:s + 1], sd[:, s:s + 1]))
                V.tensor_scalar(rows[:, s % 3, :], rows[:, s % 3, :], rs[:, s:s + 1], None, ALU.mult).then_inc(xn_done, 1)

            def mean_square(s):
                dve.wait_ge(ss_done, s + 1)
                V.tensor_scalar(ms[:, s:s + 1], ss[:, s:s + 1], 1.0 / D, EPS, ALU.mult, ALU.add).then_inc(ms_done, 1)

            def xT_evac(s):
                dve.wait_ge(xT_ready, s + 1)
                gain = V_GMIX if s < TT else V_GMEM
                for b in range(2):
                    dst = xnT[:, 4 * b:4 * b + 4, s * P:(s + 1) * P] if s < TT else \
                        memnT[:, 4 * b:4 * b + 4, (s - TT) * P:(s - TT + 1) * P]
                    V.tensor_tensor(dst, bank(4 + 2 * (s % 2) + b)[:, 0, :].rearrange("p (k t) -> p k t", k=4),
                                    vec[:, gain + 4 * b:gain + 4 * b + 4].unsqueeze(2).broadcast_to([P, 4, P]),
                                    ALU.mult).then_inc(xT_done, 1)

            mean_square(0)
            row_scale(0)
            vector_columns()
            dve.wait_ge(vec_done, 1)
            for s in range(1, NORMED):
                mean_square(s)
                xT_evac(s - 1)
                row_scale(s)
            xT_evac(NORMED - 1)

            y, z, s_, s2_, p_, t_ = (lam[:, i, :] for i in (2, 1, 3, 4, 5, 6))
            link(V.tensor_scalar(y, vec[:, V_LAM:V_LAM + RT], -1.0, None, ALU.mult))
            V.tensor_tensor(lam[:, 0, :], y, vec[:, V_LAM:V_LAM + RT], ALU.max).then_inc(lam_abs, 1)
            dve.wait_ge(lam_exp, 1)
            link(V.tensor_scalar(t_, z, 2.0, None, ALU.add))
            link(V.reciprocal(t_, t_))
            link(V.tensor_tensor(s_, z, t_, ALU.mult))
            link(V.tensor_tensor(s2_, s_, s_, ALU.mult))
            link(V.tensor_scalar(p_, s2_, 1.0 / 17, None, ALU.mult))
            for k in (15, 13, 11, 9, 7, 5, 3):
                link(V.scalar_tensor_tensor(p_, p_, 1.0 / k, s2_, ALU.add, ALU.mult))
            link(V.scalar_tensor_tensor(p_, p_, 1.0, s_, ALU.add, ALU.mult))
            link(V.tensor_scalar(p_, p_, 2.0, None, ALU.mult))
            link(V.scalar_tensor_tensor(t_, y, 0.0, p_, ALU.max, ALU.add))
            V.tensor_scalar(lam[:, 7, :], t_, -LRU_C / 2, None, ALU.mult).then_inc(lam_done, 1)
            dve.wait_ge(consts, 8)
            for j in range(PT_):
                for g in range(2):
                    part = inv_w[g * HD:(g + 1) * HD, j, :]
                    link(V.tensor_scalar(part, part, float(POOL_WINDOWS[2 * j + g]), None, ALU.min))
            link(V.reciprocal(inv_w[:, :, :], inv_w[:, :, :]))

            U0 = PAD - (CONV - 1)
            r_f, i_f = r_pad[:, 0:SEQ], i_pad[:, 0:SEQ]
            for c in range(RT):
                dve.wait_ge(u_done, 2 * c + 2)
                tap = [vec[:, V_CONVW + w * RT + c:V_CONVW + w * RT + c + 1] for w in range(CONV)]
                link(V.tensor_scalar(uc, u_pad[:, PAD:PAD + SEQ], tap[CONV - 1], vec[:, V_CONVB + c:V_CONVB + c + 1],
                                     ALU.mult, ALU.add))
                for w in range(CONV - 1):
                    ins = V.scalar_tensor_tensor(uc, u_pad[:, U0 + w:U0 + w + SEQ], tap[w], uc, ALU.mult, ALU.add)
                    if w < CONV - 2:
                        link(ins)
                    else:
                        ins.then_inc(conv_done, 1)
                dve.wait_ge(tanh_done, c + 1)
                link(V.tensor_scalar(m_t, a_t, -1.0, 1.0, ALU.mult, ALU.add))
                link(V.reciprocal(m_t, m_t))
                link(V.scalar_tensor_tensor(m_t, a_t, 2.0, m_t, ALU.mult, ALU.mult))
                link(V.scalar_tensor_tensor(r_f, m_t, 2.0, m_t, ALU.add, ALU.mult))
                V.tensor_scalar(r_f, r_f, -1.0, 0.0, ALU.mult, ALU.max).then_inc(neg_done, 1)
                dve.wait_ge(sig_done, 2 * c + 2)
                link(V.tensor_tensor(i_f, i_f, uc, ALU.mult))
                link(V.tensor_scalar(a_t, m_t, 1.0, None, ALU.add))
                dve.wait_ge(mult_done, c + 1)
                link(V.memset(r_f[:, 0:1], 1.0))
                link(V.tensor_tensor(i_f, i_f, r_f, ALU.mult))
                link(V.tensor_tensor_scan(m_t, a_t, i_f, 0.0, ALU.mult, ALU.add))
                dve.wait_ge(gelu_done, 2 * c + 2)
                V.tensor_tensor(mixedT[:, c, :], m_t, g_t, ALU.mult).then_inc(rnn_done, 1)

            dve.wait_ge(rnn_done, RT)
            link(V.memset(r_pad[:, 0:PAD], 0.0))
            for j in range(PT_):
                dve.wait_ge(pu_done, 2 * j + 2)
                W = PAD + SEQ
                src, width = u_pad, 1
                bufs = [r_pad, i_pad]
                n_all = 1 if j == 0 else 3
                for k in range(n_all):
                    lead = 2 * width - 1
                    dst = bufs[k % 2]
                    link(V.tensor_tensor(dst[:, lead:W], src[:, lead:W], src[:, lead - width:W - width], ALU.add))
                    src, width = dst, 2 * width
                other = bufs[n_all % 2]
                lead = 2 * width - 1
                V.tensor_tensor(other[HD:P, lead:W], src[HD:P, lead:W], src[HD:P, lead - width:W - width], ALU.add)\
                    .then_inc(dve_step, 1)
                steps[0] += 1
                link(V.tensor_copy(other[0:HD, PAD:W], src[0:HD, PAD:W]))
                link(V.tensor_tensor(src[:, PAD:2 * PAD], other[:, PAD:2 * PAD], inv_w[:, j, :], ALU.mult))
                if j:
                    dve.wait_ge(pool_ready, j)
                link(V.scalar_tensor_tensor(m_t, other[:, PAD:W], inv_w[:, j, PAD - 1:PAD], u_pad[:, PAD:W],
                                            ALU.mult, ALU.subtract))
                V.tensor_tensor(m_t[:, 0:PAD], src[:, PAD:2 * PAD], u_pad[:, PAD:2 * PAD], ALU.subtract).then_inc(d_done, 1)

            def soft_max(t):
                dve.wait_ge(s_ready, t + 1)
                if t:
                    dve.wait_ge(prob_done, t)
                link(V.tensor_reduce(mx[:, 0, :], bank(4 + 2 * (t % 2), 2).rearrange("p b (h m) -> p (b h) m", h=2),
                                     AX.X, ALU.max))
                V.tensor_scalar(mx[:, 1, :], mx[:, 0, :], -(HD ** -0.5), None, ALU.mult).then_inc(nmax_done, 1)
                dve.wait_ge(exp_done, HEADS * (t + 1))
                link(V.reciprocal(mx[:, 3, :], mx[:, 2, :]))
                V.tensor_tensor(prob[:, t % 2], prob[:, t % 2], mx[:, 3, :].unsqueeze(2).broadcast_to([P, HEADS, N_MEM]),
                                ALU.mult).then_inc(prob_done, 1)

            def o_evac(t):
                dve.wait_ge(o_ready, t + 1)
                V.tensor_copy(mixedT[:, RT + PT_:KT, t * P:(t + 1) * P],
                              bank(2 + t % 2)[:, 0, 0:2 * P].rearrange("p (c t) -> p c t", c=2)).then_inc(o_done, 1)

            soft_max(0)
            soft_max(1)
            for t in range(TT):
                if t + 2 < TT:
                    soft_max(t + 2)
                o_evac(t)

            def residual(t):
                dve.wait_ge(out_ready, t + 1)
                item = NORMED + t
                dve.wait_ge(rows_in[item % 3], ring_value(item, 3))
                if t >= 2:
                    dve.wait_ge(stored[t % 2], 32 * (t // 2))
                V.tensor_tensor(x2[t % 2], bank(2 * (t % 2), 2).rearrange("p b n -> p (b n)"), rows[:, item % 3, :],
                                ALU.add).then_inc(x2_done, 1)

            def norm(t):
                i = t % 2
                dve.wait_ge(ss2_done, t + 1)
                V.tensor_scalar(ms2[:, i:i + 1], ss2[:, i:i + 1], 1.0 / D, EPS, ALU.mult, ALU.add).then_inc(ms2_done, 1)
                dve.wait_ge(sd2_done, t + 1)
                link(V.reciprocal(rs2[:, i:i + 1], sd2[:, i:i + 1]))
                if t >= 2:
                    dve.wait_ge(h2T_ready, t - 1)
                V.scalar_tensor_tensor(h2[i], x2[i], rs2[:, i:i + 1], g2_row, ALU.mult, ALU.mult).then_inc(h2_done, 1)

            def pick(t):
                dve.wait_ge(logits_ready, t + 1)
                link(V.tensor_tensor(logits[:, :], bank(6)[:, 0, 0:E], b_r_row[:, :], ALU.add))
                link(V.max(top8[:, :], logits[:, :]))
                V.tensor_scalar(small[:, 48:49], top8[:, 0:1], -1.0, None, ALU.mult).then_inc(top_done, 1)
                link(V.max_index(idx8[:, :], top8[:, :], logits[:, :]))
                link(V.tensor_copy(idxf[:, :], idx8[:, 0:TOPK]))
                link(V.tensor_tensor(onehot[:, :, :], iota_e[:, :].unsqueeze(1).broadcast_to([P, TOPK, E]),
                                     idxf[:, :].unsqueeze(2).broadcast_to([P, TOPK, E]), ALU.is_equal))
                V.tensor_reduce(mask[:, :], onehot[:, :, :].rearrange("p j e -> p e j"), AX.X, ALU.add).then_inc(mask_done, 1)

            def place(t):
                dve.wait_ge(gexp_done, t + 1)
                link(V.reciprocal(small[:, 50:51], small[:, 49:50]))
                link(V.tensor_scalar(entry[:, t, :, 1].bitcast(F32), gexp[:, :], small[:, 50:51], None, ALU.mult))
                link(V.tensor_copy(entry[:, t, :, 0], tokid[:, t:t + 1].broadcast_to([P, TOPK])))
                dve.wait_ge(rank_ready, t + 1)
                link(V.tensor_tensor(slotm[:, :], bank(7)[:, 0, 0:E], run[:, :], ALU.add))
                link(V.tensor_tensor(run[:, :], bank(7)[:, 0, E:2 * E], run[:, :], ALU.add))
                link(V.tensor_tensor(picked[:, :, :], onehot[:, :, :], slotm[:, :].unsqueeze(1).broadcast_to([P, TOPK, E]),
                                     ALU.mult))
                link(V.tensor_reduce(slotf[:, :], picked[:, :, :], AX.X, ALU.add))
                V.tensor_copy(sloti[:, t, :], slotf[:, :]).then_inc(slot_done, 1)

            dve.wait_ge(router_in, 32)
            dve.wait_ge(gain_in, 16)
            for t in range(TT):
                residual(t)
                norm(t)
                if t >= 2:
                    place(t - 2)
                if t:
                    pick(t - 1)
            place(TT - 2)
            pick(TT - 1)
            place(TT - 1)

            rows_of, total, end, le = cnt[:, 0, :], cnt[:, 1, :], cnt[:, 2, :], cnt[:, 3, :]
            link(V.scalar_tensor_tensor(rows_of, iota_e[:, :], -float(CAP), run[:, :], ALU.mult, ALU.add))
            link(V.tensor_scalar(total, rows_of, 0.0, None, ALU.is_gt))
            link(V.memset(total[:, 0:1], 1.0))
            for k in range(1, UNITS_PER_E):
                link(V.scalar_tensor_tensor(total, rows_of, float(UNIT * k), total, ALU.is_gt, ALU.add))
            link(V.tensor_tensor_scan(end, ones[:, 0:E], total, 0.0, ALU.mult, ALU.add))
            expert, b_, row0, two, first_u, left = (ucol[:, i:i + 1] for i in range(6))
            link(V.tensor_scalar(le, end, iota_p[:, 0:1], None, ALU.is_le))
            link(V.tensor_reduce(expert, le, AX.X, ALU.add))
            link(V.tensor_tensor(cnt[:, 4, :], le, total, ALU.mult))
            link(V.tensor_reduce(first_u, cnt[:, 4, :], AX.X, ALU.add))
            link(V.tensor_tensor(b_, iota_p[:, 0:1], first_u, ALU.subtract))
            link(V.tensor_scalar(cnt[:, 5, :], iota_e[:, :], expert, None, ALU.is_equal))
            link(V.tensor_tensor(cnt[:, 6, :], cnt[:, 5, :], rows_of, ALU.mult))
            link(V.tensor_reduce(left, cnt[:, 6, :], AX.X, ALU.add))
            link(V.scalar_tensor_tensor(left, b_, -float(UNIT), left, ALU.mult, ALU.add))
            link(V.tensor_scalar(ucol[:, 8:9], left, float(P), None, ALU.is_gt))
            link(V.scalar_tensor_tensor(ucol[:, 8:9], left, float(P + TAIL), ucol[:, 8:9], ALU.is_gt, ALU.add))
            link(V.tensor_scalar(ucol[:, 6:7], expert, float(E - 1), None, ALU.min))
            link(V.scalar_tensor_tensor(row0, expert, float(UNITS_PER_E), b_, ALU.mult, ALU.add))
            link(V.tensor_scalar(ucol[:, 7:8], row0, float(E * UNITS_PER_E - 1), None, ALU.min))
            link(V.tensor_scalar(ucol[:, 7:8], ucol[:, 7:8], float(UNIT), None, ALU.mult))
            V.tensor_copy(ucol[:, 9:10], end[:, E - 1:E]).then_inc(ucol_done, 1)
            dve.wait_ge(utab_ready, 1)
            link(V.tensor_copy(utab[0:1, :], bank(6)[0:1, 0, :]))

        @block.tensor
        def _(pe):
            T = nc.tensor
            pe.wait_ge(vrows_in, 16 * 8)
            pe.wait_ge(consts, 1)
            T.transpose(bank(0)[:, 0, 0:V_N], vrows[0:V_N, :], ident[0:V_N, 0:V_N]).then_inc(vecT_ready, 1)
            for s in range(NORMED):
                pe.wait_ge(xn_done, s + 1)
                if s >= 2:
                    pe.wait_ge(xT_done, 2 * (s - 1))
                for k in range(KT):
                    last = T.transpose(bank(4 + 2 * (s % 2) + k // 4)[:, 0, (k % 4) * P:(k % 4 + 1) * P],
                                       rows[:, s % 3, k * P:(k + 1) * P], ident[:, :])
                last.then_inc(xT_ready, 1)

            def project(n):
                pe.wait_ge(w_in_in[n % 3], ring_value(n, 3))
                for h in range(2):
                    if n == 0:
                        pe.wait_ge(xT_done, 2 * 4 * (h + 1))
                        pe.wait_ge(vec_done, 1)
                    if n == 2 or n == 3:
                        pe.wait_ge(u_done if n == 2 else gelu_done, h + 1)
                    elif 4 <= n < 2 * RT + 2:
                        c = (n - 2) // 2
                        pe.wait_ge(u_done if n % 2 == 0 else gelu_done, 2 * c + h + 1)
                    elif n >= 2 * RT + 2:
                        pe.wait_ge(pu_done, 2 * (n - 2 * RT - 2) + h + 1)
                    for k in range(KT):
                        last = T.matmul(bank(2 * (n % 2) + h)[:, 0, :], w_in_sb[:, n % 3, k, :],
                                        xnT[:, k, h * HALF:(h + 1) * HALF], start=(k == 0), stop=(k == KT - 1))
                    last.then_inc(proj_ready, 1)

            def keys_values():
                pe.wait_ge(kv_in, 16)
                pe.wait_ge(xT_done, 2 * NORMED)
                for c in range(2):
                    for k in range(KT):
                        T.matmul(bank(4)[:, 0, c * N_MEM:(c + 1) * N_MEM], w_kv_sb[:, k, c * P:(c + 1) * P],
                                 memnT[:, k, :], start=(k == 0), stop=(k == KT - 1))
                for m in range(MT):
                    for k in range(KT):
                        last = T.matmul(bank(5)[:, 0, m * D_XATTN:(m + 1) * D_XATTN], memnT[:, k, m * P:(m + 1) * P],
                                        w_kv_sb[:, k, D_XATTN:2 * D_XATTN], start=(k == 0), stop=(k == KT - 1))
                last.then_inc(kv_ready, 1)

            def gates(c):
                pe.wait_ge(conv_done, c + 1)
                pe.wait_ge(bd_in, 16 * 6)
                if c == 0:
                    pe.wait_ge(kv_done, 2)
                else:
                    pe.wait_ge(sig_done, 2 * c)
                for g in range(2):
                    for h in range(2):
                        last = T.matmul(bank(4 + 2 * g + h)[:, 0, :], blockdiag[:, g * RT + c, :],
                                        uc[:, h * HALF:(h + 1) * HALF], start=True, stop=True)
                last.then_inc(gates_ready, 1)

            for c in range(RT):
                project(2 * c)
                project(2 * c + 1)
                if c == 0:
                    keys_values()
                gates(c)

            def pool_map(j):
                pe.wait_ge(d_done, j + 1)
                if j == 0:
                    pe.wait_ge(sig_done, 2 * RT)
                for h in range(2):
                    last = T.matmul(bank(4 + 2 * j + h)[:, 0, :], blockdiag[:, 2 * RT + j, :],
                                    m_t[:, h * HALF:(h + 1) * HALF], start=True, stop=True)
                last.then_inc(pool_ready, 1)

            project(2 * RT)
            project(2 * RT + 1)
            project(2 * RT + 2)
            pool_map(0)
            project(2 * RT + 3)
            pool_map(1)

            def scores(t):
                if t < 2:
                    pe.wait_ge(pool_done, t + 1)
                    pe.wait_ge(q_done, 4)
                else:
                    pe.wait_ge(exp_done, HEADS * (t - 1))
                for h in range(HEADS):
                    half = slice((h % 2) * HD, (h % 2 + 1) * HD)
                    last = T.matmul(ps[:, 4 + 2 * (t % 2) + h % 2, (h // 2) * N_MEM:(h // 2 + 1) * N_MEM],
                                    qT[half, h // 2, t * P:(t + 1) * P], kT[half, h // 2, :], start=True, stop=True)
                last.then_inc(s_ready, 1)

            def transpose_prob(t):
                pe.wait_ge(prob_done, t + 1)
                if t:
                    pe.wait_ge(pT_done, 2 * t)
                for h in range(HEADS):
                    for m in range(MT):
                        o = ((h % 2) * MT + m) * P
                        last = T.transpose(bank(h // 2)[:, 0, o:o + P], prob[:, t % 2, h, m * P:(m + 1) * P], ident[:, :])
                last.then_inc(pT_ready, 1)

            def attend(t):
                pe.wait_ge(pT_done, 2 * (t + 1))
                if t >= 2:
                    pe.wait_ge(o_done, t - 1)
                for h in range(HEADS):
                    for m in range(MT):
                        last = T.matmul(ps[(h % 2) * HD:(h % 2 + 1) * HD, 2 + t % 2, (h // 2) * P:(h // 2 + 1) * P],
                                        v_sb[:, m, h * HD:(h + 1) * HD], probT[:, t % 2, h, m, :],
                                        start=(m == 0), stop=(m == MT - 1))
                last.then_inc(o_ready, 1)

            scores(0)
            scores(1)
            for t in range(TT):
                transpose_prob(t)
                if t + 2 < TT:
                    scores(t + 2)
                attend(t)

            def transpose_h2(t):
                pe.wait_ge(h2_done, t + 1)
                if t:
                    pe.wait_ge(h2T_done, 2 * t)
                else:
                    pe.wait_ge(exp_done, HEADS * TT)
                for k in range(KT):
                    last = T.transpose(bank(4 + k // 4)[:, 0, (k % 4) * P:(k % 4 + 1) * P],
                                       h2[t % 2][:, k * P:(k + 1) * P], ident[:, :])
                last.then_inc(h2T_ready, 1)

            def out_project(t):
                if t == 0:
                    pe.wait_ge(wout_in, 16)
                    pe.wait_ge(rnn_done, RT)
                    pe.wait_ge(pool_done, PT_)
                    pe.wait_ge(o_done, TT)
                elif t >= 2:
                    pe.wait_ge(x2_done, t - 1)
                for k in range(KT):
                    if t and k == KT // 2:
                        transpose_h2(t - 1)
                    for h in range(2):
                        last = T.matmul(bank(2 * (t % 2) + h)[:, 0, :], mixedT[:, k, t * P:(t + 1) * P],
                                        w_out_sb[:, k, h * HALF:(h + 1) * HALF], start=(k == 0), stop=(k == KT - 1))
                last.then_inc(out_ready, 1)

            def route(t):
                pe.wait_ge(h2T_done, 2 * (t + 1))
                if t:
                    pe.wait_ge(mask_done, t)
                else:
                    pe.wait_ge(router_in, 32)
                for k in range(KT):
                    last = T.matmul(bank(6)[:, 0, 0:E], h2T[t % 2][:, k, :], w_r_sb[:, k, :],
                                    start=(k == 0), stop=(k == KT - 1))
                last.then_inc(logits_ready, 1)

            def rank(t):
                pe.wait_ge(mask_done, t + 1)
                pe.wait_ge(consts, 8)
                if t:
                    pe.wait_ge(slot_done, t)
                T.matmul(bank(7)[:, 0, 0:E], lower[:, :], mask[:, :], start=True, stop=True)
                T.matmul(bank(7)[:, 0, E:2 * E], ones[:, :], mask[:, :], start=True, stop=True).then_inc(rank_ready, 1)

            out_project(0)
            for t in range(1, TT):
                out_project(t)
                if t >= 2:
                    rank(t - 2)
                route(t - 1)
            transpose_h2(TT - 1)
            rank(TT - 2)
            route(TT - 1)
            rank(TT - 1)
            pe.wait_ge(ucol_done, 1)
            for i in range(4):
                last = T.matmul(bank(6)[0:1, 0, i * P:(i + 1) * P], ucol[:, 6 + i:7 + i], ident[:, :], start=True, stop=True)
            last.then_inc(utab_ready, 1)


def load_half(sp, dram, shared, expert, j):
    at = bass.ds(expert, 1) if not isinstance(expert, int) else slice(expert, expert + 1)
    c, h = j // 2, j % 2
    ks = slice(h * HALFK, (h + 1) * HALFK)
    slot, signal = shared["raw"][:, j % RAW, :, :], shared["raw_in"][j % RAW]
    if c < GU_CH:
        w = dram["w_gu"][0, at].rearrange("a (k p) n -> p (a k) n", p=P)
        q = FF // GU_CH
        for g in range(2):
            lo = g * FF + c * q
            sp.dma_start(slot[:, :, g * q:(g + 1) * q], w[:, ks, lo:lo + q]).then_inc(signal, 16)
    else:
        w = dram["w_down"][0, at].rearrange("a (k p) n -> p (a k) n", p=P)
        lo = (c - GU_CH) * HALF
        for g in range(2):
            part = slice(h * HALFK + g * HALFK // 2, h * HALFK + (g + 1) * HALFK // 2)
            sp.dma_start(slot[:, g * HALFK // 2:(g + 1) * HALFK // 2, :], w[:, part, lo:lo + HALF]).then_inc(signal, 16)


def expert_phase(nc, dram, scratch, shared):
    ctx = ExitStack()
    with ctx:
        def sb(name, shape, dt=F32):
            return ctx.enter_context(nc.sbuf_tensor(name, shape, dt))

        def sem(name):
            return ctx.enter_context(nc.semaphore(name))

        raw, utab, ps, raw_in = shared["raw"], shared["utab"], shared["ps"], shared["raw_in"]
        w_hi = sb("w_hi", [P, SPLIT, HALFK, HALF], F32R)
        w_lo = sb("w_lo", [P, SPLIT, HALFK, HALF], F32R)
        x_rows = sb("x_rows", [P, 2, D])
        xT = sb("xT", [P, KT, 4 * P], F32R)
        hT = sb("hT", [P, KT, 4 * P], F32R)
        y = sb("y", [P, 2, D])
        b_gu_row = sb("b_gu_row", [P, 2, FF])
        b_dn_row = sb("b_dn_row", [P, D])
        gu = sb("gu", [P, 2, 2, HALF])
        sg = sb("sg", [P, 2, 2, HALF // 2])
        next_list = sb("next_list", [P, 2, 2], I32)
        this_list = sb("this_list", [P, 2, 2], I32)
        stand_in = sb("stand_in", [1, 2], I32)
        ident = sb("ident2", [P, P])

        hi_done, lo_done, mm_done, acc_free = (sem(n) for n in ("hi_done", "lo_done", "mm_done", "acc_free"))
        gmin_done, sig_done, h_done, pool_step = (sem(n) for n in ("gmin_done", "sig_done2", "h_done", "pool_step2"))
        hT_ready, hT_hi_done, hT_lo_done = (sem(n) for n in ("hT_ready", "hT_hi_done", "hT_lo_done"))
        xT_ready, xT_hi_done, xT_lo_done = (sem(n) for n in ("xT_ready2", "xT_hi_done", "xT_lo_done"))
        y_biased, y_gated = sem("y_biased"), sem("y_gated")
        b_gu_in, b_dn_in, next_in, this_in, x_in, added = (
            sem(n) for n in ("b_gu_in", "b_dn_in", "next_in", "this_in", "x_in", "added"))
        cleared = sem("cleared")
        id_done, tail_step = sem("id_done"), sem("tail_step")
        b_gu_done, b_dn_done = sem("b_gu_done"), sem("b_dn_done")
        held = {e: sem(f"held_{e}") for e in ("sp", "pool", "act", "dve", "pe")}
        Q = FF // GU_CH

        block = ctx.enter_context(nc.Block("experts"))

        def rounded(buf, pair, nb):
            return buf[:, 2 * pair:2 * pair + 2, :].rearrange("p k (b s t) -> p k b s t", b=2, s=2)[:, :, 0:nb, 0, :]

        def transposed(bank, nb):
            return ps[:, bank, :].rearrange("p (k b t) -> p k b t", k=2, b=2)[:, :, 0:nb, :]

        def unit_value(eng, row, u, top):
            return eng.value_load(utab[0:1, bass.ds(u + row * P, 1)], min_val=0, max_val=top)

        def n_units(eng):
            return eng.value_load(utab[0:1, 3 * P:3 * P + 1], min_val=1, max_val=E + TOPK * SEQ // UNIT)

        @block.sync
        def _(sp):
            n = n_units(sp)

            with sp.Fori(0, n) as u:
                expert = unit_value(sp, 0, u, E - 1)
                after = unit_value(sp, 0, u + 1, E - 1)
                for j in range(RAW, RAW + 2 * CH):
                    hold(sp, lo_done, 2 * CH * u + j - RAW + 1, held["sp"])
                    if j < 2 * CH:
                        load_half(sp, dram, shared, expert, j)
                    else:
                        with sp.If(u + 1 < n):
                            load_half(sp, dram, shared, after, j - 2 * CH)

        @block.gpsimd
        def _(pool):
            G = nc.gpsimd
            n = n_units(pool)
            pool.memset(ident[:, :], 0.0).then_inc(pool_step, 1)
            pool.wait_ge(pool_step, 1)
            pool.affine_select(out=ident[:, :], in_=ident[:, :], compare_op=ALU.not_equal, fill=1.0,
                               base=0, pattern=[[-1, P]], channel_multiplier=1).then_inc(id_done, 1)

            def load_list(dst, row0, signal):
                pool.dma_start(dst[:, :, :], scratch["table"][bass.ds(row0, UNIT), :]
                               .rearrange("(b p) w -> p b w", p=P)).then_inc(signal, 16)

            def gather(two):
                pool.indirect_dma_start(
                    out=x_rows[:, 0, :], out_offset=None, in_=scratch["h2"],
                    in_offset=bass.IndirectOffsetOnAxis(ap=next_list[:, 0, 0:1], axis=0)).then_inc(x_in, 16)
                def second(rows):
                    pool.indirect_dma_start(
                        out=x_rows[0:rows, 1, :], out_offset=None, in_=scratch["h2"],
                        in_offset=bass.IndirectOffsetOnAxis(ap=next_list[0:rows, 1, 0:1], axis=0)).then_inc(x_in, 16)
                with pool.If(two > 0):
                    with pool.If(two > 1):
                        second(P)
                    with pool.Else():
                        second(TAIL)
                with pool.Else():
                    pool.dma_start(stand_in[:, :], scratch["table"][0:1, :]).then_inc(x_in, 16)

            def gate_up_bias(expert):
                pool.dma_start(x_rows[0:1, :, :].rearrange("p b n -> p (b n)"), dram["b_gu"][0, bass.ds(expert, 1)])\
                    .then_inc(b_gu_in, 16)

            def gate_up_bias_spread(landed):
                G.partition_broadcast(b_gu_row[:, :, :].rearrange("p g f -> p (g f)"),
                                      landed[0:1, :, :].rearrange("p b n -> p (b n)")).then_inc(b_gu_done, 1)

            pool.wait_ge(id_done, 1)
            load_list(next_list, unit_value(pool, 1, 0, E * CAP - UNIT), next_in)
            for i, buf in enumerate((x_rows[TAIL:P, 1, :], y[TAIL:P, 1, :], gu[TAIL:P, :, 1, :])):
                if i:
                    pool.wait_ge(cleared, i)
                pool.memset(buf, 0.0).then_inc(cleared, 1)
            pool.wait_ge(cleared, 3)
            pool.wait_ge(next_in, 16)
            gather(unit_value(pool, 2, 0, 2))
            pool.dma_start(y[0:1, :, :].rearrange("p b n -> p (b n)"), dram["b_gu"][0, bass.ds(unit_value(pool, 0, 0, E - 1), 1)])\
                .then_inc(b_gu_in, 16)
            pool.wait_ge(x_in, 32)
            for i in range(2):
                pool.dma_start(stand_in[:, :], scratch["table"][0:1, :]).then_inc(added, 16)
                pool.wait_ge(added, 16 * (i + 1))
            pool.wait_ge(b_gu_in, 16)
            gate_up_bias_spread(y)
            with pool.Fori(0, n) as u:
                expert = unit_value(pool, 0, u, E - 1)
                expert_next = unit_value(pool, 0, u + 1, E - 1)
                row0 = unit_value(pool, 1, u, E * CAP - UNIT)
                row0_next = unit_value(pool, 1, u + 1, E * CAP - UNIT)
                two = unit_value(pool, 2, u, 2)
                two_next = unit_value(pool, 2, u + 1, 2)
                for c in range(GU_CH):
                    par = c % 2
                    hold(pool, sig_done, 2 * (GU_CH * u + c + 1), held["pool"])

                    def swiglu(nb, c=c, par=par):
                        gate, up = gu[:, par, 0:nb, 0:Q], gu[:, par, 0:nb, Q:2 * Q]
                        G.tensor_tensor(gate, gate, sg[:, par, 0:nb, :], ALU.mult).then_inc(pool_step, 1)
                        pool.wait_ge(pool_step, GU_CH * u + c + 2)
                        G.tensor_tensor(up, up, gate, ALU.mult).then_inc(h_done, 1)

                    with pool.If(two > 0):
                        swiglu(2)
                    with pool.Else():
                        swiglu(1)
                    if c == 0:
                        hold(pool, x_in, 32 * (u + 1), held["pool"])
                        load_list(next_list, row0_next, next_in)
                        hold(pool, added, 32 * u + 32, held["pool"])
                        load_list(this_list, row0, this_in)
                        pool.dma_start(y[0:1, 0, :], dram["b_down"][0, bass.ds(expert, 1)]).then_inc(b_dn_in, 16)
                    if c == 1:
                        hold(pool, next_in, 16 * (u + 2), held["pool"])
                        hold(pool, xT_ready, KT // 2 * (u + 1), held["pool"])
                        gather(two_next)
                        hold(pool, b_dn_in, 16 * (u + 1), held["pool"])
                        G.partition_broadcast(b_dn_row[:, :], y[0:1, 0, :]).then_inc(b_dn_done, 1)
                hold(pool, xT_ready, KT // 2 * (u + 2), held["pool"])
                gate_up_bias(expert_next)
                hold(pool, b_gu_in, 16 * (u + 2), held["pool"])
                gate_up_bias_spread(x_rows)
                hold(pool, y_gated, DN_CH * (u + 1), held["pool"])

                def add_second(rows):
                    pool.indirect_dma_start(
                        out=scratch["acc"], out_offset=bass.IndirectOffsetOnAxis(ap=this_list[0:rows, 1, 0:1], axis=0),
                        in_=y[0:rows, 1, :], in_offset=None, compute_op=ALU.add).then_inc(added, 16)
                with pool.If(two > 0):
                    with pool.If(two > 1):
                        add_second(P)
                    with pool.Else():
                        add_second(TAIL)
                with pool.Else():
                    pool.dma_start(stand_in[:, :], scratch["table"][0:1, :]).then_inc(added, 16)
                pool.indirect_dma_start(
                    out=scratch["acc"], out_offset=bass.IndirectOffsetOnAxis(ap=this_list[:, 0, 0:1], axis=0),
                    in_=y[:, 0, :], in_offset=None, compute_op=ALU.add).then_inc(added, 16)
            hold(pool, added, 32 * n + 32, held["pool"])
            hold(pool, x_in, 32 * (n + 1), held["pool"])
            hold(pool, next_in, 16 * (n + 1), held["pool"])

        @block.scalar
        def _(act):
            n = n_units(act)

            def split_hi(j):
                nc.scalar.activation(w_hi[:, j % SPLIT, :, :], raw[:, j % RAW, :, :], ACT.Copy).then_inc(hi_done, 1)

            def x_hi(nb):
                def emit(g):
                    nc.scalar.activation(rounded(xT, g, nb),
                                         transposed(6 + g % 2, nb),
                                         ACT.Copy).then_inc(xT_hi_done, 1)
                return emit

            def next_x(base, two, groups):
                with act.If(two > 0):
                    for g in groups:
                        act.wait_ge(xT_ready, base + g + 1)
                        x_hi(2)(g)
                with act.Else():
                    for g in groups:
                        act.wait_ge(xT_ready, base + g + 1)
                        x_hi(1)(g)

            act.preload_act_table(ACT.Sigmoid)
            for j in range(SPLIT):
                if j == RAW:
                    next_x(0, unit_value(act, 2, 0, 2), range(KT // 2))
                act.wait_ge(raw_in[j % RAW], 32 * (j // RAW + 1))
                split_hi(j)
            with act.Fori(0, n) as u:
                two = unit_value(act, 2, u, 2)
                two_next = unit_value(act, 2, u + 1, 2)

                def sigmoid(c):
                    hold(act, gmin_done, 2 * (GU_CH * u + c) + 1, held["act"])

                    def for_nb(nb):
                        up = gu[:, c % 2, 0:nb, Q:2 * Q]
                        nc.scalar.activation(sg[:, c % 2, 0:nb, :], gu[:, c % 2, 0:nb, 0:Q], ACT.Sigmoid,
                                             scale=SWIGLU_ALPHA).then_inc(sig_done, 1)
                        act.wait_ge(gmin_done, 2 * (GU_CH * u + c) + 2)
                        nc.scalar.activation(up, up, ACT.Copy, bias=1.0).then_inc(sig_done, 1)
                    with act.If(two > 0):
                        for_nb(2)
                    with act.Else():
                        for_nb(1)

                def h_hi(c):
                    hold(act, hT_ready, GU_CH * u + c + 1, held["act"])
                    for_nb = lambda nb: nc.scalar.activation(
                        rounded(hT, c, nb),
                        transposed(4 + c % 2, nb),
                        ACT.Copy).then_inc(hT_hi_done, 1)
                    with act.If(two > 0):
                        for_nb(2)
                    with act.Else():
                        for_nb(1)

                def gate_y(c):
                    i = c - GU_CH
                    hold(act, y_biased, DN_CH * u + i + 1, held["act"])
                    cols = slice(i * HALF, (i + 1) * HALF)
                    gates = this_list[:, :, 1].bitcast(F32)
                    hold(act, this_in, 16 * (u + 1), held["act"])
                    with act.If(two > 0):
                        nc.scalar.activation(y[:, 1, cols], y[:, 1, cols], ACT.Copy, scale=gates[:, 1:2])
                        nc.scalar.activation(y[:, 0, cols], y[:, 0, cols], ACT.Copy, scale=gates[:, 0:1]).then_inc(y_gated, 1)
                    with act.Else():
                        nc.scalar.activation(y[:, 0, cols], y[:, 0, cols], ACT.Copy, scale=gates[:, 0:1]).then_inc(y_gated, 1)

                def refill(c, h):
                    j = 2 * (c + AHEAD) + h

                    def emit():
                        act.wait_ge(mm_done, 2 * (CH * u + c) + h + 1)
                        act.wait_ge(raw_in[j % RAW], 32 * 2 * CH // RAW * u + 32 * (j // RAW + 1))
                        split_hi(j)
                    if j < 2 * CH:
                        emit()
                    else:
                        with act.If(u + 1 < n):
                            emit()

                for c in range(CH):
                    if c == GU_CH:
                        h_hi(c - 1)
                        next_x(KT // 2 * (u + 1), two_next, (0, 1))
                    if c == CH - 1:
                        next_x(KT // 2 * (u + 1), two_next, (2, 3))
                    refill(c, 0)
                    if c == CH - 1:
                        gate_y(c - 1)
                    if 0 < c < GU_CH:
                        h_hi(c - 1)
                    if c == GU_CH - 1:
                        sigmoid(c)
                    refill(c, 1)
                    if c < GU_CH - 1:
                        sigmoid(c)
                gate_y(CH - 1)

        @block.vector
        def _(dve):
            V = nc.vector
            n = n_units(dve)
            dve.sem_inc(acc_free, 2)
            dve.sem_inc(hT_lo_done, 1)

            def split_lo(j, before):
                dve.wait_ge(hi_done, before + j + 1)
                V.tensor_tensor(w_lo[:, j % SPLIT, :, :], raw[:, j % RAW, :, :], w_hi[:, j % SPLIT, :, :].bitcast(F32),
                                ALU.subtract).then_inc(lo_done, 1)

            def remainders(buf, pair, bank, two, signal, wait):
                def sub(rows, b0, nb, at):
                    cols = buf[:, 2 * pair:2 * pair + 2, :]
                    hi = cols.rearrange("p k (b s t) -> p k b s t", b=2, s=2)[:, :, b0:b0 + nb, 0, 0:rows]
                    out = cols[:, :, at:at + rows].unsqueeze(2) if nb == 1 else \
                        cols.rearrange("p k (b s t) -> p k b s t", b=2, s=2)[:, :, :, 1, :]
                    return V.tensor_tensor(out, transposed(bank, 2)[:, :, b0:b0 + nb, 0:rows], hi.bitcast(F32), ALU.subtract)
                wait()
                if two == 2:
                    sub(P, 0, 2, P).then_inc(signal, 1)
                else:
                    if two == 1:
                        sub(TAIL, 1, 1, 2 * P + TAIL)
                    sub(P, 0, 1, P).then_inc(signal, 1)

            def per_blocks(two, emit):
                with dve.If(two > 0):
                    with dve.If(two > 1):
                        emit(2)
                    with dve.Else():
                        emit(1)
                with dve.Else():
                    emit(0)

            def next_x(base, two, groups):
                def emit(case):
                    for g in groups:
                        remainders(xT, g, 6 + g % 2, case, xT_lo_done, lambda g=g: dve.wait_ge(xT_hi_done, base + g + 1))
                per_blocks(two, emit)

            for j in range(SPLIT):
                if j == RAW:
                    next_x(0, unit_value(dve, 2, 0, 2), range(KT // 2))
                split_lo(j, 0)
            with dve.Fori(0, n) as u:
                two = unit_value(dve, 2, u, 2)
                two_next = unit_value(dve, 2, u + 1, 2)

                def evacuate(c):
                    hold(dve, mm_done, 2 * (CH * u + c) + 2, held["dve"])
                    if c < GU_CH:
                        if c == 0:
                            hold(dve, b_gu_done, u + 1, held["dve"])
                        if c >= 2:
                            hold(dve, hT_ready, GU_CH * u + c - 1, held["dve"])
                        bias = b_gu_row[:, :, c * Q:(c + 1) * Q]
                        dst = lambda nb: gu[:, c % 2, 0:nb, :]
                    else:
                        if c == GU_CH:
                            hold(dve, b_dn_done, u + 1, held["dve"])
                            hold(dve, added, 32 * u + 32, held["dve"])
                        i = c - GU_CH
                        bias = b_dn_row[:, i * HALF:(i + 1) * HALF].rearrange("p (g q) -> p g q", g=2)
                        dst = lambda nb: y[:, 0:nb, i * HALF:(i + 1) * HALF]

                    def biased(out, acc, bias, nb):
                        return V.tensor_tensor(out.rearrange("p b (g q) -> p b g q", g=2),
                                               acc.rearrange("p b (g q) -> p b g q", g=2),
                                               bias.unsqueeze(1).broadcast_to([bias.shape[0], nb, 2, HALF // 2]), ALU.add)

                    acc = ps[:, 2 * (c % 2):2 * (c % 2) + 2, :]

                    def clip(nb):
                        gate, up = gu[:, c % 2, 0:nb, 0:Q], gu[:, c % 2, 0:nb, Q:2 * Q]
                        V.tensor_scalar(gate, gate, SWIGLU_LIMIT, None, ALU.min).then_inc(gmin_done, 1)
                        V.tensor_scalar(up, up, -SWIGLU_LIMIT, SWIGLU_LIMIT, ALU.max, ALU.min).then_inc(gmin_done, 1)

                    def finish(nb):
                        if c >= GU_CH:
                            V.engine_nop().then_inc(y_biased, 1)
                        if c < GU_CH:
                            dve.wait_ge(acc_free, CH * u + c + 3)
                            clip(nb)

                    with dve.If(two > 0):
                        with dve.If(two > 1):
                            biased(dst(2), acc, bias, 2).then_inc(acc_free, 1)
                            dve.sem_inc(tail_step, 1)
                        with dve.Else():
                            tail = dst(2)[0:TAIL, 1:2, :]
                            biased(tail, acc[TAIL:P, 1:2, :], bias[TAIL:P], 1).then_inc(tail_step, 1)
                            biased(dst(1), acc[:, 0:1, :], bias, 1)
                            dve.wait_ge(tail_step, CH * u + c + 1)
                            V.tensor_tensor(tail, acc[0:TAIL, 1:2, :], tail, ALU.add).then_inc(acc_free, 1)
                        finish(2)
                    with dve.Else():
                        biased(dst(1), acc[:, 0:1, :], bias, 1).then_inc(acc_free, 1)
                        dve.sem_inc(tail_step, 1)
                        finish(1)

                def h_lo(c):
                    hold(dve, hT_hi_done, GU_CH * u + c + 1, held["dve"])
                    per_blocks(two, lambda case: remainders(hT, c, 4 + c % 2, case, hT_lo_done, lambda: None))

                def refill(c, h):
                    j = 2 * (c + AHEAD) + h
                    if j < 2 * CH:
                        split_lo(j, 2 * CH * u)
                    else:
                        with dve.If(u + 1 < n):
                            split_lo(j, 2 * CH * u)

                for c in range(CH):
                    if c == GU_CH:
                        h_lo(c - 1)
                        next_x(KT // 2 * (u + 1), two_next, (0, 1))
                    if c == CH - 1:
                        next_x(KT // 2 * (u + 1), two_next, (2, 3))
                    refill(c, 0)
                    evacuate(c)
                    if 0 < c < GU_CH:
                        h_lo(c - 1)
                    refill(c, 1)

        @block.tensor
        def _(pe):
            T = nc.tensor
            n = n_units(pe)

            def transpose_x(base, two, after_unit, groups=range(KT // 2)):
                for g in groups:
                    if g >= 2 or after_unit:
                        pe.wait_ge(xT_lo_done, base + g - 1)
                    def block_of(b, g=g):
                        for j in range(2):
                            last = T.transpose(ps[:, 6 + g % 2, (2 * j + b) * P:(2 * j + b + 1) * P],
                                               x_rows[:, b, (2 * g + j) * P:(2 * g + j + 1) * P], ident[:, :])
                        return last
                    with pe.If(two > 0):
                        block_of(1)
                    block_of(0).then_inc(xT_ready, 1)

            pe.wait_ge(id_done, 1)
            pe.wait_ge(x_in, 32)
            transpose_x(0, unit_value(pe, 2, 0, 2), False)
            with pe.Fori(0, n) as u:
                two = unit_value(pe, 2, u, 2)
                two_next = unit_value(pe, 2, u + 1, 2)

                def part(c, b, ks):
                    xs = xT if c < GU_CH else hT
                    out = ps[:, 2 * (c % 2) + b, :]
                    for k in ks:
                        slot, kk = (2 * c + k // HALFK) % SPLIT, k % HALFK
                        hi, lo = (xs[:, k, (2 * b + i) * P:(2 * b + i + 1) * P] for i in range(2))
                        T.matmul(out, hi, w_hi[:, slot, kk, :], start=k == 0, stop=False)
                        T.matmul(out, hi, w_lo[:, slot, kk, :], start=False, stop=False)
                        last = T.matmul(out, lo, w_hi[:, slot, kk, :], start=False, stop=k == KT - 1)
                    return last

                def tail_part(c, ks):
                    xs = xT if c < GU_CH else hT
                    out = ps[:, 2 * (c % 2) + 1, :]
                    for k in ks:
                        slot, kk = (2 * c + k // HALFK) % SPLIT, k % HALFK
                        both = xs[:, k, 2 * P:2 * P + 2 * TAIL]
                        T.matmul(out, both, w_hi[:, slot, kk, :], start=k == 0, stop=False)
                        T.matmul(out, both, w_lo[:, slot, kk, :], start=False, stop=k == KT - 1)

                def steps(c, ks):
                    pe.wait_ge(lo_done, 2 * CH * u + 2 * c + ks[0] // HALFK + 1)
                    with pe.If(two > 0):
                        with pe.If(two > 1):
                            part(c, 1, ks)
                        with pe.Else():
                            tail_part(c, ks)
                    return part(c, 0, ks)

                def transpose_h(c):
                    hold(pe, h_done, GU_CH * u + c + 1, held["pe"])
                    if c >= 2:
                        pe.wait_ge(hT_lo_done, GU_CH * u + c - 1 + 1)
                    else:
                        pe.wait_ge(hT_lo_done, GU_CH * u + 1)

                    def block_of(b):
                        for j in range(2):
                            last = T.transpose(ps[:, 4 + c % 2, (2 * j + b) * P:(2 * j + b + 1) * P],
                                               gu[:, c % 2, b, Q + j * P:Q + (j + 1) * P], ident[:, :])
                        return last
                    with pe.If(two > 0):
                        block_of(1)
                    block_of(0).then_inc(hT_ready, 1)

                first_half, second_half = range(HALFK), range(HALFK, KT)
                pe.wait_ge(xT_lo_done, KT // 2 * (u + 1))
                for c in range(GU_CH):
                    pe.wait_ge(acc_free, CH * u + c - 1 + 2)
                    steps(c, first_half).then_inc(mm_done, 1)
                    steps(c, second_half).then_inc(mm_done, 1)
                    if c:
                        transpose_h(c - 1)
                pe.wait_ge(acc_free, CH * u + GU_CH - 1 + 2)
                pe.wait_ge(hT_lo_done, GU_CH * u + 2 + 1)
                steps(GU_CH, first_half).then_inc(mm_done, 1)
                pe.wait_ge(hT_lo_done, GU_CH * u + 3 + 1)
                steps(GU_CH, range(HALFK, KT - 2))
                transpose_h(GU_CH - 1)
                pe.wait_ge(x_in, 32 * (u + 2))
                transpose_x(KT // 2 * (u + 1), two_next, True, (0, 1))
                pe.wait_ge(hT_lo_done, GU_CH * (u + 1) + 1)
                steps(GU_CH, range(KT - 2, KT)).then_inc(mm_done, 1)
                pe.wait_ge(acc_free, CH * u + CH - 2 + 2)
                steps(CH - 1, first_half).then_inc(mm_done, 1)
                transpose_x(KT // 2 * (u + 1), two_next, True, (2, 3))
                steps(CH - 1, second_half).then_inc(mm_done, 1)


def final_phase(nc, dram, scratch, out):
    ctx = ExitStack()
    with ctx:
        def sb(name, shape, dt=F32):
            return ctx.enter_context(nc.sbuf_tensor(name, shape, dt))

        def sem(name):
            return ctx.enter_context(nc.semaphore(name))

        acc = sb("acc_sb", [P, TT, D])
        square = sb("square", [P, D])
        gain = sb("gain", [P, D])
        stat = sb("stat", [P, 4, TT])
        acc_in = [sem(f"acc_in{t}") for t in range(TT)]
        gain_in, ssq, msq, root, inv, normed, out_done = (
            sem(n) for n in ("gain_in", "ssq", "msq", "root", "inv", "normed", "out_done"))
        block = ctx.enter_context(nc.Block("final"))

        @block.sync
        def _(sp):
            for t in range(TT):
                sp.dma_start(acc[:, t, :], scratch["acc"][t * P:(t + 1) * P, :]).then_inc(acc_in[t], 16)
            for t in range(TT):
                sp.wait_ge(normed, t + 1)
                sp.dma_start(out[0, t * P:(t + 1) * P, :], acc[:, t, :]).then_inc(out_done, 16)
            sp.wait_ge(out_done, 16 * TT)

        @block.scalar
        def _(act):
            act.dma_start(gain[:, :], dram["final_norm_g"].unsqueeze(0).broadcast_to([P, D])).then_inc(gain_in, 16)
            for t in range(TT):
                act.wait_ge(acc_in[t], 16)
                if t:
                    act.wait_ge(ssq, t)
                nc.scalar.activation(square[:, :], acc[:, t, :], ACT.Square, accum_out=stat[:, 0, t:t + 1]).then_inc(ssq, 1)
                act.wait_ge(msq, t + 1)
                nc.scalar.activation(stat[:, 2, t:t + 1], stat[:, 1, t:t + 1], ACT.Sqrt).then_inc(root, 1)

        @block.vector
        def _(dve):
            V = nc.vector
            for t in range(TT):
                dve.wait_ge(ssq, t + 1)
                V.tensor_scalar(stat[:, 1, t:t + 1], stat[:, 0, t:t + 1], 1.0 / D, EPS, ALU.mult, ALU.add).then_inc(msq, 1)
                dve.wait_ge(root, t + 1)
                V.reciprocal(stat[:, 3, t:t + 1], stat[:, 2, t:t + 1]).then_inc(inv, 1)
                dve.wait_ge(inv, t + 1)
                if t == 0:
                    dve.wait_ge(gain_in, 16)
                V.scalar_tensor_tensor(acc[:, t, :], acc[:, t, :], stat[:, 3, t:t + 1], gain[:, :], ALU.mult, ALU.mult)\
                    .then_inc(normed, 1)


def hymba_moe_kernel(nc, dram, out):
    scratch = {
        "h2": nc.dram_tensor("h2_rows", (ROWS, D), F32, kind="Internal").ap(),
        "acc": nc.dram_tensor("acc_rows", (ROWS, D), F32, kind="Internal").ap(),
        "table": nc.dram_tensor("token_lists", (E * CAP, 2), I32, kind="Internal").ap(),
    }
    with ExitStack() as ctx:
        shared = {
            "raw": ctx.enter_context(nc.sbuf_tensor("raw_weights", [P, RAW, HALFK, HALF], F32)),
            "utab": ctx.enter_context(nc.sbuf_tensor("unit_table", [1, 4 * P], I32)),
            "ps": ctx.enter_context(nc.psum_tensor("ps", [P, 8, HALF], F32)),
            "raw_in": [ctx.enter_context(nc.semaphore(f"raw_in{i}")) for i in range(RAW)],
        }
        mixer_phase(nc, dram, scratch, shared)
        expert_phase(nc, dram, scratch, shared)
        final_phase(nc, dram, scratch, out)


_INS = ["x", "mem", "norm_mix_g", "w_in", "conv_w", "conv_b", "w_rg_a", "b_rg_a", "w_rg_i", "b_rg_i",
        "lru_lambda", "w_pool", "pool_scale", "mem_norm_g", "w_mem_kv", "w_out", "norm_ffn_g",
        "w_router", "b_router", "w_gu", "b_gu", "w_down", "b_down", "final_norm_g"]


def kernel(**inputs):
    import numpy as _np
    import concourse.bacc as _bacc
    from concourse import mybir as _mybir
    from concourse.bass_utils import run_bass_kernel_spmd as _run

    nc = _bacc.Bacc("TRN2", target_bir_lowering=False, num_devices=1)
    arrays, dram = {}, {}
    for name in _INS:
        a = _np.ascontiguousarray(inputs[name])
        arrays[f"in_{name}"] = a
        dram[name] = nc.dram_tensor(f"in_{name}", a.shape, _mybir.dt.from_np(a.dtype), kind="ExternalInput").ap()
    out = nc.dram_tensor("out_rows", (1, SEQ, D), _mybir.dt.float32, kind="ExternalOutput").ap()
    hymba_moe_kernel(nc, dram, out)
    r = _run(nc, [arrays], core_ids=[0])
    return r.results[0]["out_rows"]
```

```python
import concourse.bass as bass
import numpy as np
from concourse import mybir
from contextlib import ExitStack

F32 = mybir.dt.float32
F32R = mybir.dt.float32r
I32 = mybir.dt.int32
U32 = mybir.dt.uint32
ALU = mybir.AluOpType
ACT = mybir.ActivationFunctionType
AX = mybir.AxisListType

P = 128
SEQ, D = 1024, 1024
TT, KT = SEQ // P, D // P
HALF = 512
N_MEM = 256
MT = N_MEM // P
D_RNN, D_POOL, D_XATTN = 512, 256, 256
D_IN = 2 * D_RNN + D_POOL + D_XATTN
RT, PT_ = D_RNN // P, D_POOL // P
CONV = 4
POOL_WINDOWS = (2, 4, 8, 16)
PAD = max(POOL_WINDOWS)
HEADS, HD = 4, 64
E, TOPK = 32, 4
FF = D
EPS = 1e-6
LRU_C = 8.0
SWIGLU_ALPHA, SWIGLU_LIMIT = 1.702, 7.0

UNIT = 256
TAIL = P // 2
CAP = SEQ
UNITS_PER_E = CAP // UNIT
DUMP = P
ROWS = SEQ + DUMP
GU_CH, DN_CH = 4, 2
CH = GU_CH + DN_CH
HALFK = KT // 2
RAW = 4
SPLIT = 6
AHEAD = SPLIT // 2

V_CONVW, V_CONVB, V_BA, V_BI, V_LAM, V_PS, V_GMIX, V_GMEM, V_N = 0, 16, 20, 24, 28, 32, 34, 42, 50


def hold(eng, sem, value, held):
    eng.wait_ge(sem, value)
    eng.sem_inc(held, 1)


def ring_value(item, slots):
    return 16 * (item // slots + 1)


def mixer_phase(nc, dram, scratch, shared):
    ctx = ExitStack()
    with ctx:
        start = {"raw": shared["raw_start"]}

        def sb(name, shape, dt=F32):
            tensor = ctx.enter_context(nc.sbuf_tensor(name, shape, dt))
            start[name] = nc.sbuf_base - int(np.prod(shape[1:])) * 4
            return tensor

        def split_in(name, shape, of, byte=0):
            return nc.alloc_sbuf_tensor_at(name, shape, F32R, offset=start[of] + byte)

        def sem(name):
            return ctx.enter_context(nc.semaphore(name))

        raw, utab, ps = shared["raw"], shared["utab"], shared["ps"]

        def bank(i, n=1):
            return ps[:, i:i + n, :]

        rows = sb("rows", [P, 3, D])
        hi_part = sb("hi_part", [P, KT, SEQ], F32R)
        landing = raw[:, :, :, :].rearrange("p r k n -> p (r k n)").rearrange("p (k t) -> p k t", k=KT)
        lo_part = split_in("lo_part", [P, KT, SEQ], "raw")
        mixedT = sb("mixedT", [P, KT, SEQ])
        w_in_sb = sb("w_in_sb", [P, 3, KT, P])
        w_in_split = [split_in(f"w_in_split{i}", [P, 2, KT, P], "mixedT", (RT + 2 * i) * SEQ * 4) for i in range(2)]
        region_c = sb("region_c", [P, 3 * (PAD + SEQ) + 4 * SEQ])

        def c_tile(i):
            if i < 3:
                return region_c[:, i * (PAD + SEQ):(i + 1) * (PAD + SEQ)]
            o = 3 * (PAD + SEQ) + (i - 3) * SEQ
            return region_c[:, o:o + SEQ]

        u_pad, r_pad, i_pad = c_tile(0), c_tile(1), c_tile(2)
        uc, a_t, m_t, g_t = c_tile(3), c_tile(4), c_tile(5), c_tile(6)
        x2 = [c_tile(0)[:, 0:D], c_tile(1)[:, 0:D]]
        h2 = [c_tile(2)[:, 0:D], c_tile(3)]
        h2T = [c_tile(4).rearrange("p (k t) -> p k t", k=KT), c_tile(5).rearrange("p (k t) -> p k t", k=KT)]
        g2_row = c_tile(6)
        region_d = sb("region_d", [P, KT * 2 * D_XATTN + KT * N_MEM])
        w_kv_sb = region_d[:, 0:KT * 2 * D_XATTN].rearrange("p (k n) -> p k n", k=KT)
        memnT = region_d[:, KT * 2 * D_XATTN:].rearrange("p (k m) -> p k m", k=KT)
        prob = region_d[:, 0:2 * D].rearrange("p (b h m) -> p b h m", b=2, h=HEADS)
        probT = region_d[:, 2 * D:4 * D].rearrange("p (b h c t) -> p b h c t", b=2, h=HEADS, c=MT)
        qT = region_d[:, 4 * D:4 * D + 2 * SEQ].rearrange("p (c t) -> p c t", c=2)
        mixed_hi = [split_in(f"mixed_hi{i}", [P, KT, P], "w_in_sb", i * D * 4) for i in range(2)]
        mixed_lo = [split_in("mixed_lo0", [P, KT, P], "w_in_sb", 2 * D * 4), split_in("mixed_lo1", [P, KT, P], "region_d")]
        kT = sb("kT", [P, 2, N_MEM])
        v_sb = sb("v_sb", [P, MT, D_XATTN])
        ident = sb("ident", [P, P])
        lower = sb("lower", [P, P])
        ones = sb("ones", [P, P])
        blockdiag = sb("blockdiag", [P, 10, P])
        vrows = sb("vrows", [64, P])
        vec = sb("vec", [P, V_N])
        small = sb("small", [P, 64])
        lam = sb("lam", [P, 8, RT])
        inv_w = sb("inv_w", [P, PT_, PAD])
        iota_e = sb("iota_e", [P, E])
        iota_p = sb("iota_p", [P, 1])
        tokid = sb("tokid", [P, TT], I32)
        empty = a_t[:, 0:2 * UNIT].bitcast(I32).rearrange("p (s w) -> p s w", w=2)
        w_r_sb = sb("w_r_sb", [P, KT, E])
        b_r_row = sb("b_r_row", [P, E])
        logits = sb("logits", [P, E])
        top8 = sb("top8", [P, 8])
        idx8 = sb("idx8", [P, 8], U32)
        idxf = sb("idxf", [P, TOPK])
        onehot = sb("onehot", [P, TOPK, E])
        picked = sb("picked", [P, TOPK, E])
        mask = sb("mask", [P, E])
        run = sb("run", [P, E])
        slotm = sb("slotm", [P, E])
        slotf = sb("slotf", [P, TOPK])
        sloti = sb("sloti", [P, TT, TOPK], I32)
        entry = sb("entry", [P, TT, TOPK, 2], I32)
        gexp = sb("gexp", [P, TOPK])
        cnt = sb("cnt", [P, 8, E])
        ucol = sb("ucol", [P, 12])
        mx = sb("mx", [P, 4, HEADS])

        ss, ms, sd, rs = (small[:, i * 10:(i + 1) * 10] for i in range(4))
        ss2, ms2, sd2, rs2 = (small[:, 40 + i * 2:42 + i * 2] for i in range(4))

        rows_in = [sem(f"rows_in{i}") for i in range(7)]
        w_in_in = [sem(f"w_in_in{i}") for i in range(3)]
        vrows_in, bd_in, kv_in, wout_in, router_in = (sem(n) for n in ("vrows_in", "bd_in", "kv_in", "wout_in", "router_in"))
        gain_in = sem("gain_in_ffn")
        consts, bd_zero, zero_set, zero_out, table_set = (sem(n) for n in ("consts", "bd_zero", "zero_set", "zero_out", "table_set"))
        vecT_ready, vec_done, lam_abs, lam_exp, lam_done, inv_done = (sem(n) for n in ("vecT_ready", "vec_done", "lam_abs", "lam_exp", "lam_done", "inv_done"))
        ss_done, ms_done, sd_done, xn_done, xT_ready, xT_done = (sem(n) for n in ("ss_done", "ms_done", "sd_done", "xn_done", "xT_ready", "xT_done"))
        proj_ready, kv_ready, kv_done = (sem(n) for n in ("proj_ready", "kv_ready", "kv_done"))
        u_done, pu_done, conv_done, gates_ready, sig_done, tanh_done, neg_done, mult_done, gelu_done, rnn_done = (
            sem(n) for n in ("u_done", "pu_done", "conv_done", "gates_ready", "sig_done", "tanh_done", "neg_done", "mult_done", "gelu_done", "rnn_done"))
        pads_zero, d_done, pool_ready, pool_done, q_done = (sem(n) for n in ("pads_zero", "d_done", "pool_ready", "pool_done", "q_done"))
        s_ready, nmax_done, exp_done, prob_done, pT_ready, pT_done, o_ready, o_done = (
            sem(n) for n in ("s_ready", "nmax_done", "exp_done", "prob_done", "pT_ready", "pT_done", "o_ready", "o_done"))
        out_ready, x2_done, ss2_done, ms2_done, sd2_done, h2_done, h2T_ready, h2T_done = (
            sem(n) for n in ("out_ready", "x2_done", "ss2_done", "ms2_done", "sd2_done", "h2_done", "h2T_ready", "h2T_done"))
        stored = [sem("stored0"), sem("stored1")]
        logits_ready, logits_done, top_done, gexp_done, mask_done, rank_ready, slot_done, scattered = (
            sem(n) for n in ("logits_ready", "logits_done", "top_done", "gexp_done", "mask_done", "rank_ready", "slot_done", "scattered"))
        ucol_done, utab_ready = sem("ucol_done"), sem("utab_ready")
        x_hi_done, w_in_scaled, w_in_hi_done, w_in_lo_done = (sem(n) for n in ("x_hi_done", "w_in_scaled", "w_in_hi_done", "w_in_lo_done"))
        w_out_hi_done, w_out_lo_done, mixed_hi_done, mixed_lo_done = (
            sem(n) for n in ("w_out_hi_done", "w_out_lo_done", "mixed_hi_done", "mixed_lo_done"))
        dve_step, pool_step = sem("dve_step"), sem("pool_step")

        NORMED = TT + MT
        row_slots = [rows[:, i, :] for i in range(3)] + [region_d[:, i * D:(i + 1) * D] for i in range(4)]

        def row_slot(item):
            n = len(row_slots)
            if item < NORMED:
                return item % n, item // n + 1
            return (item - NORMED) % 3, sum(i % n == (item - NORMED) % 3 for i in range(NORMED)) + (item - NORMED) // 3 + 1

        def row_tile(item):
            return row_slots[row_slot(item)[0]]
        NPROJ = D_IN // P
        PROJ = [c for r in range(RT) for c in (r, RT + r)] + list(range(2 * RT, NPROJ))

        W_OUT_SPLIT = [[], [0], [1], [2], [3, 4], [5, 6], [7], []]

        block = ctx.enter_context(nc.Block("mixer"))

        @block.sync
        def _(sp):
            def load_rows(item):
                if item < TT or item >= NORMED:
                    t = item if item < TT else item - NORMED
                    src = dram["x"][0, t * P:(t + 1) * P, :]
                else:
                    src = dram["mem"][0, (item - TT) * P:(item - TT + 1) * P, :]
                sp.dma_start(row_tile(item), src).then_inc(rows_in[row_slot(item)[0]], 16)

            def load_w_in(n):
                c = PROJ[n]
                sp.dma_start(w_in_sb[:, n % 3, :, :],
                             dram["w_in"][0].rearrange("(k p) n -> p k n", p=P)[:, :, c * P:(c + 1) * P])\
                    .then_inc(w_in_in[n % 3], 16)

            for item in range(len(row_slots)):
                load_rows(item)
            for n in range(3):
                load_w_in(n)
            for item in range(len(row_slots), NORMED):
                sp.wait_ge(xT_ready, item - len(row_slots) + 1)
                load_rows(item)
            sp.wait_ge(xT_ready, len(row_slots))
            sp.dma_start(w_kv_sb, dram["w_mem_kv"][0].rearrange("(k p) n -> p k n", p=P)).then_inc(kv_in, 16)
            for n in range(3, NPROJ):
                sp.wait_ge(w_in_lo_done, n - 2)
                load_w_in(n)
                if n == 3:
                    sp.wait_ge(xT_ready, NORMED)
                    for item in range(NORMED, NORMED + 3):
                        load_rows(item)
            sp.wait_ge(proj_ready, 2 * NPROJ)
            sp.dma_start(landing, dram["w_out"][0].rearrange("(k p) n -> p k n", p=P)).then_inc(wout_in, 16)
            sp.wait_ge(rnn_done, RT)
            sp.dma_start(g2_row, dram["norm_ffn_g"][0:1, :].broadcast_to([P, D])).then_inc(gain_in, 16)
            for t in range(TT):
                sp.wait_ge(h2_done, t + 1)
                sp.dma_start(scratch["acc"][t * P:(t + 1) * P, :], x2[t % 2]).then_inc(stored[t % 2], 16)
                sp.dma_start(scratch["h2"][t * P:(t + 1) * P, :], h2[t % 2]).then_inc(stored[t % 2], 16)
                if t + 3 < TT:
                    sp.wait_ge(x2_done, t + 1)
                    load_rows(NORMED + t + 3)
            sp.wait_ge(out_ready, TT)
            for j in range(RAW):
                load_half(sp, dram, shared, 0, j)
            for i in range(2):
                sp.wait_ge(stored[i], 32 * (TT // 2))
            sp.wait_ge(zero_out, 32)
            sp.wait_ge(scattered, 16 * TT * TOPK)

        @block.gpsimd
        def _(pool):
            pool.memset(ident[:, :], 0.0).then_inc(pool_step, 1)
            pool.memset(ones[:, :], 1.0).then_inc(pool_step, 1)
            pool.memset(vrows[:, :], 0.0).then_inc(pool_step, 1)
            pool.wait_ge(pool_step, 3)
            pool.affine_select(out=ident[:, :], in_=ident[:, :], compare_op=ALU.not_equal, fill=1.0,
                               base=0, pattern=[[-1, P]], channel_multiplier=1).then_inc(consts, 1)
            vector_rows = [
                (V_CONVW, CONV * RT, dram["conv_w"][0].rearrange("w (c p) -> (w c) p", p=P)),
                (V_CONVB, RT, dram["conv_b"][0].rearrange("(c p) -> c p", p=P)),
                (V_BA, RT, dram["b_rg_a"][0].rearrange("(c p) -> c p", p=P)),
                (V_BI, RT, dram["b_rg_i"][0].rearrange("(c p) -> c p", p=P)),
                (V_LAM, RT, dram["lru_lambda"][0].rearrange("(c p) -> c p", p=P)),
                (V_PS, PT_, dram["pool_scale"][0].rearrange("(c p) -> c p", p=P)),
                (V_GMIX, KT, dram["norm_mix_g"][0].rearrange("(c p) -> c p", p=P)),
                (V_GMEM, KT, dram["mem_norm_g"][0].rearrange("(c p) -> c p", p=P)),
            ]
            for r, n, src in vector_rows:
                pool.dma_start(vrows[r:r + n, :], src).then_inc(vrows_in, 16)
            pool.affine_select(out=lower[:, :], in_=ones[:, :], compare_op=ALU.is_gt, fill=0.0,
                               base=0, pattern=[[1, P]], channel_multiplier=-1).then_inc(consts, 1)
            pool.iota(iota_e[:, :], [[1, E]], base=0, channel_multiplier=0,
                      allow_small_or_imprecise_dtypes=True).then_inc(consts, 1)
            pool.iota(iota_p[:, :], [[0, 1]], base=0, channel_multiplier=1,
                      allow_small_or_imprecise_dtypes=True).then_inc(consts, 1)
            pool.iota(tokid[:, :], [[P, TT]], base=0, channel_multiplier=1).then_inc(consts, 1)
            for j in range(PT_):
                pool.iota(inv_w[:, j, :], [[1, PAD]], base=1, channel_multiplier=0,
                          allow_small_or_imprecise_dtypes=True).then_inc(consts, 1)
            pool.iota(run[:, :], [[CAP, E]], base=0, channel_multiplier=0,
                      allow_small_or_imprecise_dtypes=True).then_inc(consts, 1)
            pool.memset(blockdiag[:, :, :], 0.0).then_inc(bd_zero, 1)
            pool.wait_ge(bd_zero, 1)
            maps = [(0, RT, dram["w_rg_a"][0]), (RT, RT, dram["w_rg_i"][0]), (2 * RT, PT_, dram["w_pool"][0])]
            for first, n, w in maps:
                pairs = w.rearrange("(c two) i j -> two i c j", two=2)
                pool.dma_start(blockdiag[0:HD, first:first + n, 0:HD], pairs[0]).then_inc(bd_in, 16)
                pool.dma_start(blockdiag[HD:P, first:first + n, HD:P], pairs[1]).then_inc(bd_in, 16)
            pool.memset(r_pad, 0.0).then_inc(zero_set, 1)
            pool.memset(i_pad[:, 0:PAD], 0.0).then_inc(pads_zero, 1)
            pool.memset(u_pad[:, 0:PAD], 0.0).then_inc(pads_zero, 1)
            pool.iota(empty[:, :, 0].rearrange("p (b s) -> p b s", b=2), [[0, 2], [1, P]], base=SEQ,
                      channel_multiplier=0).then_inc(zero_set, 1)
            pool.memset(empty[:, :, 1], 0).then_inc(zero_set, 1)
            pool.wait_ge(zero_set, 3)
            pool.dma_start(scratch["acc"][SEQ:ROWS, :], r_pad[:, 0:D]).then_inc(zero_out, 16)
            pool.dma_start(scratch["h2"][SEQ:ROWS, :], r_pad[:, 0:D]).then_inc(zero_out, 16)
            pool.dma_start(scratch["table"].rearrange("(p s) w -> p s w", p=P), empty[:, :, :]).then_inc(table_set, 16)
            pool.dma_start(w_r_sb[:, :, :], dram["w_router"][0].rearrange("(k p) n -> p k n", p=P)).then_inc(router_in, 16)
            pool.dma_start(b_r_row[:, :], dram["b_router"][0:1, :].broadcast_to([P, E])).then_inc(router_in, 16)
            pool.wait_ge(vec_done, 1)
            def scale(n):
                pool.wait_ge(w_in_in[n % 3], ring_value(n, 3))
                nc.gpsimd.tensor_tensor(w_in_sb[:, n % 3, :, :], w_in_sb[:, n % 3, :, :],
                                        vec[:, V_GMIX:V_GMIX + KT].unsqueeze(2).broadcast_to([P, KT, P]), ALU.mult)\
                    .then_inc(w_in_scaled, 1)

            def w_in_lo(n):
                pool.wait_ge(w_in_hi_done, n + 1)
                pool.wait_ge(w_in_scaled, n + 1)
                nc.gpsimd.tensor_tensor(w_in_split[n % 2][:, 1, :, :], w_in_sb[:, n % 3, :, :],
                                        w_in_split[n % 2][:, 0, :, :].bitcast(F32), ALU.subtract).then_inc(w_in_lo_done, 1)

            for n in range(NPROJ):
                scale(n)
                if n >= 3:
                    w_in_lo(n - 1)
            w_in_lo(NPROJ - 1)

            def w_out_lo(k):
                pool.wait_ge(w_out_hi_done, k + 1)
                nc.gpsimd.tensor_tensor(lo_part[:, k, :], landing[:, k, :], hi_part[:, k, :].bitcast(F32), ALU.subtract)\
                    .then_inc(w_out_lo_done, 1)

            for k in range(KT):
                w_out_lo(k)
            pool.wait_ge(table_set, 16)
            for t in range(TT):
                pool.wait_ge(slot_done, t + 1)
                for j in range(TOPK):
                    pool.indirect_dma_start(
                        out=scratch["table"], out_offset=bass.IndirectOffsetOnAxis(ap=sloti[:, t, j:j + 1], axis=0),
                        in_=entry[:, t, j, :], in_offset=None).then_inc(scattered, 16)

        @block.scalar
        def _(act):
            def square(s):
                act.wait_ge(rows_in[row_slot(s)[0]], 16 * row_slot(s)[1])
                if s:
                    act.wait_ge(ss_done, s)
                nc.scalar.activation(g_t, row_tile(s), ACT.Square, accum_out=ss[:, s:s + 1])\
                    .then_inc(ss_done, 1)

            def root(s):
                act.wait_ge(ms_done, s + 1)
                nc.scalar.activation(sd[:, s:s + 1], ms[:, s:s + 1], ACT.Sqrt).then_inc(sd_done, 1)

            def x_hi(s):
                act.wait_ge(xT_ready, s + 1)
                for b in range(2):
                    nc.scalar.activation(hi_part[:, 4 * b:4 * b + 4, s * P:(s + 1) * P],
                                         bank(4 + 2 * (s % 2) + b)[:, 0, :].rearrange("p (k t) -> p k t", k=4),
                                         ACT.Copy).then_inc(x_hi_done, 1)

            def w_in_hi(n):
                act.wait_ge(w_in_scaled, n + 1)
                if n >= 2:
                    act.wait_ge(proj_ready, 2 * (n - 1))
                nc.scalar.activation(w_in_split[n % 2][:, 0, :, :], w_in_sb[:, n % 3, :, :], ACT.Copy).then_inc(w_in_hi_done, 1)

            square(0)
            square(1)
            for s in range(NORMED):
                root(s)
                if 1 <= s <= TT:
                    x_hi(s - 1)
                if s + 2 < NORMED:
                    square(s + 2)
                if s == TT - 1:
                    w_in_hi(0)
            w_in_hi(1)
            act.wait_ge(lam_abs, 1)
            nc.scalar.activation(lam[:, 1, :], lam[:, 0, :], ACT.Exp, scale=-1.0).then_inc(lam_exp, 1)
            act.wait_ge(pads_zero, 2)
            act.wait_ge(zero_out, 32)
            act.wait_ge(table_set, 16)
            act.wait_ge(vec_done, 1)
            act.wait_ge(lam_done, 1)
            def u_evac(c):
                if c:
                    act.wait_ge(conv_done, c)
                for h in range(2):
                    act.wait_ge(proj_ready, 4 * c + h + 1)
                    nc.scalar.activation(u_pad[:, PAD + h * HALF:PAD + (h + 1) * HALF], bank(2 * ((2 * c) % 2) + h)[:, 0, :],
                                         ACT.Copy).then_inc(u_done, 1)
                w_in_hi(2 * c + 2)

            u_evac(0)
            for c in range(RT):
                if c:
                    act.wait_ge(rnn_done, c)
                act.wait_ge(ss_done, NORMED)
                for h in range(2):
                    act.wait_ge(proj_ready, 4 * c + 2 + h + 1)
                    nc.scalar.activation(g_t[:, h * HALF:(h + 1) * HALF], bank(2 + h)[:, 0, :],
                                         ACT.Gelu_apprx_tanh).then_inc(gelu_done, 1)
                w_in_hi(2 * c + 3)
                if c == 0:
                    act.wait_ge(kv_ready, 1)
                    nc.scalar.activation(kT[:, :, :], bank(4)[:, 0, :].rearrange("p (c m) -> p c m", c=2), ACT.Copy)\
                        .then_inc(kv_done, 1)
                    nc.scalar.activation(v_sb[:, :, :], bank(5)[:, 0, :].rearrange("p (c m) -> p c m", c=MT), ACT.Copy)\
                        .then_inc(kv_done, 1)
                act.wait_ge(gates_ready, c + 1)
                r_f, i_f = r_pad[:, 0:SEQ], i_pad[:, 0:SEQ]
                nc.scalar.activation(r_f, bank(4, 2).rearrange("p b n -> p (b n)"), ACT.Sigmoid,
                                     bias=vec[:, V_BA + c:V_BA + c + 1]).then_inc(sig_done, 1)
                nc.scalar.activation(i_f, bank(6, 2).rearrange("p b n -> p (b n)"), ACT.Sigmoid,
                                     bias=vec[:, V_BI + c:V_BI + c + 1]).then_inc(sig_done, 1)
                act.wait_ge(sig_done, 2 * c + 1)
                nc.scalar.activation(a_t, r_f, ACT.Tanh, scale=lam[:, 7, c:c + 1]).then_inc(tanh_done, 1)
                if c + 1 < RT:
                    u_evac(c + 1)
                act.wait_ge(neg_done, c + 1)
                nc.scalar.activation(r_f, r_f, ACT.Sqrt).then_inc(mult_done, 1)
            for j in range(PT_):
                n = 2 * RT + j
                w_in_hi(n + 2)
                if j == 0:
                    act.wait_ge(conv_done, RT)
                else:
                    act.wait_ge(d_done, j)
                for h in range(2):
                    act.wait_ge(proj_ready, 2 * n + h + 1)
                    nc.scalar.activation(u_pad[:, PAD + h * HALF:PAD + (h + 1) * HALF], bank(2 * (n % 2) + h)[:, 0, :],
                                         ACT.Copy).then_inc(pu_done, 1)
            for j in range(2):
                n = 2 * RT + PT_ + j
                for h in range(2):
                    act.wait_ge(proj_ready, 2 * n + h + 1)
                    nc.scalar.activation(qT[:, j, h * HALF:(h + 1) * HALF], bank(2 * (n % 2) + h)[:, 0, :],
                                         ACT.Copy).then_inc(q_done, 1)
            for j in range(PT_):
                act.wait_ge(pool_ready, j + 1)
                nc.scalar.activation(mixedT[:, RT + j, :], bank(4 + 2 * j, 2).rearrange("p b n -> p (b n)"), ACT.Copy,
                                     scale=vec[:, V_PS + j:V_PS + j + 1]).then_inc(pool_done, 1)

            def probT_evac(t):
                act.wait_ge(pT_ready, t + 1)
                if t >= 2:
                    act.wait_ge(o_ready, t - 1)
                for b in range(2):
                    nc.scalar.activation(probT[:, t % 2, 2 * b:2 * b + 2, :, :],
                                         bank(b)[:, 0, :].rearrange("p (h c t) -> p h c t", h=2, c=MT), ACT.Copy)\
                        .then_inc(pT_done, 1)

            def exps(t):
                act.wait_ge(nmax_done, t + 1)
                if t >= 2:
                    act.wait_ge(pT_ready, t - 1)
                for h in range(HEADS):
                    at = 2 * (h % 2) + h // 2
                    nc.scalar.activation(prob[:, t % 2, h, :], ps[:, 4 + 2 * (t % 2) + h % 2, (h // 2) * N_MEM:(h // 2 + 1) * N_MEM],
                                         ACT.Exp, bias=mx[:, 1, at:at + 1], scale=HD ** -0.5,
                                         accum_out=mx[:, 2, h:h + 1]).then_inc(exp_done, 1)

            def w_out_hi(k):
                act.wait_ge(wout_in, 16)
                nc.scalar.activation(hi_part[:, k, :], landing[:, k, :], ACT.Copy).then_inc(w_out_hi_done, 1)

            def mixed_hi_tile(t):
                act.wait_ge(o_done, t + 1)
                if t >= 2:
                    act.wait_ge(out_ready, t - 1)
                nc.scalar.activation(mixed_hi[t % 2][:, :, :], mixedT[:, :, t * P:(t + 1) * P], ACT.Copy).then_inc(mixed_hi_done, 1)

            exps(0)
            exps(1)
            for t in range(TT):
                probT_evac(t)
                if t + 2 < TT:
                    exps(t + 2)
                for k in W_OUT_SPLIT[t]:
                    w_out_hi(k)

            def h2T_evac(t):
                act.wait_ge(h2T_ready, t + 1)
                if t >= 2:
                    act.wait_ge(logits_ready, t - 1)
                for b in range(2):
                    nc.scalar.activation(h2T[t % 2][:, 4 * b:4 * b + 4, :], bank(4 + b)[:, 0, :].rearrange("p (k t) -> p k t", k=4),
                                         ACT.Copy).then_inc(h2T_done, 1)

            def gate_exp(t):
                act.wait_ge(top_done, t + 1)
                nc.scalar.activation(gexp[:, :], top8[:, 0:TOPK], ACT.Exp, bias=small[:, 48:49],
                                     accum_out=small[:, 49:50]).then_inc(gexp_done, 1)

            act.wait_ge(rnn_done, RT)
            act.wait_ge(pool_done, PT_)
            mixed_hi_tile(0)
            for t in range(TT):
                if t + 1 < TT:
                    mixed_hi_tile(t + 1)
                if t >= 2:
                    gate_exp(t - 2)
                if t:
                    act.preload_act_table(ACT.Sqrt)
                    h2T_evac(t - 1)
                act.wait_ge(x2_done, t + 1)
                if t >= 2:
                    act.wait_ge(stored[t % 2], 32 * (t // 2))
                nc.scalar.activation(h2[t % 2], x2[t % 2], ACT.Square, accum_out=ss2[:, t % 2:t % 2 + 1]).then_inc(ss2_done, 1)
                act.wait_ge(ms2_done, t + 1)
                nc.scalar.activation(sd2[:, t % 2:t % 2 + 1], ms2[:, t % 2:t % 2 + 1], ACT.Sqrt).then_inc(sd2_done, 1)
            gate_exp(TT - 2)
            h2T_evac(TT - 1)
            gate_exp(TT - 1)

        @block.vector
        def _(dve):
            steps = [0]

            def link(ins):
                steps[0] += 1
                ins.then_inc(dve_step, 1)
                dve.wait_ge(dve_step, steps[0])

            V = nc.vector

            def vector_columns():
                dve.wait_ge(vecT_ready, 1)
                V.tensor_copy(vec[:, :], bank(0)[:, 0, 0:V_N]).then_inc(vec_done, 1)

            def row_scale(s):
                dve.wait_ge(sd_done, s + 1)
                link(V.reciprocal(rs[:, s:s + 1], sd[:, s:s + 1]))
                V.tensor_scalar(row_tile(s), row_tile(s), rs[:, s:s + 1], None, ALU.mult).then_inc(xn_done, 1)

            def mean_square(s):
                dve.wait_ge(ss_done, s + 1)
                V.tensor_scalar(ms[:, s:s + 1], ss[:, s:s + 1], 1.0 / D, EPS, ALU.mult, ALU.add).then_inc(ms_done, 1)

            def xT_evac(s):
                dve.wait_ge(xT_ready, s + 1)
                for b in range(2):
                    src = bank(4 + 2 * (s % 2) + b)[:, 0, :].rearrange("p (k t) -> p k t", k=4)
                    if s < TT:
                        dve.wait_ge(x_hi_done, 2 * s + b + 1)
                        at = (slice(None), slice(4 * b, 4 * b + 4), slice(s * P, (s + 1) * P))
                        V.tensor_tensor(lo_part[at], src, hi_part[at].bitcast(F32), ALU.subtract).then_inc(xT_done, 1)
                    else:
                        V.tensor_tensor(memnT[:, 4 * b:4 * b + 4, (s - TT) * P:(s - TT + 1) * P], src,
                                        vec[:, V_GMEM + 4 * b:V_GMEM + 4 * b + 4].unsqueeze(2).broadcast_to([P, 4, P]),
                                        ALU.mult).then_inc(xT_done, 1)

            def w_in_lo(n):
                dve.wait_ge(w_in_hi_done, n + 1)
                V.tensor_tensor(w_in_split[n % 2][:, 1, :, :], w_in_sb[:, n % 3, :, :],
                                w_in_split[n % 2][:, 0, :, :].bitcast(F32), ALU.subtract).then_inc(w_in_lo_done, 1)

            def mixed_lo_tile(t):
                dve.wait_ge(mixed_hi_done, t + 1)
                if t >= 2:
                    dve.wait_ge(out_ready, t - 1)
                V.tensor_tensor(mixed_lo[t % 2][:, :, :], mixedT[:, :, t * P:(t + 1) * P], mixed_hi[t % 2][:, :, :].bitcast(F32),
                                ALU.subtract).then_inc(mixed_lo_done, 1)

            mean_square(0)
            for s in range(NORMED):
                row_scale(s)
                if s + 1 < NORMED:
                    mean_square(s + 1)
                if s:
                    xT_evac(s - 1)
                if s == 4:
                    vector_columns()
                    dve.wait_ge(vec_done, 1)
                if s == TT:
                    w_in_lo(0)
            xT_evac(NORMED - 1)
            w_in_lo(1)

            y, z, s_, s2_, p_, t_ = (lam[:, i, :] for i in (2, 1, 3, 4, 5, 6))
            link(V.tensor_scalar(y, vec[:, V_LAM:V_LAM + RT], -1.0, None, ALU.mult))
            V.tensor_tensor(lam[:, 0, :], y, vec[:, V_LAM:V_LAM + RT], ALU.max).then_inc(lam_abs, 1)
            dve.wait_ge(lam_exp, 1)
            link(V.tensor_scalar(t_, z, 2.0, None, ALU.add))
            link(V.reciprocal(t_, t_))
            link(V.tensor_tensor(s_, z, t_, ALU.mult))
            link(V.tensor_tensor(s2_, s_, s_, ALU.mult))
            link(V.tensor_scalar(p_, s2_, 1.0 / 17, None, ALU.mult))
            for k in (15, 13, 11, 9, 7, 5, 3):
                link(V.scalar_tensor_tensor(p_, p_, 1.0 / k, s2_, ALU.add, ALU.mult))
            link(V.scalar_tensor_tensor(p_, p_, 1.0, s_, ALU.add, ALU.mult))
            link(V.tensor_scalar(p_, p_, 2.0, None, ALU.mult))
            link(V.scalar_tensor_tensor(t_, y, 0.0, p_, ALU.max, ALU.add))
            V.tensor_scalar(lam[:, 7, :], t_, -LRU_C / 2, None, ALU.mult).then_inc(lam_done, 1)
            dve.wait_ge(consts, 8)
            for j in range(PT_):
                for g in range(2):
                    part = inv_w[g * HD:(g + 1) * HD, j, :]
                    link(V.tensor_scalar(part, part, float(POOL_WINDOWS[2 * j + g]), None, ALU.min))
            link(V.reciprocal(inv_w[:, :, :], inv_w[:, :, :]))

            U0 = PAD - (CONV - 1)
            r_f, i_f = r_pad[:, 0:SEQ], i_pad[:, 0:SEQ]
            def conv(c):
                dve.wait_ge(u_done, 2 * c + 2)
                tap = [vec[:, V_CONVW + w * RT + c:V_CONVW + w * RT + c + 1] for w in range(CONV)]
                link(V.tensor_scalar(uc, u_pad[:, PAD:PAD + SEQ], tap[CONV - 1], vec[:, V_CONVB + c:V_CONVB + c + 1],
                                     ALU.mult, ALU.add))
                for w in range(CONV - 1):
                    ins = V.scalar_tensor_tensor(uc, u_pad[:, U0 + w:U0 + w + SEQ], tap[w], uc, ALU.mult, ALU.add)
                    if w < CONV - 2:
                        link(ins)
                    else:
                        ins.then_inc(conv_done, 1)

            conv(0)
            for c in range(RT):
                dve.wait_ge(sig_done, 2 * c + 2)
                dve.wait_ge(conv_done, c + 1)
                link(V.tensor_tensor(i_f, i_f, uc, ALU.mult))
                dve.wait_ge(tanh_done, c + 1)
                link(V.tensor_scalar(m_t, a_t, -1.0, 1.0, ALU.mult, ALU.add))
                link(V.reciprocal(m_t, m_t))
                link(V.scalar_tensor_tensor(m_t, a_t, 2.0, m_t, ALU.mult, ALU.mult))
                link(V.scalar_tensor_tensor(r_f, m_t, 2.0, m_t, ALU.add, ALU.mult))
                V.tensor_scalar(r_f, r_f, -1.0, 0.0, ALU.mult, ALU.max).then_inc(neg_done, 1)
                link(V.tensor_scalar(a_t, m_t, 1.0, None, ALU.add))
                if c + 1 < RT:
                    conv(c + 1)
                dve.wait_ge(mult_done, c + 1)
                link(V.memset(r_f[:, 0:1], 1.0))
                link(V.tensor_tensor(i_f, i_f, r_f, ALU.mult))
                link(V.tensor_tensor_scan(m_t, a_t, i_f, 0.0, ALU.mult, ALU.add))
                dve.wait_ge(gelu_done, 2 * c + 2)
                V.tensor_tensor(mixedT[:, c, :], m_t, g_t, ALU.mult).then_inc(rnn_done, 1)

            dve.wait_ge(rnn_done, RT)
            link(V.memset(r_pad[:, 0:PAD], 0.0))
            for j in range(PT_):
                dve.wait_ge(pu_done, 2 * j + 2)
                W = PAD + SEQ
                src, width = u_pad, 1
                bufs = [r_pad, i_pad]
                n_all = 1 if j == 0 else 3
                for k in range(n_all):
                    lead = 2 * width - 1
                    dst = bufs[k % 2]
                    link(V.tensor_tensor(dst[:, lead:W], src[:, lead:W], src[:, lead - width:W - width], ALU.add))
                    src, width = dst, 2 * width
                other = bufs[n_all % 2]
                lead = 2 * width - 1
                V.tensor_tensor(other[HD:P, lead:W], src[HD:P, lead:W], src[HD:P, lead - width:W - width], ALU.add)\
                    .then_inc(dve_step, 1)
                steps[0] += 1
                link(V.tensor_copy(other[0:HD, PAD:W], src[0:HD, PAD:W]))
                link(V.tensor_tensor(src[:, PAD:2 * PAD], other[:, PAD:2 * PAD], inv_w[:, j, :], ALU.mult))
                if j:
                    dve.wait_ge(pool_ready, j)
                link(V.scalar_tensor_tensor(m_t, other[:, PAD:W], inv_w[:, j, PAD - 1:PAD], u_pad[:, PAD:W],
                                            ALU.mult, ALU.subtract))
                V.tensor_tensor(m_t[:, 0:PAD], src[:, PAD:2 * PAD], u_pad[:, PAD:2 * PAD], ALU.subtract).then_inc(d_done, 1)

            def soft_max(t):
                dve.wait_ge(s_ready, t + 1)
                if t:
                    dve.wait_ge(prob_done, t)
                link(V.tensor_reduce(mx[:, 0, :], bank(4 + 2 * (t % 2), 2).rearrange("p b (h m) -> p (b h) m", h=2),
                                     AX.X, ALU.max))
                V.tensor_scalar(mx[:, 1, :], mx[:, 0, :], -(HD ** -0.5), None, ALU.mult).then_inc(nmax_done, 1)
                dve.wait_ge(exp_done, HEADS * (t + 1))
                link(V.reciprocal(mx[:, 3, :], mx[:, 2, :]))
                V.tensor_tensor(prob[:, t % 2], prob[:, t % 2], mx[:, 3, :].unsqueeze(2).broadcast_to([P, HEADS, N_MEM]),
                                ALU.mult).then_inc(prob_done, 1)

            def o_evac(t):
                dve.wait_ge(o_ready, t + 1)
                V.tensor_copy(mixedT[:, RT + PT_:KT, t * P:(t + 1) * P],
                              bank(2 + t % 2)[:, 0, 0:2 * P].rearrange("p (c t) -> p c t", c=2)).then_inc(o_done, 1)

            soft_max(0)
            soft_max(1)
            for t in range(TT):
                if t + 2 < TT:
                    soft_max(t + 2)
                o_evac(t)

            def residual(t):
                dve.wait_ge(out_ready, t + 1)
                item = NORMED + t
                dve.wait_ge(rows_in[row_slot(item)[0]], 16 * row_slot(item)[1])
                if t >= 2:
                    dve.wait_ge(stored[t % 2], 32 * (t // 2))
                V.tensor_tensor(x2[t % 2], bank(2 * (t % 2), 2).rearrange("p b n -> p (b n)"), row_tile(item),
                                ALU.add).then_inc(x2_done, 1)

            def norm(t):
                i = t % 2
                dve.wait_ge(ss2_done, t + 1)
                V.tensor_scalar(ms2[:, i:i + 1], ss2[:, i:i + 1], 1.0 / D, EPS, ALU.mult, ALU.add).then_inc(ms2_done, 1)
                dve.wait_ge(sd2_done, t + 1)
                link(V.reciprocal(rs2[:, i:i + 1], sd2[:, i:i + 1]))
                if t >= 2:
                    dve.wait_ge(h2T_ready, t - 1)
                V.scalar_tensor_tensor(h2[i], x2[i], rs2[:, i:i + 1], g2_row, ALU.mult, ALU.mult).then_inc(h2_done, 1)

            def pick(t):
                dve.wait_ge(logits_ready, t + 1)
                link(V.tensor_tensor(logits[:, :], bank(6)[:, 0, 0:E], b_r_row[:, :], ALU.add))
                link(V.max(top8[:, :], logits[:, :]))
                V.tensor_scalar(small[:, 48:49], top8[:, 0:1], -1.0, None, ALU.mult).then_inc(top_done, 1)
                link(V.max_index(idx8[:, :], top8[:, :], logits[:, :]))
                link(V.tensor_copy(idxf[:, :], idx8[:, 0:TOPK]))
                link(V.tensor_tensor(onehot[:, :, :], iota_e[:, :].unsqueeze(1).broadcast_to([P, TOPK, E]),
                                     idxf[:, :].unsqueeze(2).broadcast_to([P, TOPK, E]), ALU.is_equal))
                V.tensor_reduce(mask[:, :], onehot[:, :, :].rearrange("p j e -> p e j"), AX.X, ALU.add).then_inc(mask_done, 1)

            def place(t):
                dve.wait_ge(gexp_done, t + 1)
                link(V.reciprocal(small[:, 50:51], small[:, 49:50]))
                link(V.tensor_scalar(entry[:, t, :, 1].bitcast(F32), gexp[:, :], small[:, 50:51], None, ALU.mult))
                link(V.tensor_copy(entry[:, t, :, 0], tokid[:, t:t + 1].broadcast_to([P, TOPK])))
                dve.wait_ge(rank_ready, t + 1)
                link(V.tensor_tensor(slotm[:, :], bank(7)[:, 0, 0:E], run[:, :], ALU.add))
                link(V.tensor_tensor(run[:, :], bank(7)[:, 0, E:2 * E], run[:, :], ALU.add))
                link(V.tensor_tensor(picked[:, :, :], onehot[:, :, :], slotm[:, :].unsqueeze(1).broadcast_to([P, TOPK, E]),
                                     ALU.mult))
                link(V.tensor_reduce(slotf[:, :], picked[:, :, :], AX.X, ALU.add))
                V.tensor_copy(sloti[:, t, :], slotf[:, :]).then_inc(slot_done, 1)

            dve.wait_ge(router_in, 32)
            dve.wait_ge(gain_in, 16)
            mixed_lo_tile(0)
            for t in range(TT):
                if t + 1 < TT:
                    mixed_lo_tile(t + 1)
                residual(t)
                norm(t)
                if t >= 2:
                    place(t - 2)
                if t:
                    pick(t - 1)
            place(TT - 2)
            pick(TT - 1)
            place(TT - 1)

            rows_of, total, end, le = cnt[:, 0, :], cnt[:, 1, :], cnt[:, 2, :], cnt[:, 3, :]
            link(V.scalar_tensor_tensor(rows_of, iota_e[:, :], -float(CAP), run[:, :], ALU.mult, ALU.add))
            link(V.tensor_scalar(total, rows_of, 0.0, None, ALU.is_gt))
            link(V.memset(total[:, 0:1], 1.0))
            for k in range(1, UNITS_PER_E):
                link(V.scalar_tensor_tensor(total, rows_of, float(UNIT * k), total, ALU.is_gt, ALU.add))
            link(V.tensor_tensor_scan(end, ones[:, 0:E], total, 0.0, ALU.mult, ALU.add))
            expert, b_, row0, two, first_u, left = (ucol[:, i:i + 1] for i in range(6))
            link(V.tensor_scalar(le, end, iota_p[:, 0:1], None, ALU.is_le))
            link(V.tensor_reduce(expert, le, AX.X, ALU.add))
            link(V.tensor_tensor(cnt[:, 4, :], le, total, ALU.mult))
            link(V.tensor_reduce(first_u, cnt[:, 4, :], AX.X, ALU.add))
            link(V.tensor_tensor(b_, iota_p[:, 0:1], first_u, ALU.subtract))
            link(V.tensor_scalar(cnt[:, 5, :], iota_e[:, :], expert, None, ALU.is_equal))
            link(V.tensor_tensor(cnt[:, 6, :], cnt[:, 5, :], rows_of, ALU.mult))
            link(V.tensor_reduce(left, cnt[:, 6, :], AX.X, ALU.add))
            link(V.scalar_tensor_tensor(left, b_, -float(UNIT), left, ALU.mult, ALU.add))
            link(V.tensor_scalar(ucol[:, 8:9], left, float(P), None, ALU.is_gt))
            link(V.scalar_tensor_tensor(ucol[:, 8:9], left, float(P + TAIL), ucol[:, 8:9], ALU.is_gt, ALU.add))
            link(V.tensor_scalar(ucol[:, 6:7], expert, float(E - 1), None, ALU.min))
            link(V.scalar_tensor_tensor(row0, expert, float(UNITS_PER_E), b_, ALU.mult, ALU.add))
            link(V.tensor_scalar(ucol[:, 7:8], row0, float(E * UNITS_PER_E - 1), None, ALU.min))
            link(V.tensor_scalar(ucol[:, 7:8], ucol[:, 7:8], float(UNIT), None, ALU.mult))
            V.tensor_copy(ucol[:, 9:10], end[:, E - 1:E]).then_inc(ucol_done, 1)
            dve.wait_ge(utab_ready, 1)
            link(V.tensor_copy(utab[0:1, :], bank(6)[0:1, 0, :]))

        @block.tensor
        def _(pe):
            T = nc.tensor
            pe.wait_ge(consts, 1)
            for s in range(NORMED):
                if s == 3:
                    pe.wait_ge(vrows_in, 16 * 8)
                    T.transpose(bank(0)[:, 0, 0:V_N], vrows[0:V_N, :], ident[0:V_N, 0:V_N]).then_inc(vecT_ready, 1)
                pe.wait_ge(xn_done, s + 1)
                if s >= 2:
                    pe.wait_ge(xT_done, 2 * (s - 1))
                for k in range(KT):
                    last = T.transpose(bank(4 + 2 * (s % 2) + k // 4)[:, 0, (k % 4) * P:(k % 4 + 1) * P],
                                       row_tile(s)[:, k * P:(k + 1) * P], ident[:, :])
                last.then_inc(xT_ready, 1)

            def project(n):
                pe.wait_ge(w_in_lo_done, n + 1)
                w_hi, w_lo = (w_in_split[n % 2][:, i, :, :] for i in range(2))
                for h in range(2):
                    if n == 0:
                        pe.wait_ge(xT_done, 2 * 4 * (h + 1))
                        pe.wait_ge(vec_done, 1)
                    if n == 2 or n == 3:
                        pe.wait_ge(u_done if n == 2 else gelu_done, h + 1)
                    elif 4 <= n < 2 * RT + 2:
                        c = (n - 2) // 2
                        pe.wait_ge(u_done if n % 2 == 0 else gelu_done, 2 * c + h + 1)
                    elif n >= 2 * RT + 2:
                        pe.wait_ge(pu_done, 2 * (n - 2 * RT - 2) + h + 1)
                    acc, cols = bank(2 * (n % 2) + h)[:, 0, :], slice(h * HALF, (h + 1) * HALF)
                    for k in range(KT):
                        T.matmul(acc, w_hi[:, k, :], hi_part[:, k, cols], start=(k == 0), stop=False)
                        T.matmul(acc, w_hi[:, k, :], lo_part[:, k, cols], start=False, stop=False)
                        last = T.matmul(acc, w_lo[:, k, :], hi_part[:, k, cols], start=False, stop=(k == KT - 1))
                    last.then_inc(proj_ready, 1)

            def keys_values():
                pe.wait_ge(kv_in, 16)
                pe.wait_ge(xT_done, 2 * NORMED)
                for c in range(2):
                    for k in range(KT):
                        T.matmul(bank(4)[:, 0, c * N_MEM:(c + 1) * N_MEM], w_kv_sb[:, k, c * P:(c + 1) * P],
                                 memnT[:, k, :], start=(k == 0), stop=(k == KT - 1))
                for m in range(MT):
                    for k in range(KT):
                        last = T.matmul(bank(5)[:, 0, m * D_XATTN:(m + 1) * D_XATTN], memnT[:, k, m * P:(m + 1) * P],
                                        w_kv_sb[:, k, D_XATTN:2 * D_XATTN], start=(k == 0), stop=(k == KT - 1))
                last.then_inc(kv_ready, 1)

            def gates(c):
                pe.wait_ge(conv_done, c + 1)
                pe.wait_ge(bd_in, 16 * 6)
                if c == 0:
                    pe.wait_ge(kv_done, 2)
                else:
                    pe.wait_ge(sig_done, 2 * c)
                for g in range(2):
                    for h in range(2):
                        last = T.matmul(bank(4 + 2 * g + h)[:, 0, :], blockdiag[:, g * RT + c, :],
                                        uc[:, h * HALF:(h + 1) * HALF], start=True, stop=True)
                last.then_inc(gates_ready, 1)

            for c in range(RT):
                project(2 * c)
                project(2 * c + 1)
                if c == 0:
                    keys_values()
                gates(c)

            def pool_map(j):
                pe.wait_ge(d_done, j + 1)
                if j == 0:
                    pe.wait_ge(sig_done, 2 * RT)
                for h in range(2):
                    last = T.matmul(bank(4 + 2 * j + h)[:, 0, :], blockdiag[:, 2 * RT + j, :],
                                    m_t[:, h * HALF:(h + 1) * HALF], start=True, stop=True)
                last.then_inc(pool_ready, 1)

            project(2 * RT)
            project(2 * RT + 1)
            project(2 * RT + 2)
            pool_map(0)
            project(2 * RT + 3)
            pool_map(1)

            def scores(t):
                if t < 2:
                    pe.wait_ge(pool_done, t + 1)
                    pe.wait_ge(q_done, 4)
                else:
                    pe.wait_ge(exp_done, HEADS * (t - 1))
                for h in range(HEADS):
                    half = slice((h % 2) * HD, (h % 2 + 1) * HD)
                    last = T.matmul(ps[:, 4 + 2 * (t % 2) + h % 2, (h // 2) * N_MEM:(h // 2 + 1) * N_MEM],
                                    qT[half, h // 2, t * P:(t + 1) * P], kT[half, h // 2, :], start=True, stop=True)
                last.then_inc(s_ready, 1)

            def transpose_prob(t):
                pe.wait_ge(prob_done, t + 1)
                if t:
                    pe.wait_ge(pT_done, 2 * t)
                for h in range(HEADS):
                    for m in range(MT):
                        o = ((h % 2) * MT + m) * P
                        last = T.transpose(bank(h // 2)[:, 0, o:o + P], prob[:, t % 2, h, m * P:(m + 1) * P], ident[:, :])
                last.then_inc(pT_ready, 1)

            def attend(t):
                pe.wait_ge(pT_done, 2 * (t + 1))
                if t >= 2:
                    pe.wait_ge(o_done, t - 1)
                for h in range(HEADS):
                    for m in range(MT):
                        last = T.matmul(ps[(h % 2) * HD:(h % 2 + 1) * HD, 2 + t % 2, (h // 2) * P:(h // 2 + 1) * P],
                                        v_sb[:, m, h * HD:(h + 1) * HD], probT[:, t % 2, h, m, :],
                                        start=(m == 0), stop=(m == MT - 1))
                last.then_inc(o_ready, 1)

            scores(0)
            scores(1)
            for t in range(TT):
                transpose_prob(t)
                if t + 2 < TT:
                    scores(t + 2)
                attend(t)

            def transpose_h2(t):
                pe.wait_ge(h2_done, t + 1)
                if t:
                    pe.wait_ge(h2T_done, 2 * t)
                else:
                    pe.wait_ge(exp_done, HEADS * TT)
                for k in range(KT):
                    last = T.transpose(bank(4 + k // 4)[:, 0, (k % 4) * P:(k % 4 + 1) * P],
                                       h2[t % 2][:, k * P:(k + 1) * P], ident[:, :])
                last.then_inc(h2T_ready, 1)

            def out_project(t):
                pe.wait_ge(mixed_lo_done, t + 1)
                if t == 0:
                    pe.wait_ge(w_out_lo_done, KT)
                elif t >= 2:
                    pe.wait_ge(x2_done, t - 1)
                for k in range(KT):
                    if t and k == KT // 2:
                        transpose_h2(t - 1)
                    hi, lo = mixed_hi[t % 2][:, k, :], mixed_lo[t % 2][:, k, :]
                    for h in range(2):
                        acc, cols = bank(2 * (t % 2) + h)[:, 0, :], slice(h * HALF, (h + 1) * HALF)
                        T.matmul(acc, hi, hi_part[:, k, cols], start=(k == 0), stop=False)
                        T.matmul(acc, hi, lo_part[:, k, cols], start=False, stop=False)
                        last = T.matmul(acc, lo, hi_part[:, k, cols], start=False, stop=(k == KT - 1))
                last.then_inc(out_ready, 1)

            def route(t):
                pe.wait_ge(h2T_done, 2 * (t + 1))
                if t:
                    pe.wait_ge(mask_done, t)
                else:
                    pe.wait_ge(router_in, 32)
                for k in range(KT):
                    last = T.matmul(bank(6)[:, 0, 0:E], h2T[t % 2][:, k, :], w_r_sb[:, k, :],
                                    start=(k == 0), stop=(k == KT - 1))
                last.then_inc(logits_ready, 1)

            def rank(t):
                pe.wait_ge(mask_done, t + 1)
                pe.wait_ge(consts, 8)
                if t:
                    pe.wait_ge(slot_done, t)
                T.matmul(bank(7)[:, 0, 0:E], lower[:, :], mask[:, :], start=True, stop=True)
                T.matmul(bank(7)[:, 0, E:2 * E], ones[:, :], mask[:, :], start=True, stop=True).then_inc(rank_ready, 1)

            out_project(0)
            for t in range(1, TT):
                out_project(t)
                if t >= 2:
                    rank(t - 2)
                route(t - 1)
            transpose_h2(TT - 1)
            rank(TT - 2)
            route(TT - 1)
            rank(TT - 1)
            pe.wait_ge(ucol_done, 1)
            for i in range(4):
                last = T.matmul(bank(6)[0:1, 0, i * P:(i + 1) * P], ucol[:, 6 + i:7 + i], ident[:, :], start=True, stop=True)
            last.then_inc(utab_ready, 1)


def load_half(sp, dram, shared, expert, j):
    at = bass.ds(expert, 1) if not isinstance(expert, int) else slice(expert, expert + 1)
    c, h = j // 2, j % 2
    ks = slice(h * HALFK, (h + 1) * HALFK)
    slot, signal = shared["raw"][:, j % RAW, :, :], shared["raw_in"][j % RAW]
    if c < GU_CH:
        w = dram["w_gu"][0, at].rearrange("a (k p) n -> p (a k) n", p=P)
        q = FF // GU_CH
        for g in range(2):
            lo = g * FF + c * q
            sp.dma_start(slot[:, :, g * q:(g + 1) * q], w[:, ks, lo:lo + q]).then_inc(signal, 16)
    else:
        w = dram["w_down"][0, at].rearrange("a (k p) n -> p (a k) n", p=P)
        lo = (c - GU_CH) * HALF
        for g in range(2):
            part = slice(h * HALFK + g * HALFK // 2, h * HALFK + (g + 1) * HALFK // 2)
            sp.dma_start(slot[:, g * HALFK // 2:(g + 1) * HALFK // 2, :], w[:, part, lo:lo + HALF]).then_inc(signal, 16)


def expert_phase(nc, dram, scratch, shared):
    ctx = ExitStack()
    with ctx:
        def sb(name, shape, dt=F32):
            return ctx.enter_context(nc.sbuf_tensor(name, shape, dt))

        def sem(name):
            return ctx.enter_context(nc.semaphore(name))

        raw, utab, ps, raw_in = shared["raw"], shared["utab"], shared["ps"], shared["raw_in"]
        w_hi = sb("w_hi", [P, SPLIT, HALFK, HALF], F32R)
        w_lo = sb("w_lo", [P, SPLIT, HALFK, HALF], F32R)
        x_rows = sb("x_rows", [P, 2, D])
        xT = sb("xT", [P, KT, 4 * P], F32R)
        hT = sb("hT", [P, KT, 4 * P], F32R)
        y = sb("y", [P, 2, D])
        b_gu_row = sb("b_gu_row", [P, 2, FF])
        b_dn_row = sb("b_dn_row", [P, D])
        gu = sb("gu", [P, 2, 2, HALF])
        sg = sb("sg", [P, 2, 2, HALF // 2])
        next_list = sb("next_list", [P, 2, 2], I32)
        this_list = sb("this_list", [P, 2, 2], I32)
        stand_in = sb("stand_in", [1, 2], I32)
        ident = sb("ident2", [P, P])

        hi_done, lo_done, mm_done, acc_free = (sem(n) for n in ("hi_done", "lo_done", "mm_done", "acc_free"))
        gmin_done, sig_done, h_done, pool_step = (sem(n) for n in ("gmin_done", "sig_done2", "h_done", "pool_step2"))
        hT_ready, hT_hi_done, hT_lo_done = (sem(n) for n in ("hT_ready", "hT_hi_done", "hT_lo_done"))
        xT_ready, xT_hi_done, xT_lo_done = (sem(n) for n in ("xT_ready2", "xT_hi_done", "xT_lo_done"))
        y_biased, y_gated = sem("y_biased"), sem("y_gated")
        b_gu_in, b_dn_in, next_in, this_in, x_in, added = (
            sem(n) for n in ("b_gu_in", "b_dn_in", "next_in", "this_in", "x_in", "added"))
        cleared = sem("cleared")
        id_done, tail_step = sem("id_done"), sem("tail_step")
        b_gu_done, b_dn_done = sem("b_gu_done"), sem("b_dn_done")
        held = {e: sem(f"held_{e}") for e in ("sp", "pool", "act")}
        Q = FF // GU_CH

        block = ctx.enter_context(nc.Block("experts"))

        def rounded(buf, pair, nb):
            return buf[:, 2 * pair:2 * pair + 2, :].rearrange("p k (b s t) -> p k b s t", b=2, s=2)[:, :, 0:nb, 0, :]

        def transposed(bank, nb):
            return ps[:, bank, :].rearrange("p (k b t) -> p k b t", k=2, b=2)[:, :, 0:nb, :]

        def unit_value(eng, row, u, top):
            return eng.value_load(utab[0:1, bass.ds(u + row * P, 1)], min_val=0, max_val=top)

        def n_units(eng):
            return eng.value_load(utab[0:1, 3 * P:3 * P + 1], min_val=1, max_val=E + TOPK * SEQ // UNIT)

        @block.sync
        def _(sp):
            n = n_units(sp)

            with sp.Fori(0, n) as u:
                expert = unit_value(sp, 0, u, E - 1)
                after = unit_value(sp, 0, u + 1, E - 1)
                for j in range(RAW, RAW + 2 * CH):
                    hold(sp, lo_done, 2 * CH * u + j - RAW + 1, held["sp"])
                    if j < 2 * CH:
                        load_half(sp, dram, shared, expert, j)
                    else:
                        with sp.If(u + 1 < n):
                            load_half(sp, dram, shared, after, j - 2 * CH)

        @block.gpsimd
        def _(pool):
            G = nc.gpsimd
            n = n_units(pool)

            def load_list(dst, row0, signal):
                pool.dma_start(dst[:, :, :], scratch["table"][bass.ds(row0, UNIT), :]
                               .rearrange("(b p) w -> p b w", p=P)).then_inc(signal, 16)

            def gather(two):
                pool.indirect_dma_start(
                    out=x_rows[:, 0, :], out_offset=None, in_=scratch["h2"],
                    in_offset=bass.IndirectOffsetOnAxis(ap=next_list[:, 0, 0:1], axis=0)).then_inc(x_in, 16)
                def second(rows):
                    pool.indirect_dma_start(
                        out=x_rows[0:rows, 1, :], out_offset=None, in_=scratch["h2"],
                        in_offset=bass.IndirectOffsetOnAxis(ap=next_list[0:rows, 1, 0:1], axis=0)).then_inc(x_in, 16)
                with pool.If(two > 0):
                    with pool.If(two > 1):
                        second(P)
                    with pool.Else():
                        second(TAIL)
                with pool.Else():
                    pool.dma_start(stand_in[:, :], scratch["table"][0:1, :]).then_inc(x_in, 16)

            def gate_up_bias(expert):
                pool.dma_start(x_rows[0:1, :, :].rearrange("p b n -> p (b n)"), dram["b_gu"][0, bass.ds(expert, 1)])\
                    .then_inc(b_gu_in, 16)

            def gate_up_bias_spread(landed):
                G.partition_broadcast(b_gu_row[:, :, :].rearrange("p g f -> p (g f)"),
                                      landed[0:1, :, :].rearrange("p b n -> p (b n)")).then_inc(b_gu_done, 1)

            load_list(next_list, unit_value(pool, 1, 0, E * CAP - UNIT), next_in)
            pool.memset(ident[:, :], 0.0).then_inc(pool_step, 1)
            pool.wait_ge(pool_step, 1)
            pool.affine_select(out=ident[:, :], in_=ident[:, :], compare_op=ALU.not_equal, fill=1.0,
                               base=0, pattern=[[-1, P]], channel_multiplier=1).then_inc(id_done, 1)
            pool.wait_ge(id_done, 1)
            for i, buf in enumerate((x_rows[TAIL:P, 1, :], y[TAIL:P, 1, :], gu[TAIL:P, :, 1, :])):
                if i:
                    pool.wait_ge(cleared, i)
                pool.memset(buf, 0.0).then_inc(cleared, 1)
            pool.wait_ge(cleared, 3)
            pool.wait_ge(next_in, 16)
            gather(unit_value(pool, 2, 0, 2))
            pool.dma_start(y[0:1, :, :].rearrange("p b n -> p (b n)"), dram["b_gu"][0, bass.ds(unit_value(pool, 0, 0, E - 1), 1)])\
                .then_inc(b_gu_in, 16)
            pool.wait_ge(b_gu_in, 16)
            gate_up_bias_spread(y)
            pool.wait_ge(x_in, 32)
            for i in range(2):
                pool.dma_start(stand_in[:, :], scratch["table"][0:1, :]).then_inc(added, 16)
                pool.wait_ge(added, 16 * (i + 1))
            with pool.Fori(0, n) as u:
                expert = unit_value(pool, 0, u, E - 1)
                expert_next = unit_value(pool, 0, u + 1, E - 1)
                row0 = unit_value(pool, 1, u, E * CAP - UNIT)
                row0_next = unit_value(pool, 1, u + 1, E * CAP - UNIT)
                two = unit_value(pool, 2, u, 2)
                two_next = unit_value(pool, 2, u + 1, 2)
                for c in range(GU_CH):
                    par = c % 2
                    hold(pool, sig_done, 2 * (GU_CH * u + c + 1), held["pool"])

                    def swiglu(nb, c=c, par=par):
                        gate, up = gu[:, par, 0:nb, 0:Q], gu[:, par, 0:nb, Q:2 * Q]
                        G.tensor_tensor(gate, gate, sg[:, par, 0:nb, :], ALU.mult).then_inc(pool_step, 1)
                        pool.wait_ge(pool_step, GU_CH * u + c + 2)
                        G.tensor_tensor(up, up, gate, ALU.mult).then_inc(h_done, 1)

                    with pool.If(two > 0):
                        swiglu(2)
                    with pool.Else():
                        swiglu(1)
                    if c == 0:
                        hold(pool, x_in, 32 * (u + 1), held["pool"])
                        load_list(next_list, row0_next, next_in)
                        hold(pool, added, 32 * u + 32, held["pool"])
                        load_list(this_list, row0, this_in)
                        pool.dma_start(y[0:1, 0, :], dram["b_down"][0, bass.ds(expert, 1)]).then_inc(b_dn_in, 16)
                    if c == 1:
                        hold(pool, next_in, 16 * (u + 2), held["pool"])
                        hold(pool, xT_ready, KT // 2 * (u + 1), held["pool"])
                        gather(two_next)
                        hold(pool, b_dn_in, 16 * (u + 1), held["pool"])
                        G.partition_broadcast(b_dn_row[:, :], y[0:1, 0, :]).then_inc(b_dn_done, 1)
                hold(pool, xT_ready, KT // 2 * (u + 2), held["pool"])
                gate_up_bias(expert_next)
                hold(pool, b_gu_in, 16 * (u + 2), held["pool"])
                gate_up_bias_spread(x_rows)
                hold(pool, y_gated, DN_CH * (u + 1), held["pool"])

                def add_second(rows):
                    pool.indirect_dma_start(
                        out=scratch["acc"], out_offset=bass.IndirectOffsetOnAxis(ap=this_list[0:rows, 1, 0:1], axis=0),
                        in_=y[0:rows, 1, :], in_offset=None, compute_op=ALU.add).then_inc(added, 16)
                with pool.If(two > 0):
                    with pool.If(two > 1):
                        add_second(P)
                    with pool.Else():
                        add_second(TAIL)
                with pool.Else():
                    pool.dma_start(stand_in[:, :], scratch["table"][0:1, :]).then_inc(added, 16)
                pool.indirect_dma_start(
                    out=scratch["acc"], out_offset=bass.IndirectOffsetOnAxis(ap=this_list[:, 0, 0:1], axis=0),
                    in_=y[:, 0, :], in_offset=None, compute_op=ALU.add).then_inc(added, 16)
            hold(pool, added, 32 * n + 32, held["pool"])
            hold(pool, x_in, 32 * (n + 1), held["pool"])
            hold(pool, next_in, 16 * (n + 1), held["pool"])

        @block.scalar
        def _(act):
            n = n_units(act)

            def split_hi(j):
                nc.scalar.activation(w_hi[:, j % SPLIT, :, :], raw[:, j % RAW, :, :], ACT.Copy).then_inc(hi_done, 1)

            def x_hi(nb):
                def emit(g):
                    nc.scalar.activation(rounded(xT, g, nb),
                                         transposed(6 + g % 2, nb),
                                         ACT.Copy).then_inc(xT_hi_done, 1)
                return emit

            def next_x(base, two, groups):
                with act.If(two > 0):
                    for g in groups:
                        act.wait_ge(xT_ready, base + g + 1)
                        x_hi(2)(g)
                with act.Else():
                    for g in groups:
                        act.wait_ge(xT_ready, base + g + 1)
                        x_hi(1)(g)

            act.preload_act_table(ACT.Sigmoid)
            for j in range(SPLIT):
                if j == RAW:
                    next_x(0, unit_value(act, 2, 0, 2), range(KT // 2))
                act.wait_ge(raw_in[j % RAW], 32 * (j // RAW + 1))
                split_hi(j)
            with act.Fori(0, n) as u:
                two = unit_value(act, 2, u, 2)
                two_next = unit_value(act, 2, u + 1, 2)

                def sigmoid(c, nb):
                    up = gu[:, c % 2, 0:nb, Q:2 * Q]
                    act.wait_ge(gmin_done, 2 * (GU_CH * u + c) + 1)
                    nc.scalar.activation(sg[:, c % 2, 0:nb, :], gu[:, c % 2, 0:nb, 0:Q], ACT.Sigmoid,
                                         scale=SWIGLU_ALPHA).then_inc(sig_done, 1)
                    act.wait_ge(gmin_done, 2 * (GU_CH * u + c) + 2)
                    nc.scalar.activation(up, up, ACT.Copy, bias=1.0).then_inc(sig_done, 1)

                def h_hi(c, nb):
                    act.wait_ge(hT_ready, GU_CH * u + c + 1)
                    nc.scalar.activation(rounded(hT, c, nb), transposed(4 + c % 2, nb), ACT.Copy).then_inc(hT_hi_done, 1)

                def gate_y(c, nb):
                    i = c - GU_CH
                    cols = slice(i * HALF, (i + 1) * HALF)
                    gates = this_list[:, :, 1].bitcast(F32)
                    hold(act, y_biased, DN_CH * u + i + 1, held["act"])
                    hold(act, this_in, 16 * (u + 1), held["act"])
                    if nb == 2:
                        nc.scalar.activation(y[:, 1, cols], y[:, 1, cols], ACT.Copy, scale=gates[:, 1:2])
                    nc.scalar.activation(y[:, 0, cols], y[:, 0, cols], ACT.Copy, scale=gates[:, 0:1]).then_inc(y_gated, 1)

                def refill(c, h):
                    j = 2 * (c + AHEAD) + h

                    def emit():
                        act.wait_ge(mm_done, 2 * (CH * u + c) + h + 1)
                        act.wait_ge(raw_in[j % RAW], 32 * 2 * CH // RAW * u + 32 * (j // RAW + 1))
                        split_hi(j)
                    if j < 2 * CH:
                        emit()
                    else:
                        with act.If(u + 1 < n):
                            emit()

                def unit(nb):
                    for c in range(CH):
                        if c == GU_CH:
                            h_hi(c - 1, nb)
                            next_x(KT // 2 * (u + 1), two_next, (0, 1))
                        if c == CH - 1:
                            next_x(KT // 2 * (u + 1), two_next, (2, 3))
                        refill(c, 0)
                        if 0 < c < GU_CH:
                            h_hi(c - 1, nb)
                        if c == GU_CH - 1:
                            sigmoid(c, nb)
                        refill(c, 1)
                        if c < GU_CH - 1:
                            sigmoid(c, nb)
                    gate_y(CH - 2, nb)
                    gate_y(CH - 1, nb)

                with act.If(two > 0):
                    unit(2)
                with act.Else():
                    unit(1)

        @block.vector
        def _(dve):
            V = nc.vector
            n = n_units(dve)
            dve.sem_inc(acc_free, 2)
            dve.sem_inc(hT_lo_done, 1)

            def split_lo(j, before):
                dve.wait_ge(hi_done, before + j + 1)
                V.tensor_tensor(w_lo[:, j % SPLIT, :, :], raw[:, j % RAW, :, :], w_hi[:, j % SPLIT, :, :].bitcast(F32),
                                ALU.subtract).then_inc(lo_done, 1)

            def remainders(buf, pair, bank, two, signal, wait):
                def sub(rows, b0, nb, at):
                    cols = buf[:, 2 * pair:2 * pair + 2, :]
                    hi = cols.rearrange("p k (b s t) -> p k b s t", b=2, s=2)[:, :, b0:b0 + nb, 0, 0:rows]
                    out = cols[:, :, at:at + rows].unsqueeze(2) if nb == 1 else \
                        cols.rearrange("p k (b s t) -> p k b s t", b=2, s=2)[:, :, :, 1, :]
                    return V.tensor_tensor(out, transposed(bank, 2)[:, :, b0:b0 + nb, 0:rows], hi.bitcast(F32), ALU.subtract)
                wait()
                if two == 2:
                    sub(P, 0, 2, P).then_inc(signal, 1)
                else:
                    if two == 1:
                        sub(TAIL, 1, 1, 2 * P + TAIL)
                    sub(P, 0, 1, P).then_inc(signal, 1)

            def per_blocks(two, emit):
                with dve.If(two > 0):
                    with dve.If(two > 1):
                        emit(2)
                    with dve.Else():
                        emit(1)
                with dve.Else():
                    emit(0)

            def next_x(base, two, groups):
                def emit(case):
                    for g in groups:
                        remainders(xT, g, 6 + g % 2, case, xT_lo_done, lambda g=g: dve.wait_ge(xT_hi_done, base + g + 1))
                per_blocks(two, emit)

            for j in range(SPLIT):
                if j == RAW:
                    next_x(0, unit_value(dve, 2, 0, 2), range(KT // 2))
                split_lo(j, 0)
            with dve.Fori(0, n) as u:
                two = unit_value(dve, 2, u, 2)
                two_next = unit_value(dve, 2, u + 1, 2)

                def evacuate(c, second):
                    dve.wait_ge(mm_done, 2 * (CH * u + c) + 2)
                    if c < GU_CH:
                        if c == 0:
                            dve.wait_ge(b_gu_done, u + 1)
                        if c >= 2:
                            dve.wait_ge(hT_ready, GU_CH * u + c - 1)
                        bias = b_gu_row[:, :, c * Q:(c + 1) * Q]
                        dst = lambda nb: gu[:, c % 2, 0:nb, :]
                    else:
                        if c == GU_CH:
                            dve.wait_ge(b_dn_done, u + 1)
                            dve.wait_ge(added, 32 * u + 32)
                        i = c - GU_CH
                        bias = b_dn_row[:, i * HALF:(i + 1) * HALF].rearrange("p (g q) -> p g q", g=2)
                        dst = lambda nb: y[:, 0:nb, i * HALF:(i + 1) * HALF]

                    def biased(out, acc, bias, nb):
                        return V.tensor_tensor(out.rearrange("p b (g q) -> p b g q", g=2),
                                               acc.rearrange("p b (g q) -> p b g q", g=2),
                                               bias.unsqueeze(1).broadcast_to([bias.shape[0], nb, 2, HALF // 2]), ALU.add)

                    acc = ps[:, 2 * (c % 2):2 * (c % 2) + 2, :]

                    def clip(nb):
                        gate, up = gu[:, c % 2, 0:nb, 0:Q], gu[:, c % 2, 0:nb, Q:2 * Q]
                        V.tensor_scalar(gate, gate, SWIGLU_LIMIT, None, ALU.min).then_inc(gmin_done, 1)
                        V.tensor_scalar(up, up, -SWIGLU_LIMIT, SWIGLU_LIMIT, ALU.max, ALU.min).then_inc(gmin_done, 1)

                    def finish(nb):
                        if c >= GU_CH:
                            V.engine_nop().then_inc(y_biased, 1)
                        if c < GU_CH:
                            dve.wait_ge(acc_free, CH * u + c + 3)
                            clip(nb)

                    if second == 1:
                        tail = dst(2)[0:TAIL, 1:2, :]
                        biased(tail, acc[TAIL:P, 1:2, :], bias[TAIL:P], 1).then_inc(tail_step, 1)
                        biased(dst(1), acc[:, 0:1, :], bias, 1)
                        dve.wait_ge(tail_step, CH * u + c + 1)
                        V.tensor_tensor(tail, acc[0:TAIL, 1:2, :], tail, ALU.add).then_inc(acc_free, 1)
                    else:
                        dve.sem_inc(tail_step, 1)
                        biased(dst(1 + second // 2), acc[:, 0:1 + second // 2, :], bias, 1 + second // 2).then_inc(acc_free, 1)
                    finish(2 if second else 1)

                def h_lo(c, second):
                    remainders(hT, c, 4 + c % 2, second, hT_lo_done, lambda: dve.wait_ge(hT_hi_done, GU_CH * u + c + 1))

                def refill(c, h):
                    j = 2 * (c + AHEAD) + h
                    if j < 2 * CH:
                        split_lo(j, 2 * CH * u)
                    else:
                        with dve.If(u + 1 < n):
                            split_lo(j, 2 * CH * u)

                def unit(second):
                    for c in range(CH):
                        if c == GU_CH:
                            h_lo(c - 1, second)
                            next_x(KT // 2 * (u + 1), two_next, (0, 1))
                        if c == CH - 1:
                            next_x(KT // 2 * (u + 1), two_next, (2, 3))
                        if c >= GU_CH:
                            refill(c, 0)
                        evacuate(c, second)
                        if 0 < c < GU_CH:
                            h_lo(c - 1, second)
                        if c < GU_CH:
                            refill(c, 0)
                        refill(c, 1)

                per_blocks(two, unit)

        @block.tensor
        def _(pe):
            T = nc.tensor
            n = n_units(pe)

            def transpose_x(base, two, after_unit, groups=range(KT // 2)):
                for g in groups:
                    if g >= 2 or after_unit:
                        pe.wait_ge(xT_lo_done, base + g - 1)
                    def block_of(b, g=g):
                        for j in range(2):
                            last = T.transpose(ps[:, 6 + g % 2, (2 * j + b) * P:(2 * j + b + 1) * P],
                                               x_rows[:, b, (2 * g + j) * P:(2 * g + j + 1) * P], ident[:, :])
                        return last
                    with pe.If(two > 0):
                        block_of(1)
                    block_of(0).then_inc(xT_ready, 1)

            pe.wait_ge(id_done, 1)
            pe.wait_ge(x_in, 32)
            transpose_x(0, unit_value(pe, 2, 0, 2), False)
            with pe.Fori(0, n) as u:
                two = unit_value(pe, 2, u, 2)
                two_next = unit_value(pe, 2, u + 1, 2)

                def part(c, b, ks):
                    xs = xT if c < GU_CH else hT
                    out = ps[:, 2 * (c % 2) + b, :]
                    for k in ks:
                        slot, kk = (2 * c + k // HALFK) % SPLIT, k % HALFK
                        hi, lo = (xs[:, k, (2 * b + i) * P:(2 * b + i + 1) * P] for i in range(2))
                        T.matmul(out, hi, w_hi[:, slot, kk, :], start=k == 0, stop=False)
                        T.matmul(out, hi, w_lo[:, slot, kk, :], start=False, stop=False)
                        last = T.matmul(out, lo, w_hi[:, slot, kk, :], start=False, stop=k == KT - 1)
                    return last

                def tail_part(c, ks):
                    xs = xT if c < GU_CH else hT
                    out = ps[:, 2 * (c % 2) + 1, :]
                    for k in ks:
                        slot, kk = (2 * c + k // HALFK) % SPLIT, k % HALFK
                        both = xs[:, k, 2 * P:2 * P + 2 * TAIL]
                        T.matmul(out, both, w_hi[:, slot, kk, :], start=k == 0, stop=False)
                        T.matmul(out, both, w_lo[:, slot, kk, :], start=False, stop=k == KT - 1)

                def steps(c, ks, second):
                    pe.wait_ge(lo_done, 2 * CH * u + 2 * c + ks[0] // HALFK + 1)
                    if second == 2:
                        part(c, 1, ks)
                    elif second == 1:
                        tail_part(c, ks)
                    return part(c, 0, ks)

                def transpose_h(c, second):
                    pe.wait_ge(h_done, GU_CH * u + c + 1)
                    if c >= 2:
                        pe.wait_ge(hT_lo_done, GU_CH * u + c - 1 + 1)
                    else:
                        pe.wait_ge(hT_lo_done, GU_CH * u + 1)

                    def block_of(b):
                        for j in range(2):
                            last = T.transpose(ps[:, 4 + c % 2, (2 * j + b) * P:(2 * j + b + 1) * P],
                                               gu[:, c % 2, b, Q + j * P:Q + (j + 1) * P], ident[:, :])
                        return last
                    if second:
                        block_of(1)
                    block_of(0).then_inc(hT_ready, 1)

                def unit(second):
                    first_half, second_half = range(HALFK), range(HALFK, KT)
                    pe.wait_ge(xT_lo_done, KT // 2 * (u + 1))
                    for c in range(GU_CH):
                        pe.wait_ge(acc_free, CH * u + c - 1 + 2)
                        steps(c, first_half, second).then_inc(mm_done, 1)
                        steps(c, second_half, second).then_inc(mm_done, 1)
                        if c:
                            transpose_h(c - 1, second)
                    pe.wait_ge(acc_free, CH * u + GU_CH - 1 + 2)
                    pe.wait_ge(hT_lo_done, GU_CH * u + 2 + 1)
                    steps(GU_CH, first_half, second).then_inc(mm_done, 1)
                    pe.wait_ge(hT_lo_done, GU_CH * u + 3 + 1)
                    steps(GU_CH, range(HALFK, KT - 2), second)
                    transpose_h(GU_CH - 1, second)
                    pe.wait_ge(x_in, 32 * (u + 2))
                    transpose_x(KT // 2 * (u + 1), two_next, True, (0, 1))
                    pe.wait_ge(hT_lo_done, GU_CH * (u + 1) + 1)
                    steps(GU_CH, range(KT - 2, KT), second).then_inc(mm_done, 1)
                    pe.wait_ge(acc_free, CH * u + CH - 2 + 2)
                    steps(CH - 1, first_half, second).then_inc(mm_done, 1)
                    transpose_x(KT // 2 * (u + 1), two_next, True, (2, 3))
                    steps(CH - 1, second_half, second).then_inc(mm_done, 1)

                with pe.If(two > 0):
                    with pe.If(two > 1):
                        unit(2)
                    with pe.Else():
                        unit(1)
                with pe.Else():
                    unit(0)


def final_phase(nc, dram, scratch, out):
    ctx = ExitStack()
    with ctx:
        def sb(name, shape, dt=F32):
            return ctx.enter_context(nc.sbuf_tensor(name, shape, dt))

        def sem(name):
            return ctx.enter_context(nc.semaphore(name))

        acc = sb("acc_sb", [P, TT, D])
        square = sb("square", [P, D])
        gain = sb("gain", [P, D])
        stat = sb("stat", [P, 4, TT])
        acc_in = [sem(f"acc_in{t}") for t in range(TT)]
        gain_in, ssq, msq, root, inv, normed, out_done = (
            sem(n) for n in ("gain_in", "ssq", "msq", "root", "inv", "normed", "out_done"))
        block = ctx.enter_context(nc.Block("final"))

        @block.sync
        def _(sp):
            for t in range(TT):
                sp.dma_start(acc[:, t, :], scratch["acc"][t * P:(t + 1) * P, :]).then_inc(acc_in[t], 16)
            for t in range(TT):
                sp.wait_ge(normed, t + 1)
                sp.dma_start(out[0, t * P:(t + 1) * P, :], acc[:, t, :]).then_inc(out_done, 16)
            sp.wait_ge(out_done, 16 * TT)

        @block.scalar
        def _(act):
            act.dma_start(gain[:, :], dram["final_norm_g"].unsqueeze(0).broadcast_to([P, D])).then_inc(gain_in, 16)
            for t in range(TT):
                act.wait_ge(acc_in[t], 16)
                if t:
                    act.wait_ge(ssq, t)
                nc.scalar.activation(square[:, :], acc[:, t, :], ACT.Square, accum_out=stat[:, 0, t:t + 1]).then_inc(ssq, 1)
                act.wait_ge(msq, t + 1)
                nc.scalar.activation(stat[:, 2, t:t + 1], stat[:, 1, t:t + 1], ACT.Sqrt).then_inc(root, 1)

        @block.vector
        def _(dve):
            V = nc.vector
            for t in range(TT):
                dve.wait_ge(ssq, t + 1)
                V.tensor_scalar(stat[:, 1, t:t + 1], stat[:, 0, t:t + 1], 1.0 / D, EPS, ALU.mult, ALU.add).then_inc(msq, 1)
                dve.wait_ge(root, t + 1)
                V.reciprocal(stat[:, 3, t:t + 1], stat[:, 2, t:t + 1]).then_inc(inv, 1)
                dve.wait_ge(inv, t + 1)
                if t == 0:
                    dve.wait_ge(gain_in, 16)
                V.scalar_tensor_tensor(acc[:, t, :], acc[:, t, :], stat[:, 3, t:t + 1], gain[:, :], ALU.mult, ALU.mult)\
                    .then_inc(normed, 1)


def hymba_moe_kernel(nc, dram, out):
    scratch = {
        "h2": nc.dram_tensor("h2_rows", (ROWS, D), F32, kind="Internal").ap(),
        "acc": nc.dram_tensor("acc_rows", (ROWS, D), F32, kind="Internal").ap(),
        "table": nc.dram_tensor("token_lists", (E * CAP, 2), I32, kind="Internal").ap(),
    }
    with ExitStack() as ctx:
        shared = {
            "raw": ctx.enter_context(nc.sbuf_tensor("raw_weights", [P, RAW, HALFK, HALF], F32)),
            "raw_start": nc.sbuf_base - RAW * HALFK * HALF * 4,
            "utab": ctx.enter_context(nc.sbuf_tensor("unit_table", [1, 4 * P], I32)),
            "ps": ctx.enter_context(nc.psum_tensor("ps", [P, 8, HALF], F32)),
            "raw_in": [ctx.enter_context(nc.semaphore(f"raw_in{i}")) for i in range(RAW)],
        }
        mixer_phase(nc, dram, scratch, shared)
        expert_phase(nc, dram, scratch, shared)
        final_phase(nc, dram, scratch, out)


_INS = ["x", "mem", "norm_mix_g", "w_in", "conv_w", "conv_b", "w_rg_a", "b_rg_a", "w_rg_i", "b_rg_i",
        "lru_lambda", "w_pool", "pool_scale", "mem_norm_g", "w_mem_kv", "w_out", "norm_ffn_g",
        "w_router", "b_router", "w_gu", "b_gu", "w_down", "b_down", "final_norm_g"]


def kernel(**inputs):
    import numpy as _np
    import concourse.bacc as _bacc
    from concourse import mybir as _mybir
    from concourse.bass_utils import run_bass_kernel_spmd as _run

    nc = _bacc.Bacc("TRN2", target_bir_lowering=False, num_devices=1)
    arrays, dram = {}, {}
    for name in _INS:
        a = _np.ascontiguousarray(inputs[name])
        arrays[f"in_{name}"] = a
        dram[name] = nc.dram_tensor(f"in_{name}", a.shape, _mybir.dt.from_np(a.dtype), kind="ExternalInput").ap()
    out = nc.dram_tensor("out_rows", (1, SEQ, D), _mybir.dt.float32, kind="ExternalOutput").ap()
    hymba_moe_kernel(nc, dram, out)
    r = _run(nc, [arrays], core_ids=[0])
    return r.results[0]["out_rows"]
```
